# Optimizing a Trainium2 kernel written in Bass

```python
import jax
import jax.numpy as jnp
from jax import lax
import numpy as np
import math

D_MODEL = 2048
BATCH = 1
SEQ = 256
DEPTH = 1

MEM_LEN = 256
N_BRANCH = 4
MIX_WIDTH = D_MODEL // 4

NSA_HEAD_DIM = 64
NSA_HEADS = MIX_WIDTH // NSA_HEAD_DIM
NSA_KV_GROUPS = 2
NSA_GQA = NSA_HEADS // NSA_KV_GROUPS
NSA_N_BRANCH = 3
NSA_CMP_LEN = 32
NSA_CMP_STRIDE = 16
NSA_SEL_BLOCK = 64
NSA_N_SEL = 16
NSA_WINDOW = 512
NSA_Q_BLOCK = 128
NSA_FORCE_SCORE = 1e6

HGRN_HEAD_DIM = 128
HGRN_HEADS = MIX_WIDTH // HGRN_HEAD_DIM
HGRN_CHUNK = 64
HGRN_F_MIN = 1e-6

POOL_WINDOWS = (2, 4, 8, 16)
POOL_GROUPS = 4
POOL_GROUP_DIM = MIX_WIDTH // POOL_GROUPS

SG_CHUNK = 128
SG_HEADS = 4
SG_HEAD_DIM = MIX_WIDTH // SG_HEADS

X_HEADS = 4
X_HEAD_DIM = 128
X_WIDTH = X_HEADS * X_HEAD_DIM

D_FF = 5632
CONV_WIDTH = 3

LN_EPS = 1e-5
NEG_INF = -1e30
DEEPNORM_ALPHA = (2 * DEPTH) ** 0.25
DEEPNORM_BETA = (8 * DEPTH) ** -0.25

IN_SPLITS = (
    MIX_WIDTH,
    NSA_N_BRANCH * 2 * NSA_KV_GROUPS * NSA_HEAD_DIM,
    NSA_HEADS * NSA_N_BRANCH,
    4 * MIX_WIDTH,
    MIX_WIDTH,
    2 * MIX_WIDTH,
    N_BRANCH * D_MODEL,
)
W_IN_COLS = sum(IN_SPLITS)


def layer_norm(x, g, b):
    xf = x.astype(jnp.float32)
    mu = jnp.mean(xf, -1, keepdims=True)
    var = jnp.mean(jnp.square(xf - mu), -1, keepdims=True)
    y = (xf - mu) * lax.rsqrt(var + LN_EPS) * g.astype(jnp.float32) + b.astype(jnp.float32)
    return y.astype(x.dtype)

def rms_norm(x, g):
    xf = x.astype(jnp.float32)
    y = xf * lax.rsqrt(jnp.mean(jnp.square(xf), -1, keepdims=True) + LN_EPS) * g.astype(jnp.float32)
    return y.astype(x.dtype)

def alibi_slopes(n_heads):
    return jnp.asarray(2.0 ** (-8.0 * np.arange(1, n_heads + 1) / n_heads), dtype=jnp.float32)

def masked_softmax(s, mask, axis=-1):
    p = jax.nn.softmax(jnp.where(mask, s, NEG_INF), axis=axis)
    return jnp.where(mask, p, 0.0)

def cmp_to_sel_matrix(n_cmp, n_blk):
    c0 = np.arange(n_cmp)[:, None] * NSA_CMP_STRIDE
    s0 = np.arange(n_blk)[None, :] * NSA_SEL_BLOCK
    ov = np.clip(np.minimum(c0 + NSA_CMP_LEN, s0 + NSA_SEL_BLOCK) - np.maximum(c0, s0), 0, None)
    return jnp.asarray(ov / NSA_CMP_LEN, dtype=jnp.float32)

def nsa_mixer(q, kv, gate_logits, cmp_pos, cmp_w):
    B, S, _ = q.shape
    G, J, dh, T = NSA_KV_GROUPS, NSA_GQA, NSA_HEAD_DIM, NSA_Q_BLOCK
    f32 = jnp.float32
    q = q.reshape(B, S, G, J, dh) * dh ** -0.5
    kv = kv.reshape(B, S, NSA_N_BRANCH, 2, G, dh)
    gates = jax.nn.sigmoid(gate_logits.reshape(B, S, G, J, NSA_N_BRANCH))
    slopes = alibi_slopes(NSA_HEADS).reshape(G, J)

    n_cmp = (S - NSA_CMP_LEN) // NSA_CMP_STRIDE + 1
    blk = np.arange(n_cmp)[:, None] * NSA_CMP_STRIDE + np.arange(NSA_CMP_LEN)[None, :]

    def compress(t, pos, w):
        tb = t[:, blk] + pos[None, None, :, None, :]
        return jnp.einsum('bclgd,lde->bcge', tb, w)

    k_cmp = compress(kv[:, :, 0, 0], cmp_pos[0], cmp_w[0])
    v_cmp = compress(kv[:, :, 0, 1], cmp_pos[1], cmp_w[1])
    cmp_end = jnp.arange(n_cmp) * NSA_CMP_STRIDE + (NSA_CMP_LEN - 1)

    n_blk = S // NSA_SEL_BLOCK
    n_sel = min(NSA_N_SEL, n_blk)
    sel_map = cmp_to_sel_matrix(n_cmp, n_blk)

    def to_blocks(t):
        return t.reshape(B, n_blk, NSA_SEL_BLOCK, G, dh).transpose(0, 1, 3, 2, 4)

    k_slc = to_blocks(kv[:, :, 1, 0])
    v_slc = to_blocks(kv[:, :, 1, 1])
    blk_ids = jnp.arange(n_blk)
    in_blk = jnp.arange(NSA_SEL_BLOCK)
    b_idx = jnp.arange(B)[:, None, None, None]
    g_idx = jnp.arange(G)[None, None, :, None]

    pad = jnp.zeros((B, NSA_WINDOW, G, dh), kv.dtype)
    k_win = jnp.concatenate([pad, kv[:, :, 2, 0]], axis=1)
    v_win = jnp.concatenate([pad, kv[:, :, 2, 1]], axis=1)

    def query_block(qb):
        q0 = qb * T
        t = q0 + jnp.arange(T)
        qt = lax.dynamic_slice_in_dim(q, q0, T, axis=1)
        gt = lax.dynamic_slice_in_dim(gates, q0, T, axis=1)
        sl = slopes[None, None, :, :, None]

        dist_c = (t[:, None] - cmp_end[None, :]).astype(f32)
        mask_c = (dist_c >= 0)[None, :, None, None, :]
        s_c = jnp.einsum('btgjd,bcgd->btgjc', qt, k_cmp).astype(f32) - sl * dist_c[None, :, None, None, :]
        p_c = masked_softmax(s_c, mask_c)
        o_c = jnp.einsum('btgjc,bcgd->btgjd', p_c.astype(v_cmp.dtype), v_cmp)

        imp = jnp.einsum('btgjc,cn->btgn', p_c, sel_map)
        cur = (t // NSA_SEL_BLOCK)[:, None]
        forced = (blk_ids[None] == 0) | (blk_ids[None] == cur) | (blk_ids[None] == cur - 1)
        future = blk_ids[None] * NSA_SEL_BLOCK > t[:, None]
        imp = jnp.where(forced[None, :, None], NSA_FORCE_SCORE,
                        jnp.where(future[None, :, None], NEG_INF, imp))
        _, idx = lax.top_k(imp, n_sel)
        k_s = k_slc[b_idx, idx, g_idx]
        v_s = v_slc[b_idx, idx, g_idx]
        pos_s = idx[..., None] * NSA_SEL_BLOCK + in_blk
        dist_s = (t[None, :, None, None, None] - pos_s).astype(f32)[:, :, :, None]
        mask_s = dist_s >= 0
        s_s = (jnp.einsum('btgjd,btgnkd->btgjnk', qt, k_s).astype(f32)
               - slopes[None, None, :, :, None, None] * dist_s)
        p_s = masked_softmax(s_s, mask_s, axis=(-2, -1))
        o_s = jnp.einsum('btgjnk,btgnkd->btgjd', p_s.astype(v_s.dtype), v_s)

        k_w = lax.dynamic_slice_in_dim(k_win, q0, T + NSA_WINDOW, axis=1)
        v_w = lax.dynamic_slice_in_dim(v_win, q0, T + NSA_WINDOW, axis=1)
        pos_w = q0 - NSA_WINDOW + jnp.arange(T + NSA_WINDOW)
        dist_w = t[:, None] - pos_w[None, :]
        mask_w = ((pos_w[None] >= 0) & (dist_w >= 0) & (dist_w < NSA_WINDOW))[None, :, None, None, :]
        s_w = (jnp.einsum('btgjd,bsgd->btgjs', qt, k_w).astype(f32)
               - sl * dist_w.astype(f32)[None, :, None, None, :])
        p_w = masked_softmax(s_w, mask_w)
        o_w = jnp.einsum('btgjs,bsgd->btgjd', p_w.astype(v_w.dtype), v_w)

        o = gt[..., 0:1] * o_c + gt[..., 1:2] * o_s + gt[..., 2:3] * o_w
        return o.reshape(B, T, NSA_HEADS * dh)

    out = lax.map(query_block, jnp.arange(S // T))
    return out.transpose(1, 0, 2, 3).reshape(B, S, NSA_HEADS * dh)

def hgrn2_mixer(q, f_logit, i, g, lb, norm_g):
    B, S, _ = q.shape
    H, dk, C = HGRN_HEADS, HGRN_HEAD_DIM, HGRN_CHUNK
    n = S // C
    f32 = jnp.float32
    lbh = lb.reshape(H, dk).astype(f32)
    z = f_logit.reshape(B, S, H, dk).astype(f32)
    f = jnp.maximum(lbh + (1.0 - lbh) * jax.nn.sigmoid(z), HGRN_F_MIN)
    log_f = jnp.log(f)
    k = 1.0 - f

    def to_chunks(a):
        return a.reshape(B, n, C, H, dk).transpose(1, 0, 3, 2, 4)

    xs = (to_chunks(q.astype(f32)), to_chunks(k), to_chunks(i.astype(f32)), to_chunks(log_f))
    causal = jnp.tril(jnp.ones((C, C), dtype=bool))[:, :, None]

    def step(state, inp):
        qq, kk, vv, ll = inp
        b = jnp.cumsum(ll, axis=2)
        o_inter = jnp.einsum('bhtk,bhkv->bhtv', qq * jnp.exp(b), state)
        decay = jnp.exp(jnp.where(causal, b[:, :, :, None, :] - b[:, :, None, :, :], NEG_INF))
        a = jnp.einsum('bhtk,bhtsk,bhsk->bhts', qq, decay, kk)
        o = o_inter + jnp.einsum('bhts,bhsv->bhtv', a, vv)
        b_last = b[:, :, -1:, :]
        state = (jnp.exp(b_last[:, :, 0, :, None]) * state
                 + jnp.einsum('bhsk,bhsv->bhkv', kk * jnp.exp(b_last - b), vv))
        return state, o

    s0 = jnp.zeros((B, H, dk, dk), f32)
    _, o = lax.scan(step, s0, xs)
    o = o.transpose(1, 0, 3, 2, 4).reshape(B, S, H, dk)
    o = rms_norm(o, norm_g.reshape(H, dk)).reshape(B, S, H * dk)
    return (o * jax.nn.silu(g.astype(f32))).astype(q.dtype)

def pool_mixer(c, w, scale):
    B, S, _ = c.shape
    cf = c.astype(jnp.float32).reshape(B, S, POOL_GROUPS, POOL_GROUP_DIM)
    cs = jnp.concatenate([jnp.zeros((B, 1, POOL_GROUPS, POOL_GROUP_DIM), jnp.float32),
                          jnp.cumsum(cf, axis=1)], axis=1)
    t = jnp.arange(S)
    outs = []
    for gi, win in enumerate(POOL_WINDOWS):
        lo = jnp.maximum(t + 1 - win, 0)
        cnt = jnp.minimum(t + 1, win).astype(jnp.float32)
        mean = (cs[:, 1:, gi] - cs[:, lo, gi]) / cnt[None, :, None]
        outs.append(mean - cf[:, :, gi])
    p = jnp.stack(outs, axis=2)
    y = jnp.einsum('bsgc,gcd->bsgd', p, w.astype(jnp.float32)).reshape(B, S, MIX_WIDTH)
    return (y * scale.astype(jnp.float32)).astype(c.dtype)

def sgu_mixer(u, v, ln_g, ln_b, ws, bs):
    B, S, _ = u.shape
    n = S // SG_CHUNK
    v = layer_norm(jax.nn.gelu(v), ln_g, ln_b).reshape(B, n, SG_CHUNK, SG_HEADS, SG_HEAD_DIM)
    mask = jnp.tril(jnp.ones((SG_CHUNK, SG_CHUNK), dtype=bool))
    wm = jnp.where(mask, ws, 0.0)
    vs = jnp.einsum('gqp,bnpgc->bnqgc', wm, v) + bs.T[None, None, :, :, None]
    return jax.nn.gelu(u) * vs.reshape(B, S, MIX_WIDTH)

def cross_attention(x, mem_n, wq, wk, wv, wo):
    B, S, _ = x.shape
    M = mem_n.shape[1]
    q = (x @ wq).reshape(B, S, X_HEADS, X_HEAD_DIM)
    k = (mem_n @ wk).reshape(B, M, X_HEADS, X_HEAD_DIM)
    v = (mem_n @ wv).reshape(B, M, X_HEADS, X_HEAD_DIM)
    s = jnp.einsum('bshd,bmhd->bhsm', q, k).astype(jnp.float32) * X_HEAD_DIM ** -0.5
    p = jax.nn.softmax(s, axis=-1).astype(v.dtype)
    o = jnp.einsum('bhsm,bmhd->bshd', p, v).reshape(B, S, X_WIDTH)
    return o @ wo

def conv_ffn(x, w_in, conv_w, conv_b, w_out):
    h = x @ w_in
    gate, up = jnp.split(h, 2, axis=-1)
    gate = lax.conv_general_dilated(
        gate, conv_w[:, None, :], window_strides=(1,), padding=((CONV_WIDTH - 1, 0),),
        dimension_numbers=('NWC', 'WIO', 'NWC'), feature_group_count=D_FF) + conv_b
    return (jax.nn.silu(gate) * up) @ w_out

def first_inputs(seed: int = 0) -> dict:
    key = jax.random.key(seed)
    ks = iter(jax.random.split(key, 32))
    L, D = DEPTH, D_MODEL
    f32 = jnp.float32

    def nrm(shape, scale):
        return jax.random.normal(next(ks), shape, f32) * scale

    def gain(shape):
        return 1.0 + nrm(shape, 0.05)

    def bias(shape):
        return nrm(shape, 0.02)

    beta = DEEPNORM_BETA
    return {
        'x': nrm((BATCH, SEQ, D), 1.0),
        'mem': nrm((BATCH, MEM_LEN, D), 1.0),
        'w_in': nrm((L, D, W_IN_COLS), D ** -0.5),
        'nsa_cmp_pos': nrm((L, 2, NSA_CMP_LEN, NSA_HEAD_DIM), 0.1),
        'nsa_cmp_w': nrm((L, 2, NSA_CMP_LEN, NSA_HEAD_DIM, NSA_HEAD_DIM), (NSA_CMP_LEN * NSA_HEAD_DIM) ** -0.5),
        'hgrn_lb_logits': nrm((L, MIX_WIDTH), 1.0),
        'hgrn_norm_g': gain((L, MIX_WIDTH)),
        'pool_w': nrm((L, POOL_GROUPS, POOL_GROUP_DIM, POOL_GROUP_DIM), POOL_GROUP_DIM ** -0.5),
        'pool_scale': gain((L, MIX_WIDTH)),
        'sg_ln_g': gain((L, MIX_WIDTH)),
        'sg_ln_b': bias((L, MIX_WIDTH)),
        'sg_w': nrm((L, SG_HEADS, SG_CHUNK, SG_CHUNK), SG_CHUNK ** -0.5),
        'sg_b': gain((L, SG_HEADS, SG_CHUNK)),
        'w_branch': nrm((L, N_BRANCH, MIX_WIDTH, D), MIX_WIDTH ** -0.5),
        'w_mix_out': nrm((L, D, D), beta * D ** -0.5),
        'ln_mix_g': gain((L, D)),
        'ln_mix_b': bias((L, D)),
        'mem_ln_g': gain((D,)),
        'mem_ln_b': bias((D,)),
        'xattn_q': nrm((L, D, X_WIDTH), D ** -0.5),
        'xattn_k': nrm((L, D, X_WIDTH), D ** -0.5),
        'xattn_v': nrm((L, D, X_WIDTH), beta * D ** -0.5),
        'xattn_o': nrm((L, X_WIDTH, D), beta * X_WIDTH ** -0.5),
        'ln_x_g': gain((L, D)),
        'ln_x_b': bias((L, D)),
        'ffn_in': nrm((L, D, 2 * D_FF), D ** -0.5),
        'ffn_conv_w': nrm((L, CONV_WIDTH, D_FF), CONV_WIDTH ** -0.5),
        'ffn_conv_b': bias((L, D_FF)),
        'ffn_out': nrm((L, D_FF, D), beta * D_FF ** -0.5),
        'ln_ffn_g': gain((L, D)),
        'ln_ffn_b': bias((L, D)),
    }

def first_block(x, mem, w_in, nsa_cmp_pos, nsa_cmp_w, hgrn_lb_logits, hgrn_norm_g, pool_w, pool_scale,
              sg_ln_g, sg_ln_b, sg_w, sg_b, w_branch, w_mix_out, ln_mix_g, ln_mix_b, mem_ln_g, mem_ln_b,
              xattn_q, xattn_k, xattn_v, xattn_o, ln_x_g, ln_x_b, ffn_in, ffn_conv_w, ffn_conv_b, ffn_out,
              ln_ffn_g, ln_ffn_b):
    B, S, D = x.shape
    mem_n = layer_norm(mem, mem_ln_g, mem_ln_b)
    sm = jax.nn.softmax(hgrn_lb_logits.astype(jnp.float32), axis=0)
    lower_bounds = jnp.cumsum(sm, axis=0) - sm[0]
    split_at = [int(v) for v in np.cumsum(IN_SPLITS)[:-1]]

    for l in range(DEPTH):
        h = x @ w_in[l]
        a_q, a_kv, a_g, b_in, c_in, d_in, merge = jnp.split(h, split_at, axis=-1)
        o_a = nsa_mixer(a_q, a_kv, a_g, nsa_cmp_pos[l], nsa_cmp_w[l])
        b_q, b_f, b_i, b_g = jnp.split(b_in, 4, axis=-1)
        o_b = hgrn2_mixer(b_q, b_f, b_i, b_g, lower_bounds[l], hgrn_norm_g[l])
        o_c = pool_mixer(c_in, pool_w[l], pool_scale[l])
        d_u, d_v = jnp.split(d_in, 2, axis=-1)
        o_d = sgu_mixer(d_u, d_v, sg_ln_g[l], sg_ln_b[l], sg_w[l], sg_b[l])
        branches = jnp.stack([o_a, o_b, o_c, o_d], axis=2)
        gates = jax.nn.sigmoid(merge.reshape(B, S, N_BRANCH, D))
        y = jnp.einsum('bsnw,nwd->bsnd', branches, w_branch[l])
        mixed = jnp.sum(gates * y, axis=2) @ w_mix_out[l]
        x = layer_norm(DEEPNORM_ALPHA * x + mixed, ln_mix_g[l], ln_mix_b[l])

        xa = cross_attention(x, mem_n, xattn_q[l], xattn_k[l], xattn_v[l], xattn_o[l])
        x = layer_norm(DEEPNORM_ALPHA * x + xa, ln_x_g[l], ln_x_b[l])

        ff = conv_ffn(x, ffn_in[l], ffn_conv_w[l], ffn_conv_b[l], ffn_out[l])
        x = layer_norm(DEEPNORM_ALPHA * x + ff, ln_ffn_g[l], ln_ffn_b[l])
    return x


BLOCK = 128
BRANCH_W = D_MODEL // 4
A_HEADS = 4
A_HD = BRANCH_W // (2 * A_HEADS)
B_WIDTH = BRANCH_W
B_BLOCKS = 8
B_CONV = 4
B_C = 8.0
C_HEADS = 4
C_HD = BRANCH_W // C_HEADS
D_HEADS = 8
D_KV = 2
D_GROUP = D_HEADS // D_KV
D_HD = BRANCH_W // D_HEADS
WINDOW = 128
D_FF_2 = -(-8 * D_MODEL // (3 * 256)) * 256

IN_SIZES = (
    2 * A_HEADS * A_HD, 2 * A_HEADS * A_HD, 2 * A_HEADS * A_HD,
    B_WIDTH, B_WIDTH,
    C_HEADS * C_HD, C_HEADS * C_HD, C_HEADS * C_HD, C_HEADS,
    D_HEADS * D_HD, D_KV * D_HD, D_KV * D_HD,
    N_BRANCH * D_MODEL,
)
IN_COLS = sum(IN_SIZES)
RMS_EPS = 1e-6
NEG_INF_2 = -1e30


def rms_norm_2(x, g):
    xf = x.astype(jnp.float32)
    y = xf * lax.rsqrt(jnp.mean(xf * xf, axis=-1, keepdims=True) + RMS_EPS)
    return (y * g.astype(jnp.float32)).astype(x.dtype)

def alibi_slopes_2(n):
    return jnp.exp2(-8.0 * jnp.arange(1, n + 1, dtype=jnp.float32) / n)

def diff_attention(q, k, v, lam, slopes):
    B, S, H, _, dh = q.shape
    nb = S // BLOCK
    scale = dh ** -0.5
    qb = q.reshape(B, nb, BLOCK, H, 2, dh).transpose(1, 0, 2, 3, 4, 5)
    kpos = jnp.arange(S)

    def one_block(args):
        qblk, i = args
        qpos = i * BLOCK + jnp.arange(BLOCK)
        dist = (qpos[:, None] - kpos[None, :]).astype(jnp.float32)
        logits = jnp.einsum('bqhmd,bshmd->bmhqs', qblk, k).astype(jnp.float32) * scale
        logits = logits - slopes[:, None, None] * dist
        logits = jnp.where(dist >= 0, logits, NEG_INF_2)
        p = jax.nn.softmax(logits, axis=-1)
        w = p[:, 0] - lam * p[:, 1]
        return jnp.einsum('bhqs,bshe->bqhe', w.astype(v.dtype), v)

    out = lax.map(one_block, (qb, jnp.arange(nb)))
    return out.transpose(1, 0, 2, 3, 4).reshape(B, S, H, 2 * dh)

def rg_lru_branch(xb, gb, conv_w, conv_b, wa, ba, wx, bx, lam):
    B, S, C = xb.shape
    xc = lax.conv_general_dilated(xb, conv_w[:, None, :], window_strides=(1,),
                                  padding=[(B_CONV - 1, 0)],
                                  dimension_numbers=('NWC', 'WIO', 'NWC'),
                                  feature_group_count=C) + conv_b
    xg = xc.reshape(B, S, B_BLOCKS, C // B_BLOCKS)
    r = jax.nn.sigmoid(jnp.einsum('bsnc,ncd->bsnd', xg, wa).reshape(B, S, C) + ba)
    i = jax.nn.sigmoid(jnp.einsum('bsnc,ncd->bsnd', xg, wx).reshape(B, S, C) + bx)
    log_a = -B_C * r.astype(jnp.float32) * jax.nn.softplus(-lam.astype(jnp.float32))
    a = jnp.exp(log_a)
    u = jnp.sqrt(-jnp.expm1(2.0 * log_a)) * (i * xc).astype(jnp.float32)

    def combine(left, right):
        a1, b1 = left
        a2, b2 = right
        return a1 * a2, a2 * b1 + b2

    _, h = lax.associative_scan(combine, (a, u), axis=1)
    return jax.nn.gelu(gb) * h.astype(xb.dtype)

def forgetting_attention(q, k, v, logf):
    B, S, H, dh = q.shape
    nb = S // BLOCK
    scale = dh ** -0.5
    cum = jnp.cumsum(logf, axis=1).transpose(0, 2, 1)
    qb = q.reshape(B, nb, BLOCK, H, dh).transpose(1, 0, 2, 3, 4)
    cqb = cum.reshape(B, H, nb, BLOCK).transpose(2, 0, 1, 3)
    kpos = jnp.arange(S)

    def one_block(args):
        qblk, cq, i = args
        qpos = i * BLOCK + jnp.arange(BLOCK)
        causal = qpos[:, None] >= kpos[None, :]
        logits = jnp.einsum('bqhd,bshd->bhqs', qblk, k).astype(jnp.float32) * scale
        logits = logits + cq[..., None] - cum[:, :, None, :]
        logits = jnp.where(causal, logits, NEG_INF_2)
        p = jax.nn.softmax(logits, axis=-1)
        return jnp.einsum('bhqs,bshd->bqhd', p.astype(v.dtype), v)

    out = lax.map(one_block, (qb, cqb, jnp.arange(nb)))
    return out.transpose(1, 0, 2, 3, 4).reshape(B, S, H * dh)

def sliding_window_sink_attention(q, k, v, sinks, slopes):
    B, S, KV, G, dh = q.shape
    nb = S // BLOCK
    scale = dh ** -0.5
    pad = ((0, 0), (BLOCK, 0), (0, 0), (0, 0))

    def band(t):
        tp = jnp.pad(t, pad)
        prev = tp[:, :S].reshape(B, nb, BLOCK, KV, dh)
        cur = tp[:, BLOCK:].reshape(B, nb, BLOCK, KV, dh)
        return jnp.concatenate([prev, cur], axis=2)

    kb, vb = band(k), band(v)
    qb = q.reshape(B, nb, BLOCK, KV, G, dh)
    qi = jnp.arange(BLOCK)
    kj = jnp.arange(2 * BLOCK) - BLOCK
    dist = (qi[:, None] - kj[None, :]).astype(jnp.float32)
    key_pos = jnp.arange(nb)[:, None] * BLOCK + kj[None, :]
    valid = ((dist >= 0) & (dist < WINDOW))[None] & (key_pos >= 0)[:, None, :]
    logits = jnp.einsum('bnqkgd,bnskd->bnkgqs', qb, kb).astype(jnp.float32) * scale
    logits = logits - slopes.reshape(KV, G)[:, :, None, None] * dist
    logits = jnp.where(valid[None, :, None, None], logits, NEG_INF_2)
    sink = sinks.astype(jnp.float32).reshape(KV, G)[None, None, :, :, None, None]
    m = jnp.maximum(jnp.max(logits, axis=-1, keepdims=True), sink)
    e = jnp.exp(logits - m)
    p = e / (jnp.sum(e, axis=-1, keepdims=True) + jnp.exp(sink - m))
    out = jnp.einsum('bnkgqs,bnskd->bnqkgd', p.astype(v.dtype), vb)
    return out.reshape(B, S, KV * G * dh)

def second_inputs(seed: int = 0) -> dict:
    key = jax.random.key(seed)
    ks = jax.random.split(key, 26)
    f32 = jnp.float32

    def nrm(k, shape, scale):
        return jax.random.normal(k, shape, f32) * scale

    bw = B_WIDTH // B_BLOCKS
    a8 = jax.random.uniform(ks[15], (DEPTH, B_WIDTH), f32, 0.9, 0.999)
    a0 = a8 ** (1.0 / B_C)
    return {
        'x': nrm(ks[0], (BATCH, SEQ, D_MODEL), 1.0),
        'norm_mix': 1.0 + nrm(ks[1], (DEPTH, D_MODEL), 0.02),
        'w_in': nrm(ks[2], (DEPTH, D_MODEL, IN_COLS), D_MODEL ** -0.5),
        'b_gate': nrm(ks[3], (DEPTH, N_BRANCH * D_MODEL), 0.02),
        'diff_lq1': nrm(ks[4], (DEPTH, A_HD), 0.1),
        'diff_lk1': nrm(ks[5], (DEPTH, A_HD), 0.1),
        'diff_lq2': nrm(ks[6], (DEPTH, A_HD), 0.1),
        'diff_lk2': nrm(ks[7], (DEPTH, A_HD), 0.1),
        'diff_subln': 1.0 + nrm(ks[8], (DEPTH, 2 * A_HD), 0.02),
        'lru_conv_w': nrm(ks[9], (DEPTH, B_CONV, B_WIDTH), B_CONV ** -0.5),
        'lru_conv_b': nrm(ks[10], (DEPTH, B_WIDTH), 0.02),
        'lru_wa': nrm(ks[11], (DEPTH, B_BLOCKS, bw, bw), bw ** -0.5),
        'lru_ba': nrm(ks[12], (DEPTH, B_WIDTH), 0.02),
        'lru_wx': nrm(ks[13], (DEPTH, B_BLOCKS, bw, bw), bw ** -0.5),
        'lru_bx': nrm(ks[14], (DEPTH, B_WIDTH), 0.02),
        'lru_lambda': jnp.log(a0) - jnp.log1p(-a0),
        'fox_b_f': 2.0 + nrm(ks[16], (DEPTH, C_HEADS), 0.5),
        'swa_sinks': nrm(ks[17], (DEPTH, D_HEADS), 0.5),
        'w_branch': nrm(ks[18], (DEPTH, N_BRANCH, BRANCH_W, D_MODEL), BRANCH_W ** -0.5),
        'w_out': nrm(ks[19], (DEPTH, D_MODEL, D_MODEL), D_MODEL ** -0.5),
        'norm_ffn': 1.0 + nrm(ks[20], (DEPTH, D_MODEL), 0.02),
        'w_ffn_gate': nrm(ks[21], (DEPTH, D_MODEL, D_FF_2), D_MODEL ** -0.5),
        'w_ffn_up': nrm(ks[22], (DEPTH, D_MODEL, D_FF_2), D_MODEL ** -0.5),
        'w_ffn_down': nrm(ks[23], (DEPTH, D_FF_2, D_MODEL), D_FF_2 ** -0.5),
        'norm_final': 1.0 + nrm(ks[24], (D_MODEL,), 0.02),
    }

def second_block(x, norm_mix, w_in, b_gate, diff_lq1, diff_lk1, diff_lq2, diff_lk2, diff_subln,
              lru_conv_w, lru_conv_b, lru_wa, lru_ba, lru_wx, lru_bx, lru_lambda,
              fox_b_f, swa_sinks, w_branch, w_out, norm_ffn, w_ffn_gate, w_ffn_up, w_ffn_down,
              norm_final):
    B, S, _ = x.shape
    slopes_a = alibi_slopes_2(A_HEADS)
    slopes_d = alibi_slopes_2(D_HEADS)
    split_points = []
    acc = 0
    for size in IN_SIZES[:-1]:
        acc += size
        split_points.append(acc)

    h = x
    for l in range(DEPTH):
        u = rms_norm_2(h, norm_mix[l])
        z = u @ w_in[l]
        (aq, ak, av, bxin, bgate, cq, ck, cv, cf, dq, dk, dv, gz) = jnp.split(z, split_points, axis=-1)

        lam_init = 0.8 - 0.6 * math.exp(-0.3 * l)
        lam = (jnp.exp(jnp.sum(diff_lq1[l].astype(jnp.float32) * diff_lk1[l].astype(jnp.float32)))
               - jnp.exp(jnp.sum(diff_lq2[l].astype(jnp.float32) * diff_lk2[l].astype(jnp.float32)))
               + lam_init)
        ya = diff_attention(aq.reshape(B, S, A_HEADS, 2, A_HD), ak.reshape(B, S, A_HEADS, 2, A_HD),
                            av.reshape(B, S, A_HEADS, 2 * A_HD), lam, slopes_a)
        ya = (rms_norm_2(ya, diff_subln[l]) * (1.0 - lam_init)).reshape(B, S, BRANCH_W)

        yb = rg_lru_branch(bxin, bgate, lru_conv_w[l], lru_conv_b[l], lru_wa[l], lru_ba[l],
                           lru_wx[l], lru_bx[l], lru_lambda[l])

        logf = jax.nn.log_sigmoid((cf + fox_b_f[l]).astype(jnp.float32))
        yc = forgetting_attention(cq.reshape(B, S, C_HEADS, C_HD), ck.reshape(B, S, C_HEADS, C_HD),
                                  cv.reshape(B, S, C_HEADS, C_HD), logf)

        yd = sliding_window_sink_attention(dq.reshape(B, S, D_KV, D_GROUP, D_HD),
                                           dk.reshape(B, S, D_KV, D_HD), dv.reshape(B, S, D_KV, D_HD),
                                           swa_sinks[l], slopes_d)

        gates = jax.nn.sigmoid(gz + b_gate[l]).reshape(B, S, N_BRANCH, D_MODEL)
        branches = (ya, yb, yc, yd)
        mixed = gates[:, :, 0] * (branches[0] @ w_branch[l, 0])
        for n in range(1, N_BRANCH):
            mixed = mixed + gates[:, :, n] * (branches[n] @ w_branch[l, n])
        h = h + mixed @ w_out[l]

        v = rms_norm_2(h, norm_ffn[l])
        h = h + (jax.nn.silu(v @ w_ffn_gate[l]) * (v @ w_ffn_up[l])) @ w_ffn_down[l]

    return rms_norm_2(h, norm_final)


def setup_inputs(seed=0):
    out = dict(first_inputs(seed))
    for name, value in second_inputs(seed + 1).items():
        if name != "x":
            out[name + "_2"] = value
    return out


def reference(
    x, mem, w_in, nsa_cmp_pos, nsa_cmp_w, hgrn_lb_logits, hgrn_norm_g, pool_w, pool_scale,
    sg_ln_g, sg_ln_b, sg_w, sg_b, w_branch, w_mix_out, ln_mix_g, ln_mix_b, mem_ln_g, mem_ln_b,
    xattn_q, xattn_k, xattn_v, xattn_o, ln_x_g, ln_x_b, ffn_in, ffn_conv_w, ffn_conv_b, ffn_out,
    ln_ffn_g, ln_ffn_b, norm_mix_2, w_in_2, b_gate_2, diff_lq1_2, diff_lk1_2, diff_lq2_2,
    diff_lk2_2, diff_subln_2, lru_conv_w_2, lru_conv_b_2, lru_wa_2, lru_ba_2, lru_wx_2,
    lru_bx_2, lru_lambda_2, fox_b_f_2, swa_sinks_2, w_branch_2, w_out_2, norm_ffn_2,
    w_ffn_gate_2, w_ffn_up_2, w_ffn_down_2, norm_final_2,
):
    x = first_block(
        x, mem, w_in, nsa_cmp_pos, nsa_cmp_w, hgrn_lb_logits, hgrn_norm_g, pool_w, pool_scale,
        sg_ln_g, sg_ln_b, sg_w, sg_b, w_branch, w_mix_out, ln_mix_g, ln_mix_b, mem_ln_g,
        mem_ln_b, xattn_q, xattn_k, xattn_v, xattn_o, ln_x_g, ln_x_b, ffn_in, ffn_conv_w,
        ffn_conv_b, ffn_out, ln_ffn_g, ln_ffn_b,
    )
    return second_block(
        x, norm_mix_2, w_in_2, b_gate_2, diff_lq1_2, diff_lk1_2, diff_lq2_2, diff_lk2_2,
        diff_subln_2, lru_conv_w_2, lru_conv_b_2, lru_wa_2, lru_ba_2, lru_wx_2, lru_bx_2,
        lru_lambda_2, fox_b_f_2, swa_sinks_2, w_branch_2, w_out_2, norm_ffn_2, w_ffn_gate_2,
        w_ffn_up_2, w_ffn_down_2, norm_final_2,
    )


_drawn_inputs = setup_inputs


def setup_inputs(seed=0):
    import zlib

    import numpy as np

    out = dict(_drawn_inputs(seed))
    spreads = {}
    factors = {'hgrn_norm_g': 5.359,
     'pool_scale': 4.061,
     'sg_ln_g': 7.424,
     'sg_ln_b': 8.0,
     'sg_b': 5.249,
     'mem_ln_g': 8.0,
     'mem_ln_b': 3.937,
     'ffn_conv_b': 7.597,
     'norm_mix_2': 3.149,
     'b_gate_2': 8.0,
     'diff_lq1_2': 200.0,
     'diff_lk1_2': 3.386,
     'diff_lq2_2': 17.531,
     'diff_subln_2': 24.442,
     'lru_ba_2': 24.243,
     'lru_bx_2': 39.841,
     'swa_sinks_2': 23.321,
     'norm_ffn_2': 11.914,
     'norm_final_2': 22.967,
     'diff_lk2_2': 4.279,
     'lru_conv_b_2': 5.917}
    for name, (base, spread) in spreads.items():
        noise = np.random.default_rng([zlib.crc32(name.encode()), seed]).standard_normal(out[name].shape)
        drawn = base * np.exp(spread * noise) if base else spread * noise
        out[name] = jnp.asarray(drawn.astype(out[name].dtype))
    for name, factor in factors.items():
        out[name] = (out[name] * factor).astype(out[name].dtype)
    return out
```

```python
from contextlib import ExitStack
import math

import numpy as np
import concourse.bass as bass
from concourse import mybir

P = 128
S = 256
NT = S // P
D = 2048
KC = D // P
MIX = 512
NBR = 4
FF = 5632
FC = FF // P
W = 256
SLOTS = 4
LANDED = 64
PAIRS = FF // W
DOWN_K = FC // SLOTS
NH = 8
NJ = NH // 2
NC = (S - 32) // 16 + 1
NEG = -1e30
MIXER1_LOADS = 11
MIXER2_LOADS = 8
ALPHA = 2.0 ** 0.25
LN_EPS = 1e-5
RMS_EPS = 1e-6
HL = 7
LAM_INIT = 0.8 - 0.6 * math.exp(0.0)

A_Q, A_KV, A_G, B_IN, C_IN, D_IN, MERGE = 0, 512, 1280, 1304, 3352, 3864, 4888
AQ2, AK2, AV2, BX2, BG2, CQ2, CK2, CV2, CF2, DQ2, DKV2, GZ2 = (
    0, 512, 1024, 1536, 2048, 2560, 3072, 3584, 4096, 4100, 4612, 4868)

ALU = mybir.AluOpType
ACT = mybir.ActivationFunctionType
F32 = mybir.dt.float32
AX = mybir.AxisListType.X

STACKS = (
    (("mem_ln_g", 16), ("mem_ln_b", 16), ("norm_mix_2", 16), ("norm_ffn_2", 16), ("pool_scale", 4),
     ("hgrn_lb_logits", 4), ("lru_conv_w_2", 16), ("lru_conv_b_2", 4), ("lru_ba_2", 4), ("lru_bx_2", 4),
     ("lru_lambda_2", 4), ("sg_b", 4)),
    (("b_gate_2", 64), ("ffn_conv_b", FC)),
    (("conv_w_01", 2 * FC),),
    (("conv_w_2", FC),),
)

BIAS_NSA, BIAS_SWA, BIAS_DIFF, BIAS_FOX = 0, 8, 16, 24
T_LEVEL, T_TRI, T_COUNT, T_CBIAS, T_CMASK, T_HEAD, T_ONES = 0, 1024, 1152, 2176, 2416, 2656, 3680
T_END = 3936


def shape_tables():
    t = np.arange(S)[:, None]
    k = np.arange(S)[None, :]
    dist = (t - k).astype(np.float32)
    causal = dist >= 0
    window = causal & (dist < P)

    def table(slopes, mask):
        maps = [np.where(mask, -np.float32(s) * dist, np.float32(NEG)) for s in slopes]
        both = np.concatenate(maps, axis=1)
        return [both[q * P:(q + 1) * P] for q in range(NT)]

    bias = []
    for mask in (causal, window):
        for j in range(NJ):
            bias += table((2.0 ** -(j + 1), 2.0 ** -(j + 5)), mask)
    for h in range(4):
        bias += table((2.0 ** -(2 * (h + 1)),) * 2, causal)
    bias += table((0.0, 0.0), causal)

    small = np.zeros((P, T_END), np.float32)
    s_, t_ = np.arange(P)[:, None], np.arange(P)[None, :]
    small[:, T_LEVEL:T_LEVEL + P] = s_ == t_
    for lv in range(HL):
        h = 1 << lv
        same = s_ // (2 * h) == t_ // (2 * h)
        small[:, T_LEVEL + (lv + 1) * P:T_LEVEL + (lv + 2) * P] = same & (s_ // h % 2 == 0) & (t_ // h % 2 == 1)
    small[:, T_TRI:T_TRI + P] = s_ <= t_
    for g, win in enumerate((2, 4, 8, 16)):
        small[:, T_COUNT + g * S:T_COUNT + (g + 1) * S] = 1.0 / np.minimum(np.arange(S) + 1, win)
    end = np.arange(NC) * 16 + 31
    for q in range(NT):
        d = ((np.arange(P) + q * P)[:, None] - end[None, :]).astype(np.float32)
        for h in range(NH):
            at = (q * NH + h) * NC
            small[:, T_CBIAS + at:T_CBIAS + at + NC] = np.where(d >= 0, -np.float32(2.0 ** -(h + 1)) * d, NEG)
            small[:, T_CMASK + at:T_CMASK + at + NC] = d >= 0
    for h in range(4):
        small[h, T_HEAD + h * S:T_HEAD + (h + 1) * S] = 1.0
    small[:, T_ONES:T_ONES + S] = 1.0
    return {"t_ident": np.eye(P, dtype=np.float32), "t_bias": np.stack(bias).astype(np.float32), "t_small": small}


class Plan:

    def __init__(self):
        self.tile, self.part, self.out = 0, 0, 0
        self.at = {}

    def add(self, name, tiles=0, parts=0, outs=0):
        self.at[name] = (self.tile, self.part, self.out)
        self.tile += tiles
        self.part += parts
        self.out += outs


class Count:

    def __init__(self, eng, sem):
        self.eng, self.sem, self.n, self.i, self.per = eng, sem, 0, None, 0

    def tick(self, ins):
        ins.then_inc(self.sem, 1)
        self.n += 1
        return ins

    def value(self):
        return self.n if self.i is None else self.i * self.per + self.n

    def done(self):
        self.eng.wait_ge(self.sem, self.value())

    def link(self, ins):
        self.tick(ins)
        self.done()

    def enter(self, i, per):
        self.i, self.per, self.n0 = i, per, self.n

    def leave(self, times):
        assert self.n - self.n0 == self.per, (self.n, self.n0, self.per)
        self.n = self.n0 + self.per * times
        self.i = None


def two_layer_block_kernel(nc, t, out):
    pl = Plan()
    add = pl.add
    add("cols", parts=1, outs=1)
    add("xT1", parts=4, outs=4)
    add("hin", tiles=8, outs=8)
    B_AFTER = (2, 2, 2, 1, 1, 1, 1, 1, 1)
    b_out, b_tile, n = [], [], 0
    for lv, k in enumerate(B_AFTER):
        add(f"lvl{lv}", parts=1, outs=1)
        for _ in range(k):
            add(f"b{n}", tiles=1, outs=1)
            n += 1
    NB = n
    add("ho", parts=1, outs=1)
    add("hT", parts=1, outs=1)
    add("sgw", parts=1, outs=1)
    add("pool", parts=1, outs=1)
    add("sgo", parts=1, outs=1)
    add("sgT", parts=1, outs=1)
    add("pos", parts=1, outs=1)
    add("ckv", parts=1, outs=1)
    add("cs", parts=1, outs=1)
    add("cT", parts=2, outs=2)
    add("co", parts=1, outs=1)
    add("nT", parts=1, outs=1)
    add("merge1", tiles=32, parts=32, outs=64)
    add("memT", parts=4, outs=4)
    add("xk", tiles=2, outs=2)
    add("xv", tiles=2, outs=2)
    add("mixout1", tiles=8, outs=8)
    add("x1T", parts=4, outs=4)
    add("xq", tiles=2, outs=2)
    add("xoT", parts=1, outs=1)
    add("xo", tiles=2, parts=6, outs=8)
    add("x2T", parts=4, outs=4)
    add("ffin1", tiles=44, outs=44)
    add("ffout1", tiles=32, outs=8)
    add("xT2", parts=4, outs=4)
    add("in2", tiles=20, outs=20)
    add("lru", parts=2, outs=2)
    add("y0T", parts=1, outs=1)
    add("y2T", parts=1, outs=1)
    add("y3T", parts=1, outs=1)
    add("merge2", tiles=32, parts=32, outs=64)
    add("mixout2", tiles=8, outs=8)
    add("x3T", parts=4, outs=4)
    add("ffin2", tiles=44, outs=44)
    add("ffout2", tiles=32, outs=8)
    at = pl.at

    U_NSA, U_X, U_DIFF, U_FOX, U_SWA, U_END = 0, 16, 20, 28, 32, 40

    def bias_of(u):
        if u < U_X:
            return BIAS_NSA + (u // 2) % 4 * 2 + u % 2
        if u < U_DIFF:
            return None
        if u < U_FOX:
            return BIAS_DIFF + u - U_DIFF
        if u < U_SWA:
            return BIAS_FOX + u % 2
        return BIAS_SWA + u - U_SWA

    def biased_before(u):
        return len([v for v in range(u % 2, u + 1, 2) if bias_of(v) is not None])

    with ExitStack() as ctx:
        def sb(name, shape):
            return ctx.enter_context(nc.sbuf_tensor(name, shape, F32))

        def sem(name):
            return ctx.enter_context(nc.semaphore(name))

        ring = sb("ring", [P, SLOTS, 20 * W])
        xa = sb("xa", [P, NT, D])
        actT = sb("actT", [P, KC, S])
        arena = sb("arena", [P, 19456])
        ident = sb("ident", [P, P])
        bias = sb("bias", [P, 2, 512])
        score = sb("score", [P, 2, 512])
        probT = sb("probT", [P, 2, 512])
        cols = sb("cols", [P, 4, P])
        stats = sb("stats", [P, 96])
        vecs = sb("vecs", [P, 96])
        lbv = sb("lbv", [P, 64])
        acc = ctx.enter_context(nc.psum_tensor("acc", [P, 4, 512], F32))
        sc = ctx.enter_context(nc.psum_tensor("sc", [P, 2, 512], F32))
        pt = ctx.enter_context(nc.psum_tensor("pt", [P, 512], F32))
        pv = ctx.enter_context(nc.psum_tensor("pv", [P, 512], F32))

        def piece(off, n):
            return arena[:, off:off + n]

        def cut(off, a, b):
            return arena[:, off:off + a * b].rearrange("p (a b) -> p a b", a=a)

        xaf = xa[:, :, :].rearrange("p a b -> p (a b)")
        brT = cut(0, KC, S)
        mixT = cut(15360, KC, S)
        rowsx = cut(15360, NT, D)
        lng, lnb = piece(11264, D), piece(11264 + D, D)
        hT = cut(0, FC, S)
        gateS = cut(4096, 2, 512)
        yS = piece(5120, 512)
        hq, hp, hk, hr, hqd, hkd = (cut(4096 + i * 1024, 4, S) for i in range(6))
        hi, hg = cut(10240, NT, 512), cut(11264, NT, 512)
        ATd, ATx = piece(12288, 1024), cut(13312, 4, P)
        lmask = cut(13824, 8, P)
        hgrow = piece(14848, 512)
        ho, htmp = cut(15360, NT, 512), piece(16384, 1024)
        xapart = lambda off, a, b: xaf[:, off:off + a * b].rearrange("p (a b) -> p a b", a=a)
        qn = xapart(0, NJ, S)
        kvc, kvs, kvw = (xapart(1024 + i * 512, 2, S) for i in range(3))
        ag = xapart(2560, NT, 24)
        cpad = xapart(2624, 4, 16 + S)
        su, sv = cut(17408, NT, 512), cut(18432, NT, 512)
        cw = arena[:, 4096:8192].rearrange("p (i l e) -> p i l e", i=2, l=32)
        posT = cut(8192, 2, 32)
        win = arena[:, 8256:9216].rearrange("p (i l c) -> p i l c", i=2, l=32)
        kcmp, vcmp = piece(9216, NC), piece(9232, P)
        oa = cut(9376, NT, 512)
        ctab = piece(10400, 480)
        cS = piece(10880, 240)
        csm = piece(11120, 160)
        ping, pong = cut(11280, 4, 16 + S), cut(12368, 4, 16 + S)
        cPT = cut(11280, NT * NH, P)
        invc = cut(13456, 4, S)
        poolw = cut(14480, 4, P)
        sgrow, wmT = cut(14992, 4, P), cut(15504, 4, P)
        slg, slb = piece(16016, 512), piece(16528, 512)
        posrow = piece(17040, P)
        tri = piece(17168, P)
        memT = cut(4096, KC, S)
        kx, vx, qx = cut(8192, 4, S), cut(9216, NT, 512), cut(10240, 4, S)
        ox, oxT = cut(0, NT, 512), cut(1024, 4, S)
        convS = cut(15360, 2, 512)
        siluS = cut(16384, 2, 512)
        aq, ak, cq, ck = cut(4096, 4, S), cut(5120, 4, S), cut(7168, 4, S), cut(8192, 4, S)
        av, cv = cut(6144, NT, 512), cut(9216, NT, 512)
        dq, dkv = cut(10240, NJ, S), cut(11264, 2, S)
        cf, cum, ncum = piece(11776, S), piece(12032, S), piece(12288, S)
        bg = cut(12544, 4, S)
        bx = cut(13568, 4, 4 + S)
        bfree = cut(13568, 4, S)
        xc, lr, li = (cut(14608 + i * 1024, 4, S) for i in range(3))
        lt = score[:, :, :].rearrange("p a (b c) -> p (a b) c", b=2)
        la = probT[:, :, :].rearrange("p a (b c) -> p (a b) c", b=2)
        wl = score[:, :, :].rearrange("p i (c d) -> p i c d", c=4)
        ya, yc, yd = (cut(14608 + i * 1024, NT, 512) for i in range(3))
        lrow = piece(17680, 256)
        sinks = piece(17936, NH)
        subln = piece(17952, P)
        heads = arena[:, 18080:19360].rearrange("p (h c) -> p h c", h=5)
        bf = piece(19368, 1)
        ysq = score[:, :, :]

        def col(name, k=0, n=1):
            for i, st in enumerate(STACKS):
                r = 0
                for nm, rows in st:
                    if nm == name:
                        return cols[:, i, r + k:r + k + n]
                    r += rows
            raise KeyError(name)

        w_landed = [sem(f"w_landed{i}") for i in range(SLOTS)]
        tile_used = sem("tile_used")
        part_done = sem("part_done")
        acc_free = [sem("acc_free0"), sem("acc_free1")]
        ident_landed = sem("ident_landed")
        stack_landed = sem("stack_landed")
        x_landed = sem("x_landed")
        level_tab_landed = sem("level_tab_landed")
        mixer1_landed = sem("mixer1_landed")
        mixer2_landed = sem("mixer2_landed")
        lru_zeroed = sem("lru_zeroed")
        lru_landed = sem("lru_landed")
        mem_landed = sem("mem_landed")
        resid_landed = sem("resid_landed")
        norm_rows_landed = sem("norm_rows_landed")
        bias_landed = [sem("bias_landed0"), sem("bias_landed1")]
        out_landed = sem("out_landed")
        pe_rows = sem("pe_rows")
        v_link = sem("vector_link")
        s_link = sem("scalar_link")
        rows_ready = sem("rows_ready")
        norm_done = sem("norm_done")
        var_ready = sem("var_ready")
        std_ready = sem("std_ready")
        lb_max = sem("lb_max")
        lb_exp = sem("lb_exp")
        level_ready = sem("level_ready")
        decay_ready = sem("decay_ready")
        ho_copied = sem("ho_copied")
        mixer_rows = sem("mixer_rows")
        cmp_ready = sem("cmp_ready")
        cmp_exp = sem("cmp_exp")
        gate_ready = sem("gate_ready")
        gate_used = sem("gate_used")
        conv_ready = sem("conv_ready")
        conv_scaled = sem("conv_scaled")
        silu_ready = sem("silu_ready")
        silu_used = sem("silu_used")
        scores_done = sem("scores_done")
        biased = sem("biased")
        max_ready = sem("max_ready")
        probs_ready = sem("probs_ready")
        probs_turned = sem("probs_turned")
        probT_ready = sem("probT_ready")
        pv_done = sem("pv_done")
        pv_used = sem("pv_used")
        lru_conv = sem("lru_conv")
        lru_sig = sem("lru_sig")
        lru_arg = sem("lru_arg")
        lru_exp = sem("lru_exp")
        lru_sq = sem("lru_sq")
        lru_sqrt = sem("lru_sqrt")
        gelu_ready = sem("gelu_ready")
        sp_abs = sem("softplus_abs")
        sp_exp = sem("softplus_exp")
        lam_sum = sem("lam_sum")
        lam_exp = sem("lam_exp")
        sub_sq = sem("sub_sq")

        def wait_tile(eng, name, k=0):
            eng.wait_ge(tile_used, at[name][0] + k + 1)

        def wait_part(eng, name, k=0):
            eng.wait_ge(part_done, at[name][1] + k + 1)

        def o_of(name, k=0):
            return at[name][2] + k

        def banks(o):
            return acc[:, 2 * (o % 2):2 * (o % 2) + 2, :]

        def wait_bank(o, i=None, per=0):
            if o >= 2:
                nc.tensor.wait_ge(acc_free[o % 2], o // 2 if i is None else i * (per // 2) + o // 2)

        def wait_copied(eng, o):
            eng.wait_ge(acc_free[o % 2], o // 2 + 1)

        def release(ins, o):
            ins.then_inc(acc_free[o % 2], 1)

        def unit(u):
            q_ = u % 2
            qs = slice(q_ * P, (q_ + 1) * P)
            if u < U_X or u >= U_SWA:
                j = (u // 2) % 4
                kv_, qq = (dkv, dq) if u >= U_SWA else ((kvs, kvw)[u // 8], qn)
                half = lambda m: slice(64 * m, 64 * m + 64)
                return (lambda m: qq[half(m), j, qs], lambda m: kv_[half(m), 0, :], lambda m: [],
                        lambda m, kt: kv_[:, 1, kt * P + 64 * m:kt * P + 64 * m + 64], 64)
            if u < U_DIFF:
                p_ = (u - U_X) // 2
                return (lambda m: qx[:, 2 * p_ + m, qs], lambda m: kx[:, 2 * p_ + m, :], lambda m: [],
                        lambda m, kt: vx[:, kt, (2 * p_ + m) * P:(2 * p_ + m + 1) * P], P)
            if u < U_FOX:
                h = (u - U_DIFF) // 2
                half = lambda m: slice(64 * m, 64 * m + 64)
                return (lambda m: aq[half(m), h, qs], lambda m: ak[half(m), h, :], lambda m: [],
                        lambda m, kt: av[:, kt, h * P:(h + 1) * P], P)
            p_ = (u - U_FOX) // 2
            return (lambda m: cq[:, 2 * p_ + m, qs], lambda m: ck[:, 2 * p_ + m, :],
                    lambda m: [(cum[0:4, qs], heads[0:4, 2 * p_ + m, :]),
                               (heads[0:4, 2 * p_ + m, 0:P], ncum[0:4, :])],
                    lambda m, kt: cv[:, kt, (2 * p_ + m) * P:(2 * p_ + m + 1) * P], P)

        def scale_of(u):
            if U_FOX <= u < U_SWA:
                return 1.0
            return 64 ** -0.5 if u < U_X or U_DIFF <= u < U_FOX or u >= U_SWA else 128 ** -0.5

        block = ctx.enter_context(nc.Block())

        @block.sync
        def _(sp):
            kp = lambda ap: ap.rearrange("(k p) c -> p k c", p=P)
            w_in, w_in2 = kp(t["w_in"]), kp(t["w_in_2"])

            def slot(n, k, w, off=0):
                return ring[:, n % SLOTS, off:off + k * w].rearrange("p (k c) -> p k c", k=k)

            def load(n, pieces, i=None, per=0):
                if n >= SLOTS:
                    sp.wait_ge(tile_used, n - SLOTS + 1 if i is None else i * per + n - SLOTS + 1)
                for dst, src in pieces:
                    sp.dma_start(dst, src).then_inc(w_landed[n % SLOTS], LANDED // len(pieces))

            def plain(n, w, c, **kw):
                load(n, [(slot(n, KC, W), w[:, :, bass.ds(c, W)])], **kw)

            def paired(n, w, c):
                s_ = slot(n, KC, W)
                load(n, [(s_[:, :, y * P + g * 64:y * P + g * 64 + 64],
                          w[:, :, c + g * 256 + y * 64:c + g * 256 + y * 64 + 64])
                         for y in range(2) for g in range(2)])

            def merge_tiles(n0, w, c0, wbr):
                with sp.Fori(0, D // W) as i:
                    for b in range(NBR):
                        load(n0 + b, [(slot(n0 + b, KC, W), w[:, :, bass.ds(i * W + (c0 + b * D), W)]),
                                      (slot(n0 + b, 4, W, KC * W), wbr[:, 4 * b:4 * b + 4, bass.ds(i * W, W)])],
                             i=i, per=4)

            def square_tiles(n0, w):
                with sp.Fori(0, 2) as i:
                    for k in range(4):
                        plain(n0 + k, w, i * (4 * W) + k * W, i=i, per=4)

            def ff_tiles(n0, gate, up, g0, u0):
                with sp.Fori(0, PAIRS // 2) as i:
                    for k in range(2):
                        plain(n0 + 2 * k, gate, i * (2 * W) + (g0 + k * W), i=i, per=4)
                        plain(n0 + 2 * k + 1, up, i * (2 * W) + (u0 + k * W), i=i, per=4)

            def down_tiles(n0, w):
                with sp.Fori(0, D // W) as i:
                    for k in range(4):
                        load(n0 + k, [(slot(n0 + k, DOWN_K, W), w[:, DOWN_K * k:DOWN_K * (k + 1), bass.ds(i * W, W)])],
                             i=i, per=4)

            n = at["hin"][0]
            for c in range(8):
                plain(n + c, w_in, B_IN + c * W)
            n += 8
            for c in range(2):
                paired(n + c, w_in, A_Q + c * P)
            for c in range(3):
                plain(n + 2 + c, w_in, A_KV + c * W)
            load(n + 5, [(slot(n + 5, KC, 24), w_in[:, :, A_G:A_G + 24])])
            for c in range(6):
                plain(n + 6 + c, w_in, C_IN + c * W)
            merge_tiles(at["merge1"][0], w_in, MERGE, kp(t["w_branch"]))
            for c in range(2):
                plain(at["xk"][0] + c, kp(t["xattn_k"]), c * W)
            for c in range(2):
                plain(at["xv"][0] + c, kp(t["xattn_v"]), c * W)
            square_tiles(at["mixout1"][0], kp(t["w_mix_out"]))
            for c in range(2):
                plain(at["xq"][0] + c, kp(t["xattn_q"]), c * W)
            for c in range(2):
                n = at["xo"][0] + c
                load(n, [(slot(n, 4, 4 * W), kp(t["xattn_o"])[:, :, c * 4 * W:(c + 1) * 4 * W])])
            ff_tiles(at["ffin1"][0], kp(t["ffn_in"]), kp(t["ffn_in"]), 0, FF)
            down_tiles(at["ffout1"][0], kp(t["ffn_out"]))
            n = at["in2"][0]
            for c in range(16):
                plain(n + c, w_in2, c * W)
            load(n + 16, [(slot(n + 16, KC, 4), w_in2[:, :, CF2:CF2 + 4])])
            for c in range(2):
                paired(n + 17 + c, w_in2, DQ2 + c * P)
            plain(n + 19, w_in2, DKV2)
            merge_tiles(at["merge2"][0], w_in2, GZ2, kp(t["w_branch_2"]))
            square_tiles(at["mixout2"][0], kp(t["w_out_2"]))
            ff_tiles(at["ffin2"][0], kp(t["w_ffn_gate_2"]), kp(t["w_ffn_up_2"]), 0, 0)
            down_tiles(at["ffout2"][0], kp(t["w_ffn_down_2"]))

            sp.wait_ge(rows_ready, 6)
            sp.dma_start(out.rearrange("(a p) d -> p a d", p=P), xa[:, :, :]).then_inc(out_landed, 16)
            sp.wait_ge(out_landed, 16)

        @block.gpsimd
        def _(pool):
            rows = lambda ap: ap.partition_broadcast(P)

            def bias_table(u):
                if bias_of(u) is None:
                    return
                prev = [v for v in range(u % 2, u, 2) if bias_of(v) is not None]
                if prev:
                    pool.wait_ge(biased, prev[-1] + 1)
                pool.dma_start(bias[:, u % 2, :], t["t_bias"][bias_of(u)]).then_inc(bias_landed[u % 2], 16)

            def norm_rows(k, g, b):
                if k:
                    pool.wait_ge(norm_done, k)
                n = 0
                for dst, name in ((lng, g), (lnb, b)):
                    if name:
                        pool.dma_start(dst, rows(t[name])).then_inc(norm_rows_landed, 16 if b else 32)
                        n += 1

            pool.dma_start(ident[:, :], t["t_ident"]).then_inc(ident_landed, 16)
            pool.dma_start(rowsx, t["x"].rearrange("(a p) d -> p a d", p=P)).then_inc(x_landed, 16)
            for i, st in enumerate(STACKS):
                r = 0
                for name, n in st:
                    pool.dma_start(arena[r:r + n, i * P:(i + 1) * P], t[name]).then_inc(stack_landed, 16)
                    r += n
            pool.dma_start(lmask, t["t_small"][:, T_LEVEL:T_LEVEL + 8 * P].rearrange("p (a b) -> p a b", a=8))\
                .then_inc(level_tab_landed, 16)
            pool.dma_start(hgrow, rows(t["hgrn_norm_g"])).then_inc(level_tab_landed, 16)

            wait_copied(pool, o_of("hT"))
            ts = t["t_small"]
            half = lambda h: slice(64 * h, 64 * h + 64)
            loads = [
                (sgrow, t["sg_w"].rearrange("g q p -> q g p")),
                (tri, ts[:, T_TRI:T_TRI + P]),
                (slg, rows(t["sg_ln_g"])), (slb, rows(t["sg_ln_b"])),
                (invc, ts[:, T_COUNT:T_COUNT + 4 * S].rearrange("p (a b) -> p a b", a=4)),
                (poolw, t["pool_w"].rearrange("g c d -> c g d")),
                (ctab, ts[:, T_CBIAS:T_CBIAS + 480]),
                (posrow[0:64, 0:64], t["nsa_cmp_pos"]), (posrow[0:64, 64:128], t["nsa_cmp_pos"]),
                (cw[half(0)], t["nsa_cmp_w"].rearrange("i l d e -> d i l e")),
                (cw[half(1)], t["nsa_cmp_w"].rearrange("i l d e -> d i l e")),
            ]
            for dst, src in loads:
                pool.dma_start(dst, src).then_inc(mixer1_landed, 16)
            assert len(loads) == MIXER1_LOADS
            for u in range(U_NSA, U_X):
                bias_table(u)

            wait_copied(pool, o_of("nT"))
            pool.dma_start(xa[:, :, :], t["mem"].rearrange("(a p) d -> p a d", p=P)).then_inc(mem_landed, 16)
            norm_rows(0, "ln_mix_g", "ln_mix_b")
            wait_copied(pool, o_of("memT", 3))
            pool.dma_start(xa[:, :, :], t["x"].rearrange("(a p) d -> p a d", p=P)).then_inc(resid_landed, 16)
            norm_rows(1, "ln_x_g", "ln_x_b")
            norm_rows(2, "ln_ffn_g", "ln_ffn_b")

            wait_copied(pool, o_of("xT2", 3))
            pool.wait_ge(norm_done, 3)
            pool.memset(score[:, :, :], 0.0).then_inc(lru_zeroed, 1)
            pool.wait_ge(lru_zeroed, 1)
            for i, name in enumerate(("lru_wa_2", "lru_wx_2")):
                for h in range(2):
                    pool.dma_start(wl[half(h), i, :, half(h)],
                                   t[name].rearrange("(c h) k d -> h k c d", h=2)[h]).then_inc(lru_landed, 16)
            for j, name in enumerate(("diff_lq1_2", "diff_lk1_2", "diff_lq2_2", "diff_lk2_2")):
                pool.dma_start(lrow[:, 64 * j:64 * j + 64], rows(t[name])).then_inc(mixer2_landed, 16)
            pool.dma_start(sinks, rows(t["swa_sinks_2"])).then_inc(mixer2_landed, 16)
            pool.dma_start(subln, rows(t["diff_subln_2"])).then_inc(mixer2_landed, 16)
            pool.dma_start(heads[0:4], ts[0:4, T_HEAD:T_END].rearrange("p (h c) -> p h c", h=5))\
                .then_inc(mixer2_landed, 16)
            pool.dma_start(bf[0:4], t["fox_b_f_2"].rearrange("(a b) -> a b", b=1)).then_inc(mixer2_landed, 16)
            for u in range(U_DIFF, U_END):
                bias_table(u)
            wait_copied(pool, o_of("y3T"))
            norm_rows(3, "norm_final_2", None)

        @block.tensor
        def _(pe):
            mm, turn = nc.tensor.matmul, nc.tensor.transpose
            rows_done = Count(pe, pe_rows)

            def slot(n, k=KC, w=W, off=0):
                return ring[:, n % SLOTS, off:off + k * w].rearrange("p (k c) -> p k c", k=k)

            def landed(n, i=None, per=0):
                v = LANDED * (n // SLOTS + 1)
                pe.wait_ge(w_landed[n % SLOTS], v if i is None else i * (LANDED * per // SLOTS) + v)

            def features(dst, w, act, k0=0, kn=KC, c0=0, m=P, start=True, stop=True):
                for k in range(kn):
                    last = mm(dst, w[:, k, c0:c0 + m], act[:, k0 + k, :], start=start and k == 0,
                              stop=stop and k == kn - 1)
                return last

            def tokens(dst, w, act, q, k0=0, kn=KC, c0=0, m=W, start=True, stop=True):
                for k in range(kn):
                    last = mm(dst, act[:, k0 + k, q * P:(q + 1) * P], w[:, k, c0:c0 + m],
                              start=start and k == 0, stop=stop and k == kn - 1)
                return last

            def f_tile(n, o, act, i=None, per=0, operm=0):
                landed(n, i, per)
                wait_bank(o, i, operm)
                b = banks(o)
                for x in range(2):
                    last = features(b[:, x, 0:S], slot(n), act, c0=x * P)
                last.then_inc(tile_used, 1)

            def t_tile(n, o, act, i=None, per=0, operm=0):
                landed(n, i, per)
                wait_bank(o, i, operm)
                b = banks(o)
                for q in range(NT):
                    last = tokens(b[:, q, 0:W], slot(n), act, q)
                last.then_inc(tile_used, 1)

            def turn_rows(name, rows):
                for k in range(4):
                    o = o_of(name, k)
                    wait_bank(o)
                    b = banks(o).rearrange("p a (c t) -> p (a c) t", c=2)
                    for c in range(4):
                        for q in range(NT):
                            last = turn(b[:, c, q * P:(q + 1) * P],
                                        rows[:, q, (4 * k + c) * P:(4 * k + c + 1) * P], ident[:, :])
                    last.then_inc(part_done, 1)

            def turn_branch(name, rows):
                o = o_of(name)
                wait_bank(o)
                b = banks(o).rearrange("p a (c t) -> p (a c) t", c=2)
                for c in range(4):
                    for q in range(NT):
                        last = turn(b[:, c, q * P:(q + 1) * P], rows[:, q, c * P:(c + 1) * P], ident[:, :])
                last.then_inc(part_done, 1)

            def wait_all_copied(name, n):
                for k in range(max(0, n - 2), n):
                    wait_copied(pe, o_of(name, k))

            def merge(name):
                n0, _, o0 = at[name]
                with pe.Fori(0, D // W) as i:
                    for b in range(NBR):
                        landed(n0 + b, i, 4)
                        wait_bank(o0 + 2 * b, i, 8)
                        d = banks(o0 + 2 * b)
                        for x in range(2):
                            last = features(d[:, x, 0:S], slot(n0 + b), actT, c0=x * P)
                        last.then_inc(part_done, 1)
                        wait_bank(o0 + 2 * b + 1, i, 8)
                        d = banks(o0 + 2 * b + 1)
                        for x in range(2):
                            last = features(d[:, x, 0:S], slot(n0 + b, 4, W, KC * W), brT, k0=4 * b, kn=4, c0=x * P)
                        last.then_inc(tile_used, 1)

            def square(name, act):
                n0, _, o0 = at[name]
                with pe.Fori(0, 2) as i:
                    for k in range(4):
                        t_tile(n0 + k, o0 + k, act, i, 4, 4)

            def ff_in(name):
                n0, _, o0 = at[name]
                with pe.Fori(0, PAIRS // 2) as i:
                    for k in range(4):
                        f_tile(n0 + k, o0 + k, actT, i, 4, 4)

            def ff_out(name):
                n0, _, o0 = at[name]
                with pe.Fori(0, D // W // 2) as i:
                    for c in range(2):
                        wait_bank(o0 + c, i, 2)
                        b = banks(o0 + c)
                        for k in range(4):
                            n = n0 + 4 * c + k
                            landed(n, i, 8)
                            for q in range(NT):
                                last = tokens(b[:, q, 0:W], slot(n, DOWN_K), hT, q, k0=DOWN_K * k, kn=DOWN_K,
                                              start=k == 0, stop=k == 3)
                            last.then_inc(tile_used, 1)

            def scores(u):
                q_, k_, extra, _, _ = unit(u)
                if u >= 2:
                    pe.wait_ge(biased, u - 1)
                for m in range(2):
                    dst = sc[:, u % 2, m * S:(m + 1) * S]
                    more = extra(m)
                    last = mm(dst, q_(m), k_(m), start=True, stop=not more)
                    for x, (l_, r_) in enumerate(more):
                        last = mm(dst, l_, r_, start=False, stop=x == len(more) - 1)
                    if m == 0 and not (U_X <= u < U_DIFF or U_FOX <= u < U_SWA):
                        rows_done.link(last)
                last.then_inc(scores_done, 1)

            def turn_probs(u):
                pe.wait_ge(probs_ready, u + 1)
                if u:
                    pe.wait_ge(probT_ready, u)
                for x in range(4):
                    last = turn(pt[:, x * P:(x + 1) * P], score[:, u % 2, x * P:(x + 1) * P], ident[:, :])
                last.then_inc(probs_turned, 1)

            def values(u):
                _, _, _, v_, dv = unit(u)
                pe.wait_ge(probT_ready, u + 1)
                if u:
                    pe.wait_ge(pv_used, u)
                for m in range(2):
                    for kt in range(NT):
                        last = mm(pv[:, m * dv:(m + 1) * dv], probT[:, u % 2, (2 * m + kt) * P:(2 * m + kt + 1) * P],
                                  v_(m, kt), start=kt == 0, stop=kt == NT - 1)
                last.then_inc(pv_done, 1)

            def attend(a, b):
                scores(a)
                for u in range(a, b):
                    if u + 1 < b:
                        scores(u + 1)
                    turn_probs(u)
                    values(u)

            pe.wait_ge(ident_landed, 16)
            pe.wait_ge(stack_landed, 16 * sum(len(s_) for s_ in STACKS))
            for i, st in enumerate(STACKS):
                r = sum(n for _, n in st)
                last = turn(acc[:, 0, i * P:i * P + r], arena[0:r, i * P:(i + 1) * P], ident[0:r, 0:r])
            last.then_inc(part_done, 1)
            pe.wait_ge(x_landed, 16)
            turn_rows("xT1", rowsx)
            wait_all_copied("xT1", 4)

            n, o = at["hin"][0], o_of("hin")
            for k in range(8):
                (f_tile if k < 4 else t_tile)(n + k, o + k, actT)

            def b_tile_products(k):
                n, _, o = at[f"b{k}"]
                if k in (0, 1, 2, 6, 7):
                    f_tile(n, o, actT)
                elif k in (3, 4):
                    key_value_tile(n, o)
                elif k == 5:
                    landed(n)
                    wait_bank(o)
                    for q in range(NT):
                        last = tokens(banks(o)[:, 0, q * 24:(q + 1) * 24], slot(n, KC, 24), actT, q, m=24)
                    last.then_inc(tile_used, 1)
                else:
                    t_tile(n, o, actT)

            def key_value_tile(n, o):
                landed(n)
                wait_bank(o)
                b = banks(o)
                features(b[:, 0, 0:S], slot(n), actT)
                for q in range(NT):
                    last = tokens(b[:, 1, q * P:(q + 1) * P], slot(n), actT, q, c0=P, m=P)
                last.then_inc(tile_used, 1)

            n = 0
            for lv in range(HL + 2):
                pe.wait_ge(level_ready, lv + 1)
                o = o_of(f"lvl{lv}")
                wait_bank(o)
                b = banks(o)
                if lv <= HL:
                    for q in range(NT):
                        for h in range(4):
                            last = mm(b[:, q, h * P:(h + 1) * P], hkd[:, h, q * P:(q + 1) * P],
                                      hqd[:, h, q * P:(q + 1) * P], start=True, stop=True)
                else:
                    for h in range(4):
                        last = mm(b[:, 0, h * P:(h + 1) * P], hkd[:, h, 0:P], hqd[:, h, P:S], start=True, stop=True)
                last.then_inc(part_done, 1)
                for _ in range(B_AFTER[lv]):
                    b_tile_products(n)
                    n += 1
            pe.wait_ge(decay_ready, 1)
            o = o_of("ho")
            wait_bank(o)
            b = banks(o)
            A = lambda q, h: ATd[:, (q * 4 + h) * P:(q * 4 + h + 1) * P]
            for h in range(4):
                hs = slice(h * P, (h + 1) * P)
                mm(b[:, 0, hs], A(0, h), hi[:, 0, hs], start=True, stop=True)
                mm(b[:, 1, hs], A(1, h), hi[:, 1, hs], start=True, stop=False)
                last = mm(b[:, 1, hs], ATx[:, h, :], hi[:, 0, hs], start=False, stop=True)
            last.then_inc(part_done, 1)
            pe.wait_ge(mixer_rows, 1)
            turn_branch("hT", ho)

            pe.wait_ge(mixer1_landed, 16 * MIXER1_LOADS)
            o = o_of("sgw")
            wait_bank(o)
            for g in range(4):
                last = turn(banks(o)[:, 0, g * P:(g + 1) * P], sgrow[:, g, :], ident[:, :])
            last.then_inc(part_done, 1)
            pe.wait_ge(mixer_rows, 2)
            o = o_of("pool")
            wait_bank(o)
            b = banks(o).rearrange("p a (c t) -> p (a c) t", c=2)
            for g in range(4):
                last = mm(b[:, g, :], poolw[:, g, :], ping[:, g, 16:], start=True, stop=True)
            last.then_inc(part_done, 1)
            pe.wait_ge(mixer_rows, 3)
            o = o_of("sgo")
            wait_bank(o)
            for q in range(NT):
                for g in range(4):
                    gs = slice(g * P, (g + 1) * P)
                    last = mm(banks(o)[:, q, gs], wmT[:, g, :], sv[:, q, gs], start=True, stop=True)
            last.then_inc(part_done, 1)
            pe.wait_ge(mixer_rows, 4)
            turn_branch("sgT", su)

            o = o_of("pos")
            wait_bank(o)
            turn(banks(o)[:, 0, 0:64], posrow[0:64, :], ident[0:64, 0:64]).then_inc(part_done, 1)
            pe.wait_ge(cmp_ready, 1)
            o = o_of("ckv")
            wait_bank(o)
            b = banks(o)
            for g in range(2):
                gh = slice(64 * g, 64 * g + 64)
                for l in range(32):
                    mm(b[gh, 0, 0:NC], cw[gh, 0, l, :], win[gh, 0, l, :], start=l == 0, stop=l == 31)
            for g in range(2):
                gh = slice(64 * g, 64 * g + 64)
                for l in range(32):
                    last = mm(b[0:NC, 1, gh], win[gh, 1, l, :], cw[gh, 1, l, :], start=l == 0, stop=l == 31)
                if g == 0:
                    rows_done.link(last)
            last.then_inc(part_done, 1)
            wait_copied(pe, o_of("ckv"))
            o = o_of("cs")
            wait_bank(o)
            b = banks(o)
            for g in range(2):
                gh = slice(64 * g, 64 * g + 64)
                for q in range(NT):
                    for h in range(4 * g, 4 * g + 4):
                        last = mm(b[:, q, h * NC:(h + 1) * NC], qn[gh, h % 4, q * P:(q + 1) * P], kcmp[gh, :],
                                  start=True, stop=True)
                if g == 0:
                    rows_done.link(last)
            last.then_inc(part_done, 1)
            pe.wait_ge(cmp_ready, 3)
            for q in range(NT):
                o = o_of("cT", q)
                wait_bank(o)
                b = banks(o).rearrange("p a (c t) -> p (a c) t", c=4)
                for h in range(NH):
                    at_ = (q * NH + h) * NC
                    last = turn(b[0:NC, h, :], cS[:, at_:at_ + NC], ident[:, :])
                last.then_inc(part_done, 1)
            wait_copied(pe, o_of("cT", 0))
            wait_copied(pe, o_of("cT", 1))
            o = o_of("co")
            wait_bank(o)
            for q in range(NT):
                for h in range(NH):
                    g = h // 4
                    last = mm(banks(o)[:, q, 64 * h:64 * h + 64], cPT[0:NC, q * NH + h, :],
                              vcmp[0:NC, 64 * g:64 * g + 64], start=True, stop=True)
            last.then_inc(part_done, 1)
            attend(U_NSA, U_X)
            pe.wait_ge(mixer_rows, 5)
            turn_branch("nT", oa)
            wait_copied(pe, o_of("nT"))

            merge("merge1")
            pe.wait_ge(rows_ready, 1)
            turn_rows("memT", xa)
            wait_all_copied("memT", 4)
            for k in range(2):
                f_tile(at["xk"][0] + k, o_of("xk", k), memT)
            for k in range(2):
                t_tile(at["xv"][0] + k, o_of("xv", k), memT)
            pe.wait_ge(gate_used, 8)
            square("mixout1", mixT)

            pe.wait_ge(rows_ready, 2)
            turn_rows("x1T", xa)
            wait_all_copied("x1T", 4)
            for k in range(2):
                f_tile(at["xq"][0] + k, o_of("xq", k), actT)
            wait_all_copied("xq", 2)
            attend(U_X, U_DIFF)
            pe.wait_ge(mixer_rows, 6)
            turn_branch("xoT", ox)
            wait_copied(pe, o_of("xoT"))
            for c in range(2):
                n = at["xo"][0] + c
                landed(n)
                for k in range(4):
                    o = o_of("xo", 4 * c + k)
                    wait_bank(o)
                    for q in range(NT):
                        last = tokens(banks(o)[:, q, 0:W], slot(n, 4, 4 * W), oxT, q, kn=4, c0=k * W)
                    last.then_inc(tile_used if k == 3 else part_done, 1)

            pe.wait_ge(rows_ready, 3)
            turn_rows("x2T", xa)
            wait_all_copied("x2T", 4)
            ff_in("ffin1")
            wait_all_copied("ffin1", 44)
            ff_out("ffout1")

            pe.wait_ge(rows_ready, 4)
            turn_rows("xT2", rowsx)
            wait_all_copied("xT2", 4)
            n, o = at["in2"][0], o_of("in2")
            for k in range(16):
                (t_tile if k in (4, 5, 14, 15) else f_tile)(n + k, o + k, actT)
            landed(n + 16)
            wait_bank(o + 16)
            features(banks(o + 16)[0:4, 0, 0:S], slot(n + 16, KC, 4), actT, m=4).then_inc(tile_used, 1)
            for k in (17, 18):
                f_tile(n + k, o + k, actT)
            key_value_tile(n + 19, o + 19)

            pe.wait_ge(lru_landed, 64)
            pe.wait_ge(lru_conv, 1)
            for w_ in range(2):
                o = o_of("lru", w_)
                wait_bank(o)
                b = banks(o).rearrange("p a (c t) -> p (a c) t", c=2)
                for c in range(4):
                    last = mm(b[:, c, :], wl[:, w_, c, :], xc[:, c, :], start=True, stop=True)
                last.then_inc(part_done, 1)

            pe.wait_ge(mixer_rows, 7)
            attend(U_DIFF, U_END)
            pe.wait_ge(mixer_rows, 8)
            for name, rows in (("y0T", ya), ("y2T", yc), ("y3T", yd)):
                turn_branch(name, rows)
            wait_copied(pe, o_of("y2T"))
            wait_copied(pe, o_of("y3T"))
            merge("merge2")
            pe.wait_ge(gate_used, 16)
            square("mixout2", mixT)
            pe.wait_ge(rows_ready, 5)
            turn_rows("x3T", rowsx)
            wait_all_copied("x3T", 4)
            ff_in("ffin2")
            wait_all_copied("ffin2", 44)
            ff_out("ffout2")

        @block.scalar
        def _(act):
            f = nc.scalar.activation
            own = Count(act, s_link)

            def halves(o):
                return banks(o)[:, :, 0:S]

            def tile_out(name, k, dst, func=ACT.Copy, src=None, scale=1.0):
                o = o_of(name, k)
                wait_tile(act, name, k)
                release(f(dst, halves(o) if src is None else src(banks(o)), func, scale=scale), o)

            def part_out(name, k, dst, func=ACT.Copy, src=None):
                o = o_of(name, k)
                wait_part(act, name, k)
                release(f(dst, banks(o) if src is None else src(banks(o)), func), o)

            def turned_out(name, dst):
                for k in range(4):
                    part_out(name, k, dst[:, 4 * k:4 * k + 4, :].rearrange("p (a c) t -> p a (c t)", a=2))

            def branch_out(name, chunk):
                part_out(name, 0, brT[:, chunk:chunk + 4, :].rearrange("p (a c) t -> p a (c t)", a=2))

            def root(k, n):
                act.wait_ge(var_ready, k)
                f(stats[:, 72:72 + n], stats[:, 64:64 + n], ACT.Sqrt).then_inc(std_ready, 1)

            def exps(u):
                act.wait_ge(max_ready, u + 1)
                c = 2 * (u % 4)
                for m in range(2):
                    s_ = score[:, u % 2, m * S:(m + 1) * S]
                    last = f(s_, s_, ACT.Exp, bias=vecs[:, c + m:c + m + 1],
                             accum_out=vecs[:, 8 + c + m:9 + c + m])
                if u >= U_SWA:
                    for m in range(2):
                        h = ((u - U_SWA) // 2) + 4 * m
                        last = f(vecs[:, 24 + c + m:25 + c + m], sinks[:, h:h + 1], ACT.Exp,
                                 bias=vecs[:, c + m:c + m + 1])
                last.then_inc(probs_ready, 1)

            def copy_probs(u):
                act.wait_ge(probs_turned, u + 1)
                if u >= 2:
                    act.wait_ge(pv_done, u - 1)
                f(probT[:, u % 2, :], pt[:, :], ACT.Copy).then_inc(probT_ready, 1)

            def attend(a, b):
                exps(a)
                for u in range(a, b):
                    if u + 1 < b:
                        exps(u + 1)
                    copy_probs(u)

            wait_part(act, "cols")
            for i, st in enumerate(STACKS):
                r = sum(n for _, n in st)
                last = f(cols[:, i, 0:r], acc[:, 0, i * P:i * P + r], ACT.Copy)
            release(last, o_of("cols"))
            act.wait_ge(lb_max, 1)
            f(lbv[:, 4:8], lbv[:, 0:4], ACT.Exp).then_inc(lb_exp, 1)
            turned_out("xT1", actT)

            for k in range(2):
                tile_out("hin", k, hq[:, 2 * k:2 * k + 2, :])
            for k in range(2):
                tile_out("hin", 2 + k, hp[:, 2 * k:2 * k + 2, :], ACT.Sigmoid)
            for k in range(2):
                tile_out("hin", 4 + k, hi[:, :, k * W:(k + 1) * W])
            for k in range(2):
                tile_out("hin", 6 + k, hg[:, :, k * W:(k + 1) * W], ACT.Silu)
            for k in range(2):
                tile_out(f"b{k}", 0, qn[:, 2 * k:2 * k + 2, :])
            for k, dst in enumerate((kvc, kvs, kvw)):
                tile_out(f"b{2 + k}", 0, dst)
            tile_out("b5", 0, ag.rearrange("p a b -> p (a b)"), ACT.Sigmoid, src=lambda b: b[:, 0, 0:48])
            for k in range(2):
                tile_out(f"b{6 + k}", 0, cpad[:, 2 * k:2 * k + 2, 16:])
            for k in range(2):
                tile_out(f"b{8 + k}", 0, su[:, :, k * W:(k + 1) * W], ACT.Gelu_apprx_tanh)
            for k in range(2):
                tile_out(f"b{10 + k}", 0, sv[:, :, k * W:(k + 1) * W], ACT.Gelu_apprx_tanh)
            part_out("ho", 0, ho)
            root(1, 8)
            branch_out("hT", 4)
            root(2, 2)
            branch_out("sgT", 12)
            act.wait_ge(cmp_ready, 2)
            f(cS, cS, ACT.Exp).then_inc(cmp_exp, 1)
            for q in range(NT):
                part_out("cT", q, cPT[0:NC, q * NH:(q + 1) * NH, :].rearrange("p (a c) t -> p a (c t)", a=2),
                         src=lambda b: b[0:NC])
            attend(U_NSA, U_X)
            branch_out("nT", 0)
            root(3, 2)

            n0, p0, o0 = at["merge1"]
            with act.Fori(0, D // W) as i:
                for b in range(NBR):
                    o = o0 + 2 * b
                    act.wait_ge(part_done, i * 4 + (p0 + b + 1))
                    act.wait_ge(acc_free[(o + 1) % 2], i * 4 + ((o + 1) // 2 + 1 - 2))
                    release(f(gateS[:, b % 2, :].rearrange("p (a c) -> p a c", a=2), halves(o), ACT.Sigmoid), o)

            act.wait_ge(gate_used, 8)
            for k in range(4):
                wait_part(act, "memT", k)
                b = banks(o_of("memT", k)).rearrange("p a (c t) -> p (a c) t", c=2)
                for c in range(4):
                    last = f(memT[:, 4 * k + c, :], b[:, c, :], ACT.Identity,
                             scale=col("mem_ln_g", 4 * k + c), bias=col("mem_ln_b", 4 * k + c))
                release(last, o_of("memT", k))
            for k in range(2):
                tile_out("xk", k, kx[:, 2 * k:2 * k + 2, :])
            for k in range(2):
                tile_out("xv", k, vx[:, :, k * W:(k + 1) * W])
            root(4, 2)
            turned_out("x1T", actT)
            for k in range(2):
                tile_out("xq", k, qx[:, 2 * k:2 * k + 2, :])
            attend(U_X, U_DIFF)
            part_out("xoT", 0, oxT.rearrange("p (a c) t -> p a (c t)", a=2))
            root(5, 2)
            turned_out("x2T", actT)

            _, _, o0 = at["ffin1"]
            with act.Fori(0, PAIRS // 2) as i:
                for k in range(2):
                    o = o0 + 2 * k
                    act.wait_ge(acc_free[o % 2], i * 2 + (o // 2 + 1))
                    f(siluS[:, k, :], convS[:, k, :], ACT.Silu).then_inc(silu_ready, 1)
            root(6, 2)
            root(7, 2)

            def pair_out(k, dst, func=ACT.Copy, scale=1.0):
                for x in range(2):
                    tile_out("in2", k + x, dst[:, 2 * x:2 * x + 2, :], func, scale=scale)

            def rows_out(k, dst):
                for x in range(2):
                    tile_out("in2", k + x, dst[:, :, x * W:(x + 1) * W])

            pair_out(0, aq)
            pair_out(2, ak)
            rows_out(4, av)
            pair_out(6, bx[:, :, 4:])
            pair_out(8, bg, ACT.Gelu_apprx_tanh)
            pair_out(10, cq, scale=P ** -0.5)
            pair_out(12, ck)
            rows_out(14, cv)
            tile_out("in2", 16, cf[0:4, :], src=lambda b: b[0:4, 0, 0:S])
            pair_out(17, dq)
            tile_out("in2", 19, dkv)

            act.wait_ge(sp_abs, 1)
            f(lbv[:, 20:24], lbv[:, 16:20], ACT.Exp).then_inc(sp_exp, 1)
            for w_, (dst, bcol) in enumerate(((lr, "lru_ba_2"), (li, "lru_bx_2"))):
                wait_part(act, "lru", w_)
                b = banks(o_of("lru", w_)).rearrange("p a (c t) -> p (a c) t", c=2)
                for c in range(4):
                    last = f(dst[:, c, :], b[:, c, :], ACT.Sigmoid, bias=col(bcol, c))
                release(last, o_of("lru", w_))
            act.wait_ge(lru_arg, 1)
            f(lt, lr, ACT.Tanh, scale=-1.0)
            f(la, lr, ACT.Exp).then_inc(lru_exp, 1)
            act.wait_ge(lru_sq, 1)
            f(lt, lt, ACT.Sqrt, scale=2.0).then_inc(lru_sqrt, 1)
            act.wait_ge(sp_abs, 2)
            f(li[0:4, 1, :], li[0:4, 0, :], ACT.Exp).then_inc(sp_exp, 1)
            act.wait_ge(lam_sum, 1)
            f(lbv[:, 34:36], lbv[:, 32:34], ACT.Exp).then_inc(lam_exp, 1)
            attend(U_DIFF, U_END)
            root(8, 8)
            branch_out("y0T", 0)
            branch_out("y2T", 8)
            branch_out("y3T", 12)

            n0, p0, o0 = at["merge2"]
            with act.Fori(0, D // W) as i:
                for b in range(NBR):
                    o = o0 + 2 * b
                    act.wait_ge(acc_free[o % 2], i * 4 + (o // 2 + 1))
                    f(gateS[:, b % 2, :], gateS[:, b % 2, :], ACT.Sigmoid).then_inc(gate_ready, 1)
            root(9, 2)

            n0, _, o0 = at["ffin2"]
            with act.Fori(0, PAIRS // 2) as i:
                for k in range(2):
                    o = o0 + 2 * k
                    act.wait_ge(tile_used, i * 4 + (n0 + 2 * k + 1))
                    act.wait_ge(acc_free[(o + 1) % 2], i * 2 + ((o + 1) // 2 + 1 - 2))
                    release(f(siluS[:, k, :].rearrange("p (a c) -> p a c", a=2), halves(o), ACT.Silu), o)
            root(10, 2)

        @block.vector
        def _(dve):
            v = nc.vector
            own = Count(dve, v_link)
            link = own.link
            tt, ts_, stt = v.tensor_tensor, v.tensor_scalar, v.scalar_tensor_tensor
            mean_var = stats[:, 48:52].rearrange("p (q x) -> p q x", q=NT)
            rstd = stats[:, 80:88]

            def root(k, n):
                dve.wait_ge(std_ready, k)
                link(v.reciprocal(rstd[:, 0:n], stats[:, 72:72 + n]))

            def moments(X, width, k, eps, rms=False):
                g = width // 512
                st = stats[:, 0:NT * g * 6].rearrange("p (q g x) -> p q g x", q=NT, g=g)
                for q in range(NT):
                    for s_ in range(g):
                        own.tick(v.bn_stats(st[:, q, s_, :], X[:, q, s_ * 512:(s_ + 1) * 512]))
                own.done()
                for q in range(NT):
                    own.tick(v.bn_aggr(mean_var[:, q, :], st[:, q, :, :].rearrange("p g x -> p (g x)")))
                own.done()
                if rms:
                    link(tt(stats[:, 56:58], mean_var[:, :, 0], mean_var[:, :, 0], ALU.mult))
                    link(tt(mean_var[:, :, 1], stats[:, 56:58], mean_var[:, :, 1], ALU.add))
                ts_(stats[:, 64:66], mean_var[:, :, 1], eps, None, ALU.add).then_inc(var_ready, 1)
                root(k, 2)

            def center(dst, X):
                for q in range(NT):
                    own.tick(ts_(dst[:, q, :], X[:, q, :], mean_var[:, q, 0:1], rstd[:, q:q + 1],
                                 ALU.subtract, ALU.mult))
                own.done()

            def layer_norm_rows(k, rows_k, count):
                moments(xa, D, rows_k, LN_EPS)
                center(xa, xa)
                dve.wait_ge(norm_rows_landed, 32 * (k + 1))
                link(tt(xa[:, :, :], xa[:, :, :], lng.unsqueeze(1).broadcast_to([P, NT, D]), ALU.mult))
                ins = tt(xa[:, :, :], xa[:, :, :], lnb.unsqueeze(1).broadcast_to([P, NT, D]), ALU.add)
                if count:
                    ins.then_inc(rows_ready, 1)
                    dve.wait_ge(rows_ready, count)
                else:
                    link(ins)
                v.memset(stats[:, 90:91], 0.0).then_inc(norm_done, 1)

            def rms_rows(dst, k, count):
                moments(xa, D, k, RMS_EPS, rms=True)
                for q in range(NT):
                    ins = ts_(dst[:, q, :], xa[:, q, :], rstd[:, q:q + 1], None, ALU.mult)
                ins.then_inc(rows_ready, 1)

            def scaled_out(name, norm):
                for k in range(4):
                    wait_part(dve, name, k)
                    o = o_of(name, k)
                    b = banks(o).rearrange("p a (c t) -> p (a c) t", c=2)
                    release(tt(actT[:, 4 * k:4 * k + 4, :], b,
                               col(norm, 4 * k, 4).unsqueeze(2).broadcast_to([P, 4, S]), ALU.mult), o)

            def log1p(z, s_, s2, p_):
                link(ts_(s_, z, 2.0, None, ALU.add))
                link(v.reciprocal(s_, s_))
                link(tt(s_, s_, z, ALU.mult))
                link(tt(s2, s_, s_, ALU.mult))
                link(ts_(p_, s2, 1.0 / 15, None, ALU.mult))
                for c in (13, 11, 9, 7, 5, 3):
                    link(stt(p_, p_, 1.0 / c, s2, ALU.add, ALU.mult))
                link(stt(p_, p_, 1.0, s_, ALU.add, ALU.mult))
                link(ts_(p_, p_, 2.0, None, ALU.mult))

            def before(u):
                dve.wait_ge(scores_done, u + 1)
                if u >= 2:
                    dve.wait_ge(probs_turned, u - 1)
                S_ = score[:, u % 2, :]
                if bias_of(u) is None:
                    ts_(S_, sc[:, u % 2, :], scale_of(u), None, ALU.mult).then_inc(biased, 1)
                else:
                    dve.wait_ge(bias_landed[u % 2], 16 * biased_before(u))
                    stt(S_, sc[:, u % 2, :], scale_of(u), bias[:, u % 2, :], ALU.mult, ALU.add).then_inc(biased, 1)
                dve.wait_ge(biased, u + 1)
                c = 2 * (u % 4)
                ins = v.tensor_reduce(vecs[:, c:c + 2], S_.rearrange("p (m k) -> p m k", m=2), AX, ALU.max, negate=True)
                if u >= U_SWA:
                    link(ins)
                    j = (u - U_SWA) // 2
                    ins = tt(vecs[:, c:c + 2], vecs[:, c:c + 2], vecs[:, 40 + j:48:4], ALU.min)
                ins.then_inc(max_ready, 1)

            def after(u):
                q, c = u % 2, 2 * (u % 4)
                rr = vecs[:, 16 + c:18 + c]
                dve.wait_ge(probs_ready, u + 1)
                if u >= U_SWA:
                    link(tt(vecs[:, 8 + c:10 + c], vecs[:, 8 + c:10 + c], vecs[:, 24 + c:26 + c], ALU.add))
                link(v.reciprocal(rr, vecs[:, 8 + c:10 + c]))
                if u < U_X:
                    j = (u // 2) % 4
                    link(tt(rr, rr, ag[:, q, :].rearrange("p (h r) -> p h r", r=3)[:, j::4, 1 + u // 8], ALU.mult))
                elif U_DIFF <= u < U_FOX:
                    link(tt(rr[:, 1:2], rr[:, 1:2], lbv[:, 36:37], ALU.mult))
                dve.wait_ge(pv_done, u + 1)
                for m in range(2):
                    r_ = rr[:, m:m + 1]
                    if u < U_X:
                        h = (u // 2) % 4 + 4 * m
                        dst = oa[:, q, 64 * h:64 * h + 64]
                        ins = stt(dst, pv[:, 64 * m:64 * m + 64], r_, dst, ALU.mult, ALU.add)
                    elif U_DIFF <= u < U_FOX:
                        h = (u - U_DIFF) // 2
                        dst = ya[:, q, h * P:(h + 1) * P]
                        if m == 0:
                            link(ts_(dst, pv[:, 0:P], r_, None, ALU.mult))
                        else:
                            ins = stt(dst, pv[:, P:2 * P], r_, dst, ALU.mult, ALU.add)
                    elif u >= U_SWA:
                        h = (u - U_SWA) // 2 + 4 * m
                        ins = ts_(yd[:, q, 64 * h:64 * h + 64], pv[:, 64 * m:64 * m + 64], r_, None, ALU.mult)
                    else:
                        rows, h = (ox, 2 * ((u - U_X) // 2) + m) if u < U_DIFF else (yc, 2 * ((u - U_FOX) // 2) + m)
                        ins = ts_(rows[:, q, h * P:(h + 1) * P], pv[:, m * P:(m + 1) * P], r_, None, ALU.mult)
                ins.then_inc(pv_used, 1)

            def attend(a, b):
                before(a)
                for u in range(a, b):
                    if u + 1 < b:
                        before(u + 1)
                    after(u)
                dve.wait_ge(pv_used, b)

            wait_copied(dve, o_of("cols"))
            tt(lbv[:, 0:4], col("hgrn_lb_logits", 0, 4), col("hgrn_lb_logits", 0, 4), ALU.subtract).then_inc(lb_max, 1)
            dve.wait_ge(lb_exp, 1)
            link(v.reciprocal(lbv[:, 8:12], lbv[:, 4:8]))
            link(tt(lbv[:, 4:8], lbv[:, 4:8], lbv[:, 8:12], ALU.mult))
            link(tt(lbv[:, 8:12], lbv[:, 4:8], lbv[:, 4:8], ALU.subtract))
            link(ts_(lbv[:, 12:16], lbv[:, 8:12], -1.0, 1.0, ALU.mult, ALU.add))

            wait_copied(dve, o_of("hin", 2))
            wait_copied(dve, o_of("hin", 3))
            for h in range(4):
                own.tick(ts_(hp[:, h, :], hp[:, h, :], lbv[:, 12 + h:13 + h], lbv[:, 8 + h:9 + h], ALU.mult, ALU.add))
            own.done()
            link(ts_(hp, hp, 1e-6, None, ALU.max))
            link(ts_(hk, hp, -1.0, 1.0, ALU.mult, ALU.add))
            link(v.memset(hr, 1.0))
            link(v.memset(cpad[:, :, 0:16], 0.0))
            dve.wait_ge(level_tab_landed, 32)
            flat = lambda ap: ap.rearrange("p h t -> p (h t)")
            for lv in range(HL + 2):
                if lv:
                    wait_part(dve, f"lvl{lv - 1}")
                if lv == 0:
                    own.tick(v.tensor_copy(hqd, hq))
                    v.tensor_copy(hkd, hk).then_inc(level_ready, 1)
                else:
                    own.tick(tt(hqd, hq, hp, ALU.mult))
                    tt(hkd, hk, hr, ALU.mult).then_inc(level_ready, 1)
                if 1 <= lv <= HL:
                    h = 1 << (lv - 1)
                    P4 = flat(hp).rearrange("p (n z h) -> p n z h", z=2, h=h)
                    R4 = flat(hr).rearrange("p (n z h) -> p n z h", z=2, h=h)
                    n = 4 * S // (2 * h)
                    dve.wait_ge(level_ready, lv + 1)
                    link(tt(R4[:, :, 0, :], R4[:, :, 0, :], P4[:, :, 1, h - 1:h].broadcast_to([P, n, h]), ALU.mult))
                    link(tt(P4[:, :, 1, :], P4[:, :, 1, :], P4[:, :, 0, h - 1:h].broadcast_to([P, n, h]), ALU.mult))
                wait_part(dve, f"lvl{lv}")
                o = o_of(f"lvl{lv}")
                b = banks(o).rearrange("p a (h t) -> p (a h) t", h=4)
                if lv > HL:
                    release(v.tensor_copy(ATx, banks(o)[:, 0, :].rearrange("p (h t) -> p h t", h=4)), o)
                    wait_copied(dve, o)
                    continue
                mask = lmask[:, lv, :].unsqueeze(1).broadcast_to([P, 8, P])
                A3, tmp3 = (x.rearrange("p (a t) -> p a t", a=8) for x in (ATd, htmp))
                release(tt(A3 if lv == 0 else tmp3, b, mask, ALU.mult), o)
                wait_copied(dve, o)
                if lv:
                    link(tt(ATd, ATd, htmp, ALU.add))
            v.memset(stats[:, 92:93], 0.0).then_inc(decay_ready, 1)
            wait_copied(dve, o_of("ho"))
            hof = ho.rearrange("p q (h e) -> p (q h) e", h=4)
            tmpf = htmp.rearrange("p (a e) -> p a e", a=8)
            link(tt(tmpf, hof, hof, ALU.mult))
            link(v.tensor_reduce(stats[:, 56:64], tmpf, AX, ALU.add))
            ts_(stats[:, 64:72], stats[:, 56:64], 1.0 / P, LN_EPS, ALU.mult, ALU.add).then_inc(var_ready, 1)
            root(1, 8)
            link(tt(hof, hof, rstd.unsqueeze(2).broadcast_to([P, 8, P]), ALU.mult))
            link(tt(ho, ho, hgrow.unsqueeze(1).broadcast_to([P, NT, 512]), ALU.mult))
            tt(ho, ho, hg, ALU.mult).then_inc(mixer_rows, 1)

            wait_part(dve, "sgw")
            dve.wait_ge(mixer1_landed, 16 * MIXER1_LOADS)
            release(tt(wmT, banks(o_of("sgw"))[:, 0, :].rearrange("p (g t) -> p g t", g=4),
                       tri.unsqueeze(1).broadcast_to([P, 4, P]), ALU.mult), o_of("sgw"))

            wait_copied(dve, o_of("b6"))
            wait_copied(dve, o_of("b7"))
            own.tick(v.memset(ping[:, :, 0:16], 0.0))
            link(v.memset(pong[:, :, 0:16], 0.0))
            src = cpad
            for g, dst in enumerate((ping, pong, ping, pong)):
                w_ = 1 << g
                link(tt(dst[:, g:, 16:], src[:, g:, 16:], src[:, g:, 16 - w_:16 + S - w_], ALU.add))
                src = dst
            for g in range(4):
                own.tick(tt(ping[:, g, 16:], (ping, pong)[g % 2][:, g, 16:], invc[:, g, :], ALU.mult))
            own.done()
            tt(ping[:, :, 16:], ping[:, :, 16:], cpad[:, :, 16:], ALU.subtract).then_inc(mixer_rows, 1)
            wait_part(dve, "pool")
            o = o_of("pool")
            release(tt(brT[:, 8:12, :], banks(o).rearrange("p a (c t) -> p (a c) t", c=2),
                       col("pool_scale", 0, 4).unsqueeze(2).broadcast_to([P, 4, S]), ALU.mult), o)

            wait_copied(dve, o_of("b10"))
            wait_copied(dve, o_of("b11"))
            moments(sv, 512, 2, LN_EPS)
            center(sv, sv)
            link(tt(sv, sv, slg.unsqueeze(1).broadcast_to([P, NT, 512]), ALU.mult))
            tt(sv, sv, slb.unsqueeze(1).broadcast_to([P, NT, 512]), ALU.add).then_inc(mixer_rows, 1)
            wait_part(dve, "sgo")
            o = o_of("sgo")
            for g in range(4):
                gs = slice(g * P, (g + 1) * P)
                ins = stt(su[:, :, gs], banks(o)[:, :, gs], col("sg_b", g), su[:, :, gs], ALU.add, ALU.mult)
                if g == 2:
                    own.tick(ins)
            release(ins, o)
            wait_copied(dve, o)
            v.memset(stats[:, 93:94], 0.0).then_inc(mixer_rows, 1)

            wait_part(dve, "pos")
            o = o_of("pos")
            release(v.tensor_copy(posT.rearrange("p a b -> p (a b)"), banks(o)[:, 0, 0:64]), o)
            wait_copied(dve, o)
            for i in range(2):
                x = kvc[:, i, :].rearrange("p (m b) -> p b m", b=16)
                for a in range(2):
                    ins = tt(win[:, i, 16 * a:16 * a + 16, :], x[:, :, a:a + NC],
                             posT[:, i, 16 * a:16 * a + 16].unsqueeze(2).broadcast_to([P, 16, NC]), ALU.add)
            ins.then_inc(cmp_ready, 1)
            wait_part(dve, "ckv")
            o = o_of("ckv")
            v.tensor_copy(kcmp, banks(o)[:, 0, 0:NC])
            release(v.tensor_copy(vcmp[0:NC, :], banks(o)[0:NC, 1, 0:P]), o)
            wait_part(dve, "cs")
            o = o_of("cs")
            cS2 = cS.rearrange("p (q c) -> p q c", q=NT)
            cS3 = cS.rearrange("p (a c) -> p a c", c=NC)
            release(stt(cS2, banks(o)[:, :, 0:NH * NC], 64 ** -0.5,
                        ctab[:, 0:240].rearrange("p (q c) -> p q c", q=NT), ALU.mult, ALU.add), o)
            wait_copied(dve, o)
            link(v.tensor_reduce(csm[:, 0:16], cS3, AX, ALU.max))
            tt(cS3, cS3, csm[:, 0:16].unsqueeze(2).broadcast_to([P, 16, NC]), ALU.subtract).then_inc(cmp_ready, 1)
            dve.wait_ge(cmp_exp, 1)
            link(v.tensor_reduce(csm[:, 16:32], cS3, AX, ALU.add))
            link(v.reciprocal(csm[:, 32:48], csm[:, 16:32]))
            link(tt(csm[:, 48:64].rearrange("p (q h) -> p q h", q=NT),
                    csm[:, 32:48].rearrange("p (q h) -> p q h", q=NT),
                    ag.rearrange("p q (h r) -> p q h r", r=3)[:, :, :, 0], ALU.mult))
            tt(cS, cS, ctab[:, 240:480], ALU.mult).then_inc(cmp_ready, 1)
            wait_part(dve, "co")
            o = o_of("co")
            release(tt(oa.rearrange("p q (h e) -> p (q h) e", e=64),
                       banks(o).rearrange("p q (h e) -> p (q h) e", e=64),
                       csm[:, 48:64].unsqueeze(2).broadcast_to([P, 16, 64]), ALU.mult), o)
            wait_copied(dve, o)

            attend(U_NSA, U_X)
            v.memset(stats[:, 94:95], 0.0).then_inc(mixer_rows, 1)

            dve.wait_ge(mem_landed, 16)
            moments(xa, D, 3, LN_EPS)
            for q in range(NT):
                ins = ts_(xa[:, q, :], xa[:, q, :], mean_var[:, q, 0:1], rstd[:, q:q + 1], ALU.subtract, ALU.mult)
                if q == 0:
                    own.tick(ins)
            ins.then_inc(rows_ready, 1)

            def merge(name, biased_gates):
                n0, p0, o0 = at[name]
                yv = yS.rearrange("p (a c) -> p a c", a=2)
                with dve.Fori(0, D // W) as i:
                    own.enter(i, 2)
                    for b in range(NBR):
                        og, oy = o0 + 2 * b, o0 + 2 * b + 1
                        G = gateS[:, b % 2, :].rearrange("p (a c) -> p a c", a=2)
                        if biased_gates:
                            dve.wait_ge(part_done, i * 4 + (p0 + b + 1))
                            for x in range(2):
                                bcol = cols[:, 1, bass.ds(i * 2 + (16 * b + x), 1)]
                                ins = ts_(G[:, x, :], banks(og)[:, x, 0:S], bcol, None, ALU.add)
                            release(ins, og)
                            dve.wait_ge(gate_ready, i * 4 + (b + 1))
                        else:
                            dve.wait_ge(acc_free[og % 2], i * 4 + (og // 2 + 1))
                        dve.wait_ge(tile_used, i * 4 + (n0 + b + 1))
                        mixed = mixT[:, bass.ds(i * 2, 2), :]
                        release(tt(mixed if b == 0 else yv, banks(oy)[:, :, 0:S], G, ALU.mult), oy)
                        dve.wait_ge(acc_free[oy % 2], i * 4 + (oy // 2 + 1))
                        if b:
                            ins = tt(mixed, mixed, yv, ALU.add)
                            if b < NBR - 1:
                                link(ins)
                            else:
                                ins.then_inc(gate_used, 1)
                    own.leave(D // W)

            merge("merge1", False)
            own.done()

            def square_out(name, alpha):
                n0, _, o0 = at[name]
                with dve.Fori(0, 2) as i:
                    for k in range(4):
                        dve.wait_ge(tile_used, i * 4 + (n0 + k + 1))
                        x = xa[:, :, bass.ds(i * (4 * W) + k * W, W)]
                        release(stt(x, x, alpha, banks(o0 + k)[:, :, 0:W], ALU.mult, ALU.add), o0 + k)
                wait_copied(dve, o0 + 6)
                wait_copied(dve, o0 + 7)

            def down_out(name, alpha):
                n0, _, o0 = at[name]
                with dve.Fori(0, D // W // 2) as i:
                    for c in range(2):
                        dve.wait_ge(tile_used, i * 8 + (n0 + 4 * c + 4))
                        x = xa[:, :, bass.ds(i * (2 * W) + c * W, W)]
                        release(stt(x, x, alpha, banks(o0 + c)[:, :, 0:W], ALU.mult, ALU.add), o0 + c)
                wait_copied(dve, o0 + 6)
                wait_copied(dve, o0 + 7)

            dve.wait_ge(resid_landed, 16)
            square_out("mixout1", ALPHA)
            layer_norm_rows(0, 4, 2)

            attend(U_X, U_DIFF)
            v.memset(stats[:, 88:89], 0.0).then_inc(mixer_rows, 1)
            for k in range(8):
                o = o_of("xo", k)
                if k % 4 == 3:
                    wait_tile(dve, "xo", k // 4)
                else:
                    wait_part(dve, "xo", k - k // 4)
                x = xa[:, :, k * W:(k + 1) * W]
                release(stt(x, x, ALPHA, banks(o)[:, :, 0:W], ALU.mult, ALU.add), o)
            wait_copied(dve, o_of("xo", 6))
            wait_copied(dve, o_of("xo", 7))
            layer_norm_rows(1, 5, 3)

            n0, _, o0 = at["ffin1"]
            with dve.Fori(0, PAIRS // 2) as i:
                own.enter(i, 8)
                for k in range(2):
                    og, ou = o0 + 2 * k, o0 + 2 * k + 1
                    dve.wait_ge(tile_used, i * 4 + (n0 + 2 * k + 1))
                    g = banks(og)
                    cv_ = lambda x, a: convS[:, k, x * S + a:(x + 1) * S]
                    tap = lambda st, r, x: cols[:, st, bass.ds(i * 4 + (r + 2 * k + x), 1)]
                    for x in range(2):
                        own.tick(ts_(cv_(x, 0), g[:, x, 0:S], tap(3, 0, x), tap(1, 64, x), ALU.mult, ALU.add))
                    own.done()
                    for x in range(2):
                        own.tick(stt(cv_(x, 1), g[:, x, 0:S - 1], tap(2, FC, x), cv_(x, 1), ALU.mult, ALU.add))
                    own.done()
                    for x in range(2):
                        ins = stt(cv_(x, 2), g[:, x, 0:S - 2], tap(2, 0, x), cv_(x, 2), ALU.mult, ALU.add)
                    release(ins, og)
                    dve.wait_ge(silu_ready, i * 2 + (k + 1))
                    dve.wait_ge(tile_used, i * 4 + (n0 + 2 * k + 2))
                    release(tt(hT[:, bass.ds(i * 4 + 2 * k, 2), :], banks(ou)[:, :, 0:S],
                               siluS[:, k, :].rearrange("p (a c) -> p a c", a=2), ALU.mult), ou)
                own.leave(PAIRS // 2)
            down_out("ffout1", ALPHA)
            layer_norm_rows(2, 6, 0)

            rms_rows(rowsx, 7, 4)
            scaled_out("xT2", "norm_mix_2")
            link(v.memset(bx[:, :, 0:4], 0.0))
            lam_ = col("lru_lambda_2", 0, 4)
            link(ts_(lbv[:, 24:28], lam_, -1.0, None, ALU.mult))
            tt(lbv[:, 16:20], lbv[:, 24:28], lam_, ALU.min).then_inc(sp_abs, 1)
            wait_copied(dve, o_of("in2", 6))
            wait_copied(dve, o_of("in2", 7))
            for c in range(4):
                own.tick(ts_(xc[:, c, :], bx[:, c, 4:], col("lru_conv_w_2", 12 + c), col("lru_conv_b_2", c),
                             ALU.mult, ALU.add))
            own.done()
            for tap_ in (2, 1, 0):
                for c in range(4):
                    ins = stt(xc[:, c, :], bx[:, c, tap_ + 1:tap_ + 1 + S], col("lru_conv_w_2", 4 * tap_ + c),
                              xc[:, c, :], ALU.mult, ALU.add)
                    if tap_ or c < 3:
                        own.tick(ins)
                if tap_:
                    own.done()
            ins.then_inc(lru_conv, 1)
            dve.wait_ge(lru_conv, 1)
            dve.wait_ge(sp_exp, 1)
            log1p(lbv[:, 20:24], lbv[:, 40:44], lbv[:, 44:48], lbv[:, 48:52])
            link(stt(lbv[:, 24:28], lbv[:, 24:28], 0.0, lbv[:, 48:52], ALU.max, ALU.add))
            link(ts_(lbv[:, 24:28], lbv[:, 24:28], -8.0, None, ALU.mult))
            wait_copied(dve, o_of("lru", 0))
            wait_copied(dve, o_of("lru", 1))
            for c in range(4):
                ins = ts_(lr[:, c, :], lr[:, c, :], lbv[:, 24 + c:25 + c], None, ALU.mult)
            ins.then_inc(lru_arg, 1)
            link(tt(li, li, xc, ALU.mult))
            dve.wait_ge(lru_exp, 1)
            link(ts_(bfree, lt, 1.0, None, ALU.add))
            link(v.reciprocal(bfree, bfree))
            tt(lt, lt, bfree, ALU.mult).then_inc(lru_sq, 1)
            dve.wait_ge(lru_sqrt, 1)
            link(tt(li, li, lt, ALU.mult))
            for c in range(4):
                own.tick(v.tensor_tensor_scan(xc[:, c, :], la[:, c, :], li[:, c, :], 0.0, ALU.mult, ALU.add))
            own.done()
            wait_copied(dve, o_of("in2", 9))
            link(tt(brT[:, 4:8, :], xc, bg, ALU.mult))

            dve.wait_ge(mixer2_landed, 16 * MIXER2_LOADS)
            wait_copied(dve, o_of("in2", 16))
            z4 = cf[0:4, :]
            na, ez, t1, t2, t3 = (li[0:4, k, :] for k in (0, 1, 2, 3, 0))
            link(ts_(z4, z4, bf[0:4, :], None, ALU.add))
            link(ts_(na, z4, -1.0, None, ALU.mult))
            tt(na, na, z4, ALU.min).then_inc(sp_abs, 1)
            dve.wait_ge(sp_exp, 2)
            log1p(ez, t1, t2, t3)
            link(stt(t1, z4, 0.0, t3, ALU.min, ALU.subtract))
            link(v.tensor_tensor_scan(cum[0:4, :], heads[0:4, 4, :], t1, 0.0, ALU.mult, ALU.add))
            link(ts_(ncum[0:4, :], cum[0:4, :], -1.0, None, ALU.mult))
            for k in range(2):
                own.tick(tt(lrow[:, 128 * k:128 * k + 64], lrow[:, 128 * k:128 * k + 64],
                            lrow[:, 128 * k + 64:128 * k + 128], ALU.mult))
            own.done()
            for k in range(2):
                ins = v.tensor_reduce(lbv[:, 32 + k:33 + k], lrow[:, 128 * k:128 * k + 64], AX, ALU.add)
            ins.then_inc(lam_sum, 1)
            dve.wait_ge(lam_exp, 1)
            link(tt(lbv[:, 36:37], lbv[:, 35:36], lbv[:, 34:35], ALU.subtract))
            link(ts_(lbv[:, 36:37], lbv[:, 36:37], LAM_INIT, None, ALU.subtract))
            link(ts_(vecs[:, 40:48], sinks, -1.0, None, ALU.mult))
            wait_copied(dve, o_of("in2", 18))
            wait_copied(dve, o_of("in2", 19))
            v.memset(stats[:, 89:90], 0.0).then_inc(mixer_rows, 1)
            attend(U_DIFF, U_END)
            dve.wait_ge(probs_turned, U_END)
            yaf = ya.rearrange("p q (h e) -> p (q h) e", h=4)
            sqf = ysq.rearrange("p q (h e) -> p (q h) e", h=4)
            link(tt(sqf, yaf, yaf, ALU.mult))
            link(v.tensor_reduce(stats[:, 56:64], sqf, AX, ALU.add))
            ts_(stats[:, 64:72], stats[:, 56:64], 1.0 / P, RMS_EPS, ALU.mult, ALU.add).then_inc(var_ready, 1)
            root(8, 8)
            link(tt(yaf, yaf, rstd.unsqueeze(2).broadcast_to([P, 8, P]), ALU.mult))
            link(tt(yaf, yaf, subln.unsqueeze(1).broadcast_to([P, 8, P]), ALU.mult))
            ts_(ya, ya, 1.0 - LAM_INIT, None, ALU.mult).then_inc(mixer_rows, 1)
            merge("merge2", True)
            own.done()
            square_out("mixout2", 1.0)
            rms_rows(rowsx, 9, 5)
            scaled_out("x3T", "norm_ffn_2")
            n0, _, o0 = at["ffin2"]
            with dve.Fori(0, PAIRS // 2) as i:
                for k in range(2):
                    og, ou = o0 + 2 * k, o0 + 2 * k + 1
                    dve.wait_ge(acc_free[og % 2], i * 2 + (og // 2 + 1))
                    dve.wait_ge(tile_used, i * 4 + (n0 + 2 * k + 2))
                    release(tt(hT[:, bass.ds(i * 4 + 2 * k, 2), :], banks(ou)[:, :, 0:S],
                               siluS[:, k, :].rearrange("p (a c) -> p a c", a=2), ALU.mult), ou)
            down_out("ffout2", 1.0)
            moments(xa, D, 10, RMS_EPS, rms=True)
            for q in range(NT):
                own.tick(ts_(xa[:, q, :], xa[:, q, :], rstd[:, q:q + 1], None, ALU.mult))
            own.done()
            dve.wait_ge(norm_rows_landed, 32 * 4)
            tt(xa[:, :, :], xa[:, :, :], lng.unsqueeze(1).broadcast_to([P, NT, D]), ALU.mult).then_inc(rows_ready, 1)


def laid_out(x):
    r = lambda name, *shape: x[name].reshape(*shape)
    stacked = {name: r(name, -1, P) for st in STACKS for name, _ in st if not name.startswith("conv_w")}
    taps = r("ffn_conv_w", 3 * FC, P)
    stacked["conv_w_01"], stacked["conv_w_2"] = taps[:2 * FC], taps[2 * FC:]
    return stacked | {
        "x": r("x", S, D), "mem": r("mem", S, D), "w_in": r("w_in", D, -1), "w_in_2": r("w_in_2", D, -1),
        "nsa_cmp_pos": r("nsa_cmp_pos", 64, 64), "nsa_cmp_w": r("nsa_cmp_w", 2, 32, 64, 64),
        "hgrn_norm_g": r("hgrn_norm_g", -1), "pool_w": r("pool_w", 4, P, P),
        "sg_ln_g": r("sg_ln_g", -1), "sg_ln_b": r("sg_ln_b", -1), "sg_w": r("sg_w", 4, P, P),
        "w_branch": r("w_branch", D, D), "w_branch_2": r("w_branch_2", D, D),
        "w_mix_out": r("w_mix_out", D, D), "w_out_2": r("w_out_2", D, D),
        "ln_mix_g": r("ln_mix_g", -1), "ln_mix_b": r("ln_mix_b", -1), "ln_x_g": r("ln_x_g", -1),
        "ln_x_b": r("ln_x_b", -1), "ln_ffn_g": r("ln_ffn_g", -1), "ln_ffn_b": r("ln_ffn_b", -1),
        "xattn_q": r("xattn_q", D, -1), "xattn_k": r("xattn_k", D, -1), "xattn_v": r("xattn_v", D, -1),
        "xattn_o": r("xattn_o", -1, D), "ffn_in": r("ffn_in", D, -1), "ffn_out": r("ffn_out", -1, D),
        "diff_lq1_2": r("diff_lq1_2", -1), "diff_lk1_2": r("diff_lk1_2", -1),
        "diff_lq2_2": r("diff_lq2_2", -1), "diff_lk2_2": r("diff_lk2_2", -1),
        "diff_subln_2": r("diff_subln_2", -1), "lru_wa_2": r("lru_wa_2", 8, 64, 64),
        "lru_wx_2": r("lru_wx_2", 8, 64, 64), "fox_b_f_2": r("fox_b_f_2", -1),
        "swa_sinks_2": r("swa_sinks_2", -1), "w_ffn_gate_2": r("w_ffn_gate_2", D, -1),
        "w_ffn_up_2": r("w_ffn_up_2", D, -1), "w_ffn_down_2": r("w_ffn_down_2", -1, D),
        "norm_final_2": r("norm_final_2", -1),
    }


def kernel(**inputs):
    import concourse.bacc as _bacc
    from concourse.bass_utils import run_bass_kernel_spmd as _run

    nc = _bacc.Bacc("TRN2", target_bir_lowering=False, num_devices=1)
    arrays = {k: np.ascontiguousarray(a) for k, a in laid_out({k: np.asarray(a) for k, a in inputs.items()}).items()}
    arrays.update(shape_tables())
    arrays = {f"in_{k}": a for k, a in arrays.items()}
    t = {k[3:]: nc.dram_tensor(k, a.shape, F32, kind="ExternalInput").ap() for k, a in arrays.items()}
    out = nc.dram_tensor("out", (S, D), F32, kind="ExternalOutput").ap()
    two_layer_block_kernel(nc, t, out)
    r = _run(nc, [arrays], core_ids=[0])
    return r.results[0]["out"].reshape(1, S, D)
```

```python
from collections import namedtuple
from contextlib import ExitStack
import math

import numpy as np
import concourse.bass as bass
from concourse import mybir

P = 128
S = 256
NT = S // P
D = 2048
KC = D // P
MIX = 512
NBR = 4
FF = 5632
FC = FF // P
W = 256
SLOTS = 2
LANDED = 64
U = 4 * W
PIECES = 4
GROUPS = FC // 4
NORM_ROOT = 11
LAG = 2
NH = 8
NJ = NH // 2
NC = (S - 32) // 16 + 1
NEG = -1e30
MIXER1_LOADS = 11
MIXER2_LOADS = 8
ALPHA = 2.0 ** 0.25
LN_EPS = 1e-5
RMS_EPS = 1e-6
HL = 7
LAM_INIT = 0.8 - 0.6 * math.exp(0.0)

A_Q, A_KV, A_G, B_IN, C_IN, D_IN, MERGE = 0, 512, 1280, 1304, 3352, 3864, 4888
AQ2, AK2, AV2, BX2, BG2, CQ2, CK2, CV2, CF2, DQ2, DKV2, GZ2 = (
    0, 512, 1024, 1536, 2048, 2560, 3072, 3584, 4096, 4100, 4612, 4868)

ALU = mybir.AluOpType
ACT = mybir.ActivationFunctionType
F32 = mybir.dt.float32
F32R = mybir.dt.float32r
AX = mybir.AxisListType.X

STACKS = (
    (("mem_ln_g", 16), ("mem_ln_b", 16), ("norm_mix_2", 16), ("norm_ffn_2", 16), ("pool_scale", 4),
     ("hgrn_lb_logits", 4), ("lru_conv_w_2", 16), ("lru_conv_b_2", 4), ("lru_ba_2", 4), ("lru_bx_2", 4),
     ("lru_lambda_2", 4), ("sg_b", 4)),
    (("b_gate_2", 64), ("ffn_conv_b", FC)),
    (("conv_w_01", 2 * FC),),
    (("conv_w_2", FC),),
)

BIAS_NSA, BIAS_SWA, BIAS_DIFF, BIAS_FOX = 0, 8, 16, 24
T_LEVEL, T_TRI, T_COUNT, T_CBIAS, T_CMASK, T_HEAD, T_ONES = 0, 1024, 1152, 2176, 2416, 2656, 3680
T_END = 3936


def shape_tables():
    t = np.arange(S)[:, None]
    k = np.arange(S)[None, :]
    dist = (t - k).astype(np.float32)
    causal = dist >= 0
    window = causal & (dist < P)

    def table(slopes, mask):
        maps = [np.where(mask, -np.float32(s) * dist, np.float32(NEG)) for s in slopes]
        both = np.concatenate(maps, axis=1)
        return [both[q * P:(q + 1) * P] for q in range(NT)]

    bias = []
    for mask in (causal, window):
        for j in range(NJ):
            bias += table((2.0 ** -(j + 1), 2.0 ** -(j + 5)), mask)
    for h in range(4):
        bias += table((2.0 ** -(2 * (h + 1)),) * 2, causal)
    bias += table((0.0, 0.0), causal)

    small = np.zeros((P, T_END), np.float32)
    s_, t_ = np.arange(P)[:, None], np.arange(P)[None, :]
    small[:, T_LEVEL:T_LEVEL + P] = s_ == t_
    for lv in range(HL):
        h = 1 << lv
        same = s_ // (2 * h) == t_ // (2 * h)
        small[:, T_LEVEL + (lv + 1) * P:T_LEVEL + (lv + 2) * P] = same & (s_ // h % 2 == 0) & (t_ // h % 2 == 1)
    small[:, T_TRI:T_TRI + P] = s_ <= t_
    for g, win in enumerate((2, 4, 8, 16)):
        small[:, T_COUNT + g * S:T_COUNT + (g + 1) * S] = 1.0 / np.minimum(np.arange(S) + 1, win)
    end = np.arange(NC) * 16 + 31
    for q in range(NT):
        d = ((np.arange(P) + q * P)[:, None] - end[None, :]).astype(np.float32)
        for h in range(NH):
            at = (q * NH + h) * NC
            small[:, T_CBIAS + at:T_CBIAS + at + NC] = np.where(d >= 0, -np.float32(2.0 ** -(h + 1)) * d, NEG)
            small[:, T_CMASK + at:T_CMASK + at + NC] = d >= 0
    for h in range(4):
        small[h, T_HEAD + h * S:T_HEAD + (h + 1) * S] = 1.0
    small[:, T_ONES:T_ONES + S] = 1.0
    return {"t_ident": np.eye(P, dtype=np.float32), "t_bias": np.stack(bias).astype(np.float32), "t_small": small}


Piece = namedtuple("Piece", "tile k wide split piece out ends b x c hid per_tile per_piece per_out",
                   defaults=(None, 0, 0, 0, None, 0, 0, 0))


class Plan:

    def __init__(self):
        self.tile, self.part, self.out, self.split, self.piece = 0, 0, 0, 0, 0
        self.at, self.freed = {}, []

    def add(self, name, tiles=0, parts=0, outs=0, splits=0):
        self.at[name] = (self.tile, self.part, self.out, self.split, self.piece)
        self.freed += [("products", self.tile + i + 1) for i in range(tiles)]
        self.tile += tiles
        self.part += parts
        self.out += outs
        self.split += splits

    def add_split(self, name, tiles, outs, times=1):
        self.at[name] = (self.tile, self.part, self.out, self.split, self.piece)
        for n in tiles * times:
            self.tile += 1
            self.split += n
            self.piece += n
            self.freed.append(("split", self.split))
        self.out += outs * times


class Count:

    def __init__(self, eng, sem):
        self.eng, self.sem, self.n, self.i, self.per = eng, sem, 0, None, 0

    def tick(self, ins):
        ins.then_inc(self.sem, 1)
        self.n += 1
        return ins

    def value(self):
        return self.n if self.i is None else self.i * self.per + self.n

    def done(self):
        self.eng.wait_ge(self.sem, self.value())

    def link(self, ins):
        self.tick(ins)
        self.done()

    def enter(self, i, per, start=0):
        self.n -= start * per
        self.i, self.per, self.n0 = i, per, self.n

    def leave(self, times):
        assert self.n - self.n0 == self.per, (self.n, self.n0, self.per)
        self.n = self.n0 + self.per * times
        self.i = None


def two_layer_block_kernel(nc, t, out):
    pl = Plan()
    add = pl.add
    add("cols", parts=1, outs=1)
    add("xT1", parts=4, outs=4)
    for n in range(6):
        add(f"b{n}", tiles=1, outs=1)
    add("hin", tiles=8, outs=8)
    add("b6", tiles=1, outs=1)
    B_AFTER = (1, 1, 1, 1, 1, 0, 0, 0, 0)
    n = 7
    for lv, k in enumerate(B_AFTER):
        add(f"lvl{lv}", parts=1, outs=1)
        for _ in range(k):
            add(f"b{n}", tiles=1, outs=1)
            n += 1
    add("ho", parts=1, outs=1)
    add("hT", parts=1, outs=1)
    add("sgw", parts=1, outs=1)
    add("pool", parts=1, outs=1)
    add("sgo", parts=1, outs=1)
    add("sgT", parts=1, outs=1)
    add("pos", parts=1, outs=1)
    add("ckv", parts=1, outs=1)
    add("cs", parts=1, outs=1)
    add("cT", parts=2, outs=2)
    add("co", parts=1, outs=1)
    add("nT", parts=1, outs=1)
    add("act1", splits=4)
    add("br1", splits=4)
    pl.add_split("merge1", [5] * 4, 8, D // W)
    add("memT", parts=4, outs=4, splits=4)
    pl.add_split("xk", [4] * 2, 2)
    pl.add_split("xv", [4] * 2, 2)
    pl.add_split("mixout1", [4] * 8, 8)
    add("x1T", parts=4, outs=4, splits=4)
    pl.add_split("xq", [4] * 2, 2)
    add("xoT", parts=1, outs=1, splits=1)
    pl.add_split("xo", [4] * 2, 8)
    add("x2T", parts=4, outs=4, splits=4)
    pl.add_split("ff1", [4] * 4, 4)
    pl.add_split("ff1loop", [4] * 12, 24, (GROUPS - 1) // 2)
    pl.add_split("ff1end", [4] * 2, 8)
    add("xT2", parts=4, outs=4)
    add("in2", tiles=7, outs=7)
    add("lru", parts=2, outs=2)
    add("in2b", tiles=13, outs=13)
    add("y0T", parts=1, outs=1)
    add("y2T", parts=1, outs=1)
    add("y3T", parts=1, outs=1)
    add("act2", splits=4)
    add("br2", splits=4)
    pl.add_split("merge2", [5] * 4, 8, D // W)
    pl.add_split("mixout2", [4] * 8, 8)
    add("x3T", parts=4, outs=4, splits=4)
    pl.add_split("ff2", [4] * 4, 4)
    pl.add_split("ff2loop", [4] * 12, 24, (GROUPS - 1) // 2)
    pl.add_split("ff2end", [4] * 2, 8)
    at = pl.at

    U_NSA, U_X, U_SWA, U_DIFF, U_FOX, U_END = 0, 16, 20, 28, 36, 40

    def kind(u):
        return ("nsa", "x", "swa", "diff", "fox")[sum(u >= a for a in (U_X, U_SWA, U_DIFF, U_FOX))]

    def bias_of(u):
        if kind(u) == "nsa":
            return BIAS_NSA + (u // 2) % 4 * 2 + u % 2
        return {"x": None, "swa": BIAS_SWA + u - U_SWA, "diff": BIAS_DIFF + u - U_DIFF, "fox": BIAS_FOX + u % 2}[kind(u)]

    BEHIND_HALVES = {"hin": [(U_NSA, U_X, 0)], "in2": [(U_SWA, U_DIFF, 9), (U_DIFF, U_FOX, 14)]}

    def groups_at(name, k):
        return [(a, b) for a, b, first in BEHIND_HALVES[name] if first == k]

    def unit_behind(name, k, half):
        for a, b, first in BEHIND_HALVES[name]:
            u = a + 2 * (k - first) + half
            if a <= u < b:
                return [(u, a, b)]
        return []

    def biased_before(u):
        return len([v for v in range(u % 2, u + 1, 2) if bias_of(v) is not None])

    with ExitStack() as ctx:
        def sb(name, shape):
            return ctx.enter_context(nc.sbuf_tensor(name, shape, F32))

        def sem(name):
            return ctx.enter_context(nc.semaphore(name))

        ring = sb("ring", [P, SLOTS, 20 * W])
        whi = ctx.enter_context(nc.sbuf_tensor("whi", [P, PIECES, U], F32R))
        wlo = ctx.enter_context(nc.sbuf_tensor("wlo", [P, PIECES, U], F32R))
        xa = sb("xa", [P, NT, D])
        shared = ExitStack()
        arena = shared.enter_context(nc.sbuf_tensor("arena", [P, 3 * 2 * KC * S], F32))
        shared.close()
        brR, actR, mixR = (ctx.enter_context(nc.sbuf_tensor(n, [P, 2, KC, S], F32R)) for n in ("brR", "actR", "mixR"))
        ident = sb("ident", [P, P])
        bias = sb("bias", [P, 2, 512])
        score = sb("score", [P, 2, 512])
        probT = sb("probT", [P, 2, 512])
        cols = sb("cols", [P, 4, P])
        stats = sb("stats", [P, 100])
        vecs = sb("vecs", [P, 96])
        lbv = sb("lbv", [P, 64])
        acc = ctx.enter_context(nc.psum_tensor("acc", [P, 4, 512], F32))
        sc = ctx.enter_context(nc.psum_tensor("sc", [P, 2, 512], F32))
        pt = ctx.enter_context(nc.psum_tensor("pt", [P, 512], F32))
        pv = ctx.enter_context(nc.psum_tensor("pv", [P, 512], F32))

        def place(off):
            return off - 4096 if off >= 4096 else 16384 + off

        def piece(off, n):
            return arena[:, place(off):place(off) + n]

        def cut(off, a, b):
            return piece(off, a * b).rearrange("p (a b) -> p a b", a=a)

        xaf = xa[:, :, :].rearrange("p a b -> p (a b)")
        brT, actT = cut(0, KC, S), cut(20480 + 4096, KC, S)
        rowsx = cut(15360, NT, D)
        hq, hp, hk, hr, hqd, hkd = (cut(4096 + i * 1024, 4, S) for i in range(6))
        hi, hg = cut(10240, NT, 512), cut(11264, NT, 512)
        ATd, ATx = piece(12288, 1024), cut(13312, 4, P)
        lmask = cut(13824, 8, P)
        hgrow = piece(14848, 512)
        ho, htmp = cut(15360, NT, 512), piece(16384, 1024)
        xapart = lambda off, a, b: xaf[:, off:off + a * b].rearrange("p (a b) -> p a b", a=a)
        qn = xapart(0, NJ, S)
        kvc, kvs, kvw = (xapart(1024 + i * 512, 2, S) for i in range(3))
        ag = xapart(2560, NT, 24)
        cpad = xapart(2624, 4, 16 + S)
        su, sv = cut(17408, NT, 512), cut(18432, NT, 512)
        cw = piece(4096, 4096).rearrange("p (i l e) -> p i l e", i=2, l=32)
        posT = cut(8192, 2, 32)
        win = piece(8256, 960).rearrange("p (i l c) -> p i l c", i=2, l=32)
        kcmp, vcmp = piece(9216, NC), piece(9232, P)
        oa = cut(0, NT, 512)
        co_rows = cut(4096, NT, 512)
        ctab = piece(10400, 480)
        cS = piece(10880, 240)
        csm = piece(11120, 160)
        ping, pong = cut(11280, 4, 16 + S), cut(12368, 4, 16 + S)
        cPT = cut(11280, NT * NH, P)
        invc = cut(13456, 4, S)
        poolw = cut(14480, 4, P)
        sgrow, wmT = cut(14992, 4, P), cut(15504, 4, P)
        slg, slb = piece(16016, 512), piece(16528, 512)
        posrow = piece(17040, P)
        tri = piece(17168, P)
        def at_(off, a, b):
            return arena[:, off:off + a * b].rearrange("p (a b) -> p a b", a=a)

        kx, vx = at_(8192, 4, S), at_(9216, NT, 512)
        norm_at = (10240, 10240, 16384, 8192)
        lng = [arena[:, o:o + D] for o in norm_at]
        lnb = [arena[:, o + D:o + 2 * D] for o in norm_at]
        qx, ox = at_(14336, 4, S), at_(15360, NT, 512)
        mem_tmp = [arena[:, 12288 + i * U:12288 + (i + 1) * U] for i in range(2)]
        hidR = lambda par, part: brR[:, part, 4 * par:4 * par + 4, :]
        convS, siluS = at_(2048, 2, 512), at_(3072, 2, 512)
        aq, ak, cq, ck = cut(4096, 4, S), cut(5120, 4, S), cut(7168, 4, S), cut(8192, 4, S)
        av, cv = cut(6144, NT, 512), cut(9216, NT, 512)
        dq, dkv = cut(10240, NJ, S), cut(11264, 2, S)
        cf, cum, ncum = piece(11776, S), piece(12032, S), piece(12288, S)
        bg = cut(12544, 4, S)
        bx = cut(13568, 4, 4 + S)
        bfree = cut(13568, 4, S)
        ftmp = bfree
        xc, lr, li = (cut(14608 + i * 1024, 4, S) for i in range(3))
        lt = score[:, :, :].rearrange("p a (b c) -> p (a b) c", b=2)
        la = probT[:, :, :].rearrange("p a (b c) -> p (a b) c", b=2)
        wl = score[:, :, :].rearrange("p i (c d) -> p i c d", c=4)
        ya, yc, yd = (cut(14608 + i * 1024, NT, 512) for i in range(3))
        lrow = piece(17680, 256)
        sinks = piece(17936, NH)
        subln = piece(17952, P)
        heads = piece(18080, 1280).rearrange("p (h c) -> p h c", h=5)
        bf = piece(19368, 1)
        ysq = score[:, :, :]
        gateS, yS, mixS = score[:, :, :], probT[:, 0, :], probT[:, 1, :]
        turn_tmp = [score[:, :, :].rearrange("p a b -> p (a b)"), probT[:, :, :].rearrange("p a b -> p (a b)")]

        def stack_rows(i):
            return piece(i * P, P)

        def col(name, k=0, n=1):
            for i, st in enumerate(STACKS):
                r = 0
                for nm, rows in st:
                    if nm == name:
                        return cols[:, i, r + k:r + k + n]
                    r += rows
            raise KeyError(name)

        w_landed = [sem(f"w_landed{i}") for i in range(SLOTS)]
        tile_used = sem("tile_used")
        piece_used = sem("piece_used")
        hi_ready = sem("hi_ready")
        lo_ready = sem("lo_ready")
        hid_hi = sem("hid_hi")
        hid_lo = sem("hid_lo")
        part_done = sem("part_done")
        acc_free = [sem("acc_free0"), sem("acc_free1")]
        ident_landed = sem("ident_landed")
        stack_landed = sem("stack_landed")
        x_landed = sem("x_landed")
        level_tab_landed = sem("level_tab_landed")
        mixer1_landed = sem("mixer1_landed")
        mixer2_landed = sem("mixer2_landed")
        lru_zeroed = sem("lru_zeroed")
        lru_landed = sem("lru_landed")
        mem_landed = sem("mem_landed")
        resid_landed = sem("resid_landed")
        norm_rows_landed = sem("norm_rows_landed")
        bias_landed = [sem("bias_landed0"), sem("bias_landed1")]
        out_landed = sem("out_landed")
        pe_rows = sem("pe_rows")
        v_link = sem("vector_link")
        s_link = sem("scalar_link")
        rows_ready = sem("rows_ready")
        norm_done = sem("norm_done")
        var_ready = sem("var_ready")
        std_ready = sem("std_ready")
        lb_max = sem("lb_max")
        lb_exp = sem("lb_exp")
        level_ready = sem("level_ready")
        decay_ready = sem("decay_ready")
        ho_copied = sem("ho_copied")
        mixer_rows = sem("mixer_rows")
        cmp_ready = sem("cmp_ready")
        cmp_exp = sem("cmp_exp")
        gate_ready = sem("gate_ready")
        gate_used = sem("gate_used")
        silu_ready = sem("silu_ready")
        scores_done = sem("scores_done")
        biased = sem("biased")
        max_ready = sem("max_ready")
        probs_ready = sem("probs_ready")
        probs_turned = sem("probs_turned")
        probT_ready = sem("probT_ready")
        pv_done = sem("pv_done")
        pv_used = sem("pv_used")
        lru_conv = sem("lru_conv")
        lru_sig = sem("lru_sig")
        lru_arg = sem("lru_arg")
        lru_exp = sem("lru_exp")
        lru_sq = sem("lru_sq")
        lru_sqrt = sem("lru_sqrt")
        gelu_ready = sem("gelu_ready")
        sp_abs = sem("softplus_abs")
        sp_exp = sem("softplus_exp")
        lam_sum = sem("lam_sum")
        lam_exp = sem("lam_exp")
        sub_sq = sem("sub_sq")

        def tile_count(name, k=0):
            return len([1 for kind, _ in pl.freed[:at[name][0] + k + 1] if kind == "products"])

        def wait_tile(eng, name, k=0):
            eng.wait_ge(tile_used, tile_count(name, k))

        def wait_part(eng, name, k=0):
            eng.wait_ge(part_done, at[name][1] + k + 1)

        def reach(eng, semaphore, n, i=None, per=0):
            eng.wait_ge(semaphore, n if i is None else i * per + n)

        def o_of(name, k=0):
            return at[name][2] + k + (2 if name == "in2" and k >= 7 else 0)

        def banks(o):
            return acc[:, 2 * (o % 2):2 * (o % 2) + 2, :]

        def wait_bank(o, i=None, per=0):
            if o >= 2:
                nc.tensor.wait_ge(acc_free[o % 2], o // 2 if i is None else i * (per // 2) + o // 2)

        def wait_copied(eng, o):
            eng.wait_ge(acc_free[o % 2], o // 2 + 1)

        def release(ins, o):
            ins.then_inc(acc_free[o % 2], 1)

        hid0 = {"ff1": 0, "ff2": GROUPS}

        def copied(eng, o, i, per):
            reach(eng, acc_free[o % 2], o // 2 + 1, i, per // 2)

        def product(eng, d, i):
            reach(eng, piece_used, d.piece + 1, i, d.per_piece)

        def raw(d):
            if d.wide:
                return ring[:, d.tile % SLOTS, 0:16 * W].rearrange("p (k c) -> p k c", k=4)[:, :, d.k * W:(d.k + 1) * W]
            return ring[:, d.tile % SLOTS, d.k * U:(d.k + 1) * U].rearrange("p (k c) -> p k c", k=4)

        def part_of_piece(w, d):
            return w[:, d.piece % PIECES, :].rearrange("p (k c) -> p k c", k=4)

        def tile_pieces(name, tiles, turns=1):
            n, _, o, s_, p_ = at[name]
            m = tiles // turns
            return [Piece(n + c, k, False, s_ + 4 * c + k, p_ + 4 * c + k, o + c, "rows" if k == 3 else None,
                          c=c, per_tile=m, per_piece=4 * m, per_out=m) for c in range(m) for k in range(4)]

        def wide_pieces(name, x0=0):
            n, _, o, s_, p_ = at[name]
            return [Piece(n + x, k, True, s_ + 4 * x + k, p_ + 4 * x + k, o + 4 * x + k, "rows", c=4 * x + k)
                    for x in range(2) for k in range(4)]

        def merge_pieces(name):
            n, _, o, s_, p_ = at[name]
            ends = (None, None, None, "gate", "y")
            return [Piece(n + b, k, False, s_ + 5 * b + k, p_ + 5 * b + k, o + 2 * b + (k == 4), ends[k], b=b,
                          per_tile=4, per_piece=20, per_out=8) for b in range(NBR) for k in range(5)]

        def hidden(name, g, x, o, loop):
            per = (4, 8, 24) if loop else (0, 0, 0)
            return dict(h=2 * (hid0[name] + g) + x, x=x, par=g % 2, og=o, ou=o + 1, chunk=4 * g + 2 * x,
                        per_h=per[0], per_chunk=per[1], per_out=per[2])

        def ff_pieces(name):
            def gate_up(n, s_, p_, o, hd, steps, **kw):
                both = []
                for k in range(8):
                    hid = {3: ("gate", hd), 4: ("silu", hd), 7: ("up", hd)}.get(k, steps.get(k))
                    both.append(Piece(n + k // 4, k % 4, False, s_ + k, p_ + k, o + k // 4, None, hid=hid, **kw))
                return both

            n, _, o, s_, p_ = at[name]
            first = [hidden(name, 0, x, o + 2 * x, False) for x in range(2)]
            before = gate_up(n, s_, p_, o, first[0], {})
            before += gate_up(n + 2, s_ + 8, p_ + 8, o + 2, first[1], {0: ("hi", first[0]), 1: ("lo", first[0])})
            n, _, o, s_, p_ = at[name + "loop"]
            kw = dict(per_tile=12, per_piece=48, per_out=24)
            turn_ = []
            for z in range(2):
                for x in range(2):
                    a, d, e = 6 * z + 3 * x, 24 * z + 12 * x, 12 * z + 6 * x
                    hd = hidden(name, z + 1, x, o + e, True)
                    turn_ += gate_up(n + a, s_ + d, p_ + d, o + e, hd, {}, **kw)
                    turn_ += [Piece(n + a + 2, k, True, s_ + d + 8 + k, p_ + d + 8 + k, o + e + 2 + k, "rows",
                                    c=4 * x + k, hid={0: ("hi", hd), 1: ("lo", hd)}.get(k), **kw) for k in range(4)]
            return first, before, turn_, wide_pieces(name + "end")

        def step_through(pieces, split, finish, earlier=()):
            for q, (d, i) in enumerate(pieces):
                split(d, i)
                if q >= LAG:
                    finish(*pieces[q - LAG])
                elif earlier:
                    finish(*earlier[q - LAG])

        def straight(pieces, split, finish):
            pieces = [(d, 0) for d in pieces]
            step_through(pieces, split, finish)
            for d in pieces[-LAG:]:
                finish(*d)

        def in_turns(eng, times, turn_, split, finish, behind=(), own=None, per=0):
            step_through([(d, 0) for d in turn_], split, finish)
            with eng.Fori(1, times) as i:
                if own:
                    own.enter(i, per, 1)
                step_through([(d, i) for d in turn_], split, finish, [(d, i - 1) for d in turn_[-LAG:]])
                if own:
                    own.leave(times)
            rest = [(d, times - 1) for d in turn_[-LAG:]]
            if behind:
                step_through([(d, 0) for d in behind], split, finish, rest)
                rest = [(d, 0) for d in behind[-LAG:]]
            for d in rest:
                finish(*d)

        def unit(u):
            q_ = u % 2
            qs = slice(q_ * P, (q_ + 1) * P)
            if kind(u) in ("nsa", "swa"):
                j = (u - U_SWA) // 2 if kind(u) == "swa" else (u // 2) % 4
                kv_, qq = (dkv, dq) if kind(u) == "swa" else ((kvs, kvw)[u // 8], qn)
                half = lambda m: slice(64 * m, 64 * m + 64)
                return (lambda m: qq[half(m), j, qs], lambda m: kv_[half(m), 0, :], lambda m: [],
                        lambda m, kt: kv_[:, 1, kt * P + 64 * m:kt * P + 64 * m + 64], 64)
            if kind(u) == "x":
                p_ = (u - U_X) // 2
                return (lambda m: qx[:, 2 * p_ + m, qs], lambda m: kx[:, 2 * p_ + m, :], lambda m: [],
                        lambda m, kt: vx[:, kt, (2 * p_ + m) * P:(2 * p_ + m + 1) * P], P)
            if kind(u) == "diff":
                h = (u - U_DIFF) // 2
                half = lambda m: slice(64 * m, 64 * m + 64)
                return (lambda m: aq[half(m), h, qs], lambda m: ak[half(m), h, :], lambda m: [],
                        lambda m, kt: av[:, kt, h * P:(h + 1) * P], P)
            p_ = (u - U_FOX) // 2
            return (lambda m: cq[:, 2 * p_ + m, qs], lambda m: ck[:, 2 * p_ + m, :],
                    lambda m: [(cum[0:4, qs], heads[0:4, 2 * p_ + m, :]),
                               (heads[0:4, 2 * p_ + m, 0:P], ncum[0:4, :])],
                    lambda m, kt: cv[:, kt, (2 * p_ + m) * P:(2 * p_ + m + 1) * P], P)

        def scale_of(u):
            return {"fox": 1.0, "x": 128 ** -0.5}.get(kind(u), 64 ** -0.5)

        block = ctx.enter_context(nc.Block())

        @block.sync
        def _(sp):
            kp = lambda ap: ap.rearrange("(k p) c -> p k c", p=P)
            w_in, w_in2 = kp(t["w_in"]), kp(t["w_in_2"])

            def slot(n, k, w, off=0):
                return ring[:, n % SLOTS, off:off + k * w].rearrange("p (k c) -> p k c", k=k)

            def load(n, pieces, i=None, per=0, splits=0):
                if n >= SLOTS:
                    kind, v = pl.freed[n - SLOTS + (per if i is not None else 0)]
                    if kind == "products":
                        sp.wait_ge(tile_used, len([1 for k, _ in pl.freed[:n - SLOTS + 1] if k == kind]))
                    else:
                        reach(sp, lo_ready, v - splits if i is not None else v, i, splits)
                for dst, src in pieces:
                    sp.dma_start(dst, src).then_inc(w_landed[n % SLOTS], LANDED // len(pieces))

            def turns(times, turn):
                turn(0, None)
                with sp.Fori(1, times) as i:
                    turn(i, i)

            def plain(n, w, c, **kw):
                load(n, [(slot(n, KC, W), w[:, :, bass.ds(c, W)])], **kw)

            def paired(n, w, c):
                s_ = slot(n, KC, W)
                load(n, [(s_[:, :, y * P + g * 64:y * P + g * 64 + 64],
                          w[:, :, c + g * 256 + y * 64:c + g * 256 + y * 64 + 64])
                         for y in range(2) for g in range(2)])

            def cols_at(ap, c, w=W):
                return ap[:, :, c:c + w] if isinstance(c, int) else ap[:, :, bass.ds(c, w)]

            def merge_tiles(n0, w, c0, wbr):
                def turn(c, i):
                    for b in range(NBR):
                        load(n0 + b, [(slot(n0 + b, KC, W), cols_at(w, c * W + (c0 + b * D))),
                                      (slot(n0 + b, 4, W, KC * W), cols_at(wbr[:, 4 * b:4 * b + 4, :], c * W))],
                             i, 4, 20)
                turns(D // W, turn)

            def square_tiles(n0, w):
                for k in range(8):
                    load(n0 + k, [(slot(n0 + k, KC, W), w[:, :, k * W:(k + 1) * W])])

            def ff_tiles(name, gate, up, g0, u0, down):
                def gate_up(n, g, x, i):
                    for k, (w, c0) in enumerate(((gate, g0), (up, u0))):
                        load(n + k, [(slot(n + k, KC, W), cols_at(w, g * (2 * W) + (c0 + x * W)))], i, 12, 48)

                def down_half(n, g, x, i):
                    rows = down[:, 4 * g:4 * g + 4, x * 4 * W:(x + 1) * 4 * W] if isinstance(g, int) else \
                        down[:, bass.ds(g * 4, 4), x * 4 * W:(x + 1) * 4 * W]
                    load(n, [(slot(n, 4, 4 * W), rows)], i, 12, 48)

                n0 = at[name][0]
                gate_up(n0, 0, 0, None)
                gate_up(n0 + 2, 0, 1, None)
                n0 = at[name + "loop"][0]

                def turn(j, i):
                    for z in range(2):
                        n, g = n0 + 6 * z, 2 * j + (z + 1)
                        for x in range(2):
                            gate_up(n + 3 * x, g, x, i)
                            down_half(n + 3 * x + 2, 2 * j + z, x, i)
                turns((GROUPS - 1) // 2, turn)
                for x in range(2):
                    down_half(at[name + "end"][0] + x, GROUPS - 1, x, None)

            for c in range(2):
                paired(at["b0"][0] + c, w_in, A_Q + c * P)
            for c in range(3):
                plain(at["b2"][0] + c, w_in, A_KV + c * W)
            n = at["b5"][0]
            load(n, [(slot(n, KC, 24), w_in[:, :, A_G:A_G + 24])])
            for c in range(8):
                plain(at["hin"][0] + c, w_in, B_IN + c * W)
            for c in range(6):
                plain(at[f"b{6 + c}"][0], w_in, C_IN + c * W)
            merge_tiles(at["merge1"][0], w_in, MERGE, kp(t["w_branch"]))
            for c in range(2):
                plain(at["xk"][0] + c, kp(t["xattn_k"]), c * W)
            for c in range(2):
                plain(at["xv"][0] + c, kp(t["xattn_v"]), c * W)
            square_tiles(at["mixout1"][0], kp(t["w_mix_out"]))
            for c in range(2):
                plain(at["xq"][0] + c, kp(t["xattn_q"]), c * W)
            for c in range(2):
                n = at["xo"][0] + c
                load(n, [(slot(n, 4, 4 * W), kp(t["xattn_o"])[:, :, c * 4 * W:(c + 1) * 4 * W])])
            ff_tiles("ff1", kp(t["ffn_in"]), kp(t["ffn_in"]), 0, FF, kp(t["ffn_out"]))
            n = at["in2"][0]
            for c in range(4):
                plain(n + c, w_in2, BX2 + c * W)
            for c in range(2):
                paired(n + 4 + c, w_in2, DQ2 + c * P)
            plain(n + 6, w_in2, DKV2)
            for c in range(6):
                plain(n + 7 + c, w_in2, AQ2 + c * W)
            load(n + 13, [(slot(n + 13, KC, 4), w_in2[:, :, CF2:CF2 + 4])])
            for c in range(6):
                plain(n + 14 + c, w_in2, CQ2 + c * W)
            merge_tiles(at["merge2"][0], w_in2, GZ2, kp(t["w_branch_2"]))
            square_tiles(at["mixout2"][0], kp(t["w_out_2"]))
            ff_tiles("ff2", kp(t["w_ffn_gate_2"]), kp(t["w_ffn_up_2"]), 0, 0, kp(t["w_ffn_down_2"]))

            sp.wait_ge(rows_ready, 6)
            sp.dma_start(out.rearrange("(a p) d -> p a d", p=P), xa[:, :, :]).then_inc(out_landed, 16)
            sp.wait_ge(out_landed, 16)

        @block.gpsimd
        def _(pool):
            rows = lambda ap: ap.partition_broadcast(P)

            def bias_table(u):
                if bias_of(u) is None:
                    return
                prev = [v for v in range(u % 2, u, 2) if bias_of(v) is not None]
                if prev:
                    pool.wait_ge(biased, prev[-1] + 1)
                pool.dma_start(bias[:, u % 2, :], t["t_bias"][bias_of(u)]).then_inc(bias_landed[u % 2], 16)

            def norm_rows(k, g, b):
                if k:
                    pool.wait_ge(norm_done, k)
                n = 0
                for dst, name in ((lng[k], g), (lnb[k], b)):
                    if name:
                        pool.dma_start(dst, rows(t[name])).then_inc(norm_rows_landed, 16 if b else 32)
                        n += 1

            pool.dma_start(ident[:, :], t["t_ident"]).then_inc(ident_landed, 16)
            pool.dma_start(rowsx, t["x"].rearrange("(a p) d -> p a d", p=P)).then_inc(x_landed, 16)
            for i, st in enumerate(STACKS):
                r = 0
                for name, n in st:
                    pool.dma_start(stack_rows(i)[r:r + n, :], t[name]).then_inc(stack_landed, 16)
                    r += n
            pool.dma_start(lmask, t["t_small"][:, T_LEVEL:T_LEVEL + 8 * P].rearrange("p (a b) -> p a b", a=8))\
                .then_inc(level_tab_landed, 16)
            pool.dma_start(hgrow, rows(t["hgrn_norm_g"])).then_inc(level_tab_landed, 16)

            for u in range(U_NSA, U_X):
                bias_table(u)

            wait_copied(pool, o_of("hT"))
            ts = t["t_small"]
            half = lambda h: slice(64 * h, 64 * h + 64)
            loads = [
                (sgrow, t["sg_w"].rearrange("g q p -> q g p")),
                (tri, ts[:, T_TRI:T_TRI + P]),
                (slg, rows(t["sg_ln_g"])), (slb, rows(t["sg_ln_b"])),
                (invc, ts[:, T_COUNT:T_COUNT + 4 * S].rearrange("p (a b) -> p a b", a=4)),
                (poolw, t["pool_w"].rearrange("g c d -> c g d")),
                (ctab, ts[:, T_CBIAS:T_CBIAS + 480]),
                (posrow[0:64, 0:64], t["nsa_cmp_pos"]), (posrow[0:64, 64:128], t["nsa_cmp_pos"]),
                (cw[half(0)], t["nsa_cmp_w"].rearrange("i l d e -> d i l e")),
                (cw[half(1)], t["nsa_cmp_w"].rearrange("i l d e -> d i l e")),
            ]
            for dst, src in loads:
                pool.dma_start(dst, src).then_inc(mixer1_landed, 16)
            assert len(loads) == MIXER1_LOADS
            wait_copied(pool, o_of("nT"))
            pool.dma_start(xa[:, :, :], t["mem"].rearrange("(a p) d -> p a d", p=P)).then_inc(mem_landed, 16)
            wait_copied(pool, o_of("memT", 3))
            pool.dma_start(xa[:, :, :], t["x"].rearrange("(a p) d -> p a d", p=P)).then_inc(resid_landed, 16)
            pool.wait_ge(lo_ready, at["memT"][3] + 4)
            norm_rows(0, "ln_mix_g", "ln_mix_b")
            norm_rows(1, "ln_x_g", "ln_x_b")
            pool.wait_ge(piece_used, at["xq"][4] + 8)
            norm_rows(2, "ln_ffn_g", "ln_ffn_b")

            wait_copied(pool, o_of("xT2", 3))
            pool.wait_ge(norm_done, 3)
            pool.memset(score[:, :, :], 0.0).then_inc(lru_zeroed, 1)
            pool.wait_ge(lru_zeroed, 1)
            for i, name in enumerate(("lru_wa_2", "lru_wx_2")):
                for h in range(2):
                    pool.dma_start(wl[half(h), i, :, half(h)],
                                   t[name].rearrange("(c h) k d -> h k c d", h=2)[h]).then_inc(lru_landed, 16)
            for j, name in enumerate(("diff_lq1_2", "diff_lk1_2", "diff_lq2_2", "diff_lk2_2")):
                pool.dma_start(lrow[:, 64 * j:64 * j + 64], rows(t[name])).then_inc(mixer2_landed, 16)
            pool.dma_start(sinks, rows(t["swa_sinks_2"])).then_inc(mixer2_landed, 16)
            pool.dma_start(subln, rows(t["diff_subln_2"])).then_inc(mixer2_landed, 16)
            pool.dma_start(heads[0:4], ts[0:4, T_HEAD:T_END].rearrange("p (h c) -> p h c", h=5))\
                .then_inc(mixer2_landed, 16)
            pool.dma_start(bf[0:4], t["fox_b_f_2"].rearrange("(a b) -> a b", b=1)).then_inc(mixer2_landed, 16)
            for u in range(U_SWA, U_END):
                bias_table(u)
            wait_copied(pool, o_of("x3T", 3))
            pool.wait_ge(rows_ready, 5)
            norm_rows(3, "norm_final_2", None)

        @block.tensor
        def _(pe):
            mm, turn = nc.tensor.matmul, nc.tensor.transpose
            rows_done = Count(pe, pe_rows)

            def slot(n, k=KC, w=W, off=0):
                return ring[:, n % SLOTS, off:off + k * w].rearrange("p (k c) -> p k c", k=k)

            def landed(n):
                pe.wait_ge(w_landed[n % SLOTS], LANDED * (n // SLOTS + 1))

            def features(dst, w, act, k0=0, kn=KC, c0=0, m=P, start=True, stop=True):
                for k in range(kn):
                    last = mm(dst, w[:, k, c0:c0 + m], act[:, k0 + k, :], start=start and k == 0,
                              stop=stop and k == kn - 1)
                return last

            def tokens(dst, w, act, q, k0=0, kn=KC, c0=0, m=W, start=True, stop=True):
                for k in range(kn):
                    last = mm(dst, act[:, k0 + k, q * P:(q + 1) * P], w[:, k, c0:c0 + m],
                              start=start and k == 0, stop=stop and k == kn - 1)
                return last

            def f_tile(n, o, act, units=((), ())):
                landed(n)
                wait_bank(o)
                b = banks(o)
                for x in range(2):
                    last = features(b[:, x, 0:S], slot(n), act, c0=x * P)
                    if x:
                        last.then_inc(tile_used, 1)
                    for u in units[x]:
                        unit_step(*u)

            def t_tile(n, o, act, units=((), ())):
                landed(n)
                wait_bank(o)
                b = banks(o)
                for q in range(NT):
                    last = tokens(b[:, q, 0:W], slot(n), act, q)
                    if q:
                        last.then_inc(tile_used, 1)
                    for u in units[q]:
                        unit_step(*u)

            def tiles_with_units(name, k, by_token):
                n, o = at[name][0], o_of(name, k)
                for a, b in groups_at(name, k):
                    wait_copied(pe, o - 2)
                    wait_copied(pe, o - 1)
                    if a == U_SWA:
                        pe.wait_ge(mixer_rows, 6 + 1)
                    scores(a)
                (t_tile if by_token else f_tile)(n + k, o, actT, [unit_behind(name, k, x) for x in range(2)])

            def turn_rows(name, rows):
                for k in range(4):
                    o = o_of(name, k)
                    wait_bank(o)
                    b = banks(o).rearrange("p a (c t) -> p (a c) t", c=2)
                    for c in range(4):
                        for q in range(NT):
                            last = turn(b[:, c, q * P:(q + 1) * P],
                                        rows[:, q, (4 * k + c) * P:(4 * k + c + 1) * P], ident[:, :])
                    last.then_inc(part_done, 1)

            def turn_branch(name, rows):
                o = o_of(name)
                wait_bank(o)
                b = banks(o).rearrange("p a (c t) -> p (a c) t", c=2)
                for c in range(4):
                    for q in range(NT):
                        last = turn(b[:, c, q * P:(q + 1) * P], rows[:, q, c * P:(c + 1) * P], ident[:, :])
                last.then_inc(part_done, 1)

            def wait_all_copied(name, n):
                for k in range(max(0, n - 2), n):
                    wait_copied(pe, o_of(name, k))

            def piece_product(s_, p_, o, first, last_, act, k0, by_token, i=None, per_s=0, per_o=0):
                reach(pe, lo_ready, s_ + 1, i, per_s)
                if first:
                    wait_bank(o, i, per_o)
                b = banks(o)
                w3 = [x[:, p_ % PIECES, :].rearrange("p (k c) -> p k c", k=4) for x in (whi, wlo)]
                for x in range(2):
                    xs = slice(x * P, (x + 1) * P)
                    for k in range(4):
                        for n, (wp, ap) in enumerate(((0, 0), (0, 1), (1, 0))):
                            if by_token:
                                l_, r_ = act(ap)[:, k0 + k, xs], w3[wp][:, k, :]
                            else:
                                l_, r_ = w3[wp][:, k, xs], act(ap)[:, k0 + k, :]
                            last = mm(b[:, x, 0:W], l_, r_, start=first and k == 0 and n == 0,
                                      stop=last_ and k == 3 and n == 2)
                last.then_inc(piece_used, 1)

            part_of = lambda R: lambda ap: R[:, ap]

            def whole(s_, p_, o, act, by_token, **kw):
                for k in range(4):
                    piece_product(s_ + k, p_ + k, o, k == 0, k == 3, act, 4 * k, by_token, **kw)

            def whole_tiles(name, n, act, by_token):
                _, _, o, s_, p_ = at[name]
                for k in range(n):
                    whole(s_ + 4 * k, p_ + 4 * k, o + k, act, by_token)

            def mix_out(name):
                _, _, o, s_, p_ = at[name]
                with pe.Fori(0, 4) as i:
                    for k in range(2):
                        whole(s_ + 4 * k, p_ + 4 * k, o + k, part_of(mixR), True, i=i, per_s=8, per_o=2)

            def merge(name):
                _, _, o0, s0, p0 = at[name]
                with pe.Fori(0, D // W) as i:
                    kw = dict(i=i, per_s=20, per_o=8)
                    for b in range(NBR):
                        whole(s0 + 5 * b, p0 + 5 * b, o0 + 2 * b, part_of(actR), False, **kw)
                        piece_product(s0 + 5 * b + 4, p0 + 5 * b + 4, o0 + 2 * b + 1, True, True, part_of(brR),
                                      4 * b, False, **kw)

            def feed_forward(name, act):
                def gate_up(s_, p_, o, **kw):
                    for k in range(2):
                        whole(s_ + 4 * k, p_ + 4 * k, o + k, act, False, **kw)

                def down_half(par, g, s_, p_, o, x, i=None, **kw):
                    if x == 0:
                        reach(pe, hid_lo, 2 * g + 2, i, 4)
                    for k in range(4):
                        piece_product(s_ + k, p_ + k, o + k, True, True, lambda ap: hidR(par, ap), 0, True, i=i, **kw)

                _, _, o, s_, p_ = at[name]
                gate_up(s_, p_, o)
                gate_up(s_ + 8, p_ + 8, o + 2)
                _, _, o, s_, p_ = at[name + "loop"]
                h0 = hid0[name]
                with pe.Fori(0, (GROUPS - 1) // 2) as i:
                    kw = dict(i=i, per_s=48, per_o=24)
                    for z in range(2):
                        for x in range(2):
                            d = 24 * z + 12 * x
                            gate_up(s_ + d, p_ + d, o + 12 * z + 6 * x, **kw)
                            down_half(z, h0 + z, s_ + d + 8, p_ + d + 8, o + 12 * z + 6 * x + 2, x, **kw)
                _, _, o, s_, p_ = at[name + "end"]
                for x in range(2):
                    down_half(0, h0 + GROUPS - 1, s_ + 4 * x, p_ + 4 * x, o + 4 * x, x)

            def scores(u):
                q_, k_, extra, _, _ = unit(u)
                if u >= 2:
                    pe.wait_ge(biased, u - 1)
                for m in range(2):
                    dst = sc[:, u % 2, m * S:(m + 1) * S]
                    more = extra(m)
                    last = mm(dst, q_(m), k_(m), start=True, stop=not more)
                    for x, (l_, r_) in enumerate(more):
                        last = mm(dst, l_, r_, start=False, stop=x == len(more) - 1)
                    if m == 0 and kind(u) not in ("x", "fox"):
                        rows_done.link(last)
                last.then_inc(scores_done, 1)

            def turn_probs(u):
                pe.wait_ge(probs_ready, u + 1)
                if u:
                    pe.wait_ge(probT_ready, u)
                for x in range(4):
                    last = turn(pt[:, x * P:(x + 1) * P], score[:, u % 2, x * P:(x + 1) * P], ident[:, :])
                last.then_inc(probs_turned, 1)

            def values(u):
                _, _, _, v_, dv = unit(u)
                pe.wait_ge(probT_ready, u + 1)
                if u:
                    pe.wait_ge(pv_used, u)
                for m in range(2):
                    for kt in range(NT):
                        last = mm(pv[:, m * dv:(m + 1) * dv], probT[:, u % 2, (2 * m + kt) * P:(2 * m + kt + 1) * P],
                                  v_(m, kt), start=kt == 0, stop=kt == NT - 1)
                last.then_inc(pv_done, 1)

            def unit_step(u, a, b):
                if u + 1 < b:
                    scores(u + 1)
                if u > a:
                    values(u - 1)
                turn_probs(u)
                if u == b - 1:
                    values(u)

            def attend(a, b):
                scores(a)
                for u in range(a, b):
                    unit_step(u, a, b)

            pe.wait_ge(ident_landed, 16)
            pe.wait_ge(stack_landed, 16 * sum(len(s_) for s_ in STACKS))
            for i, st in enumerate(STACKS):
                r = sum(n for _, n in st)
                last = turn(acc[:, 0, i * P:i * P + r], stack_rows(i)[0:r, :], ident[0:r, 0:r])
            last.then_inc(part_done, 1)
            pe.wait_ge(x_landed, 16)
            turn_rows("xT1", rowsx)
            wait_all_copied("xT1", 4)

            def b_tile_products(k):
                n, _, o = at[f"b{k}"][:3]
                if k in (0, 1, 2, 6, 7):
                    f_tile(n, o, actT)
                elif k in (3, 4):
                    key_value_tile(n, o)
                elif k == 5:
                    landed(n)
                    wait_bank(o)
                    for q in range(NT):
                        last = tokens(banks(o)[:, 0, q * 24:(q + 1) * 24], slot(n, KC, 24), actT, q, m=24)
                    last.then_inc(tile_used, 1)
                else:
                    t_tile(n, o, actT)

            def key_value_tile(n, o):
                landed(n)
                wait_bank(o)
                b = banks(o)
                features(b[:, 0, 0:S], slot(n), actT)
                for q in range(NT):
                    last = tokens(b[:, 1, q * P:(q + 1) * P], slot(n), actT, q, c0=P, m=P)
                last.then_inc(tile_used, 1)

            for k in range(6):
                b_tile_products(k)
            for k in range(8):
                tiles_with_units("hin", k, k >= 4)
            b_tile_products(6)
            n = 7
            for lv in range(HL + 2):
                pe.wait_ge(level_ready, lv + 1)
                o = o_of(f"lvl{lv}")
                wait_bank(o)
                b = banks(o)
                if lv <= HL:
                    for q in range(NT):
                        for h in range(4):
                            last = mm(b[:, q, h * P:(h + 1) * P], hkd[:, h, q * P:(q + 1) * P],
                                      hqd[:, h, q * P:(q + 1) * P], start=True, stop=True)
                else:
                    for h in range(4):
                        last = mm(b[:, 0, h * P:(h + 1) * P], hkd[:, h, 0:P], hqd[:, h, P:S], start=True, stop=True)
                last.then_inc(part_done, 1)
                for _ in range(B_AFTER[lv]):
                    b_tile_products(n)
                    n += 1
            pe.wait_ge(decay_ready, 1)
            o = o_of("ho")
            wait_bank(o)
            b = banks(o)
            A = lambda q, h: ATd[:, (q * 4 + h) * P:(q * 4 + h + 1) * P]
            for h in range(4):
                hs = slice(h * P, (h + 1) * P)
                mm(b[:, 0, hs], A(0, h), hi[:, 0, hs], start=True, stop=True)
                mm(b[:, 1, hs], A(1, h), hi[:, 1, hs], start=True, stop=False)
                last = mm(b[:, 1, hs], ATx[:, h, :], hi[:, 0, hs], start=False, stop=True)
            last.then_inc(part_done, 1)
            pe.wait_ge(mixer_rows, 1)
            turn_branch("hT", ho)

            pe.wait_ge(mixer1_landed, 16 * MIXER1_LOADS)
            o = o_of("sgw")
            wait_bank(o)
            for g in range(4):
                last = turn(banks(o)[:, 0, g * P:(g + 1) * P], sgrow[:, g, :], ident[:, :])
            last.then_inc(part_done, 1)
            pe.wait_ge(mixer_rows, 2)
            o = o_of("pool")
            wait_bank(o)
            b = banks(o).rearrange("p a (c t) -> p (a c) t", c=2)
            for g in range(4):
                last = mm(b[:, g, :], poolw[:, g, :], ping[:, g, 16:], start=True, stop=True)
            last.then_inc(part_done, 1)
            pe.wait_ge(mixer_rows, 3)
            o = o_of("sgo")
            wait_bank(o)
            for q in range(NT):
                for g in range(4):
                    gs = slice(g * P, (g + 1) * P)
                    last = mm(banks(o)[:, q, gs], wmT[:, g, :], sv[:, q, gs], start=True, stop=True)
            last.then_inc(part_done, 1)
            pe.wait_ge(mixer_rows, 4)
            turn_branch("sgT", su)

            o = o_of("pos")
            wait_bank(o)
            turn(banks(o)[:, 0, 0:64], posrow[0:64, :], ident[0:64, 0:64]).then_inc(part_done, 1)
            pe.wait_ge(cmp_ready, 1)
            o = o_of("ckv")
            wait_bank(o)
            b = banks(o)
            for g in range(2):
                gh = slice(64 * g, 64 * g + 64)
                for l in range(32):
                    mm(b[gh, 0, 0:NC], cw[gh, 0, l, :], win[gh, 0, l, :], start=l == 0, stop=l == 31)
            for g in range(2):
                gh = slice(64 * g, 64 * g + 64)
                for l in range(32):
                    last = mm(b[0:NC, 1, gh], win[gh, 1, l, :], cw[gh, 1, l, :], start=l == 0, stop=l == 31)
                if g == 0:
                    rows_done.link(last)
            last.then_inc(part_done, 1)
            wait_copied(pe, o_of("ckv"))
            o = o_of("cs")
            wait_bank(o)
            b = banks(o)
            for g in range(2):
                gh = slice(64 * g, 64 * g + 64)
                for q in range(NT):
                    for h in range(4 * g, 4 * g + 4):
                        last = mm(b[:, q, h * NC:(h + 1) * NC], qn[gh, h % 4, q * P:(q + 1) * P], kcmp[gh, :],
                                  start=True, stop=True)
                if g == 0:
                    rows_done.link(last)
            last.then_inc(part_done, 1)
            pe.wait_ge(cmp_ready, 3)
            for q in range(NT):
                o = o_of("cT", q)
                wait_bank(o)
                b = banks(o).rearrange("p a (c t) -> p (a c) t", c=4)
                for h in range(NH):
                    at_ = (q * NH + h) * NC
                    last = turn(b[0:NC, h, :], cS[:, at_:at_ + NC], ident[:, :])
                last.then_inc(part_done, 1)
            wait_copied(pe, o_of("cT", 0))
            wait_copied(pe, o_of("cT", 1))
            o = o_of("co")
            wait_bank(o)
            for q in range(NT):
                for h in range(NH):
                    g = h // 4
                    last = mm(banks(o)[:, q, 64 * h:64 * h + 64], cPT[0:NC, q * NH + h, :],
                              vcmp[0:NC, 64 * g:64 * g + 64], start=True, stop=True)
            last.then_inc(part_done, 1)
            pe.wait_ge(mixer_rows, 5)
            turn_branch("nT", oa)
            wait_copied(pe, o_of("nT"))

            merge("merge1")
            pe.wait_ge(rows_ready, 1)
            turn_rows("memT", xa)
            whole_tiles("xk", 2, part_of(brR), False)
            whole_tiles("xv", 2, part_of(brR), True)
            pe.wait_ge(gate_used, 8)
            mix_out("mixout1")

            pe.wait_ge(rows_ready, 2)
            turn_rows("x1T", xa)
            whole_tiles("xq", 2, part_of(mixR), False)
            wait_all_copied("xq", 2)
            attend(U_X, U_SWA)
            pe.wait_ge(mixer_rows, 6)
            turn_branch("xoT", ox)
            _, _, o, s_, p_ = at["xo"]
            for k in range(8):
                piece_product(s_ + k, p_ + k, o + k, True, True, part_of(brR), 0, True)

            pe.wait_ge(rows_ready, 3)
            turn_rows("x2T", xa)
            feed_forward("ff1", part_of(actR))

            pe.wait_ge(rows_ready, 4)
            turn_rows("xT2", rowsx)
            wait_all_copied("xT2", 4)
            n, o = at["in2"][0], o_of("in2")

            def lru_gates():
                pe.wait_ge(lru_landed, 64)
                pe.wait_ge(lru_conv, 1)
                for w_ in range(2):
                    o = o_of("lru", w_)
                    wait_bank(o)
                    b = banks(o).rearrange("p a (c t) -> p (a c) t", c=2)
                    for c in range(4):
                        last = mm(b[:, c, :], wl[:, w_, c, :], xc[:, c, :], start=True, stop=True)
                    last.then_inc(part_done, 1)

            for k in range(6):
                f_tile(n + k, o + k, actT)
            key_value_tile(n + 6, o + 6)
            lru_gates()
            n, o = at["in2b"][0] - 7, o_of("in2b") - 7
            for k in range(7, 13):
                tiles_with_units("in2", k, k >= 11)
            landed(n + 13)
            wait_bank(o + 13)
            features(banks(o + 13)[0:4, 0, 0:S], slot(n + 13, KC, 4), actT, m=4).then_inc(tile_used, 1)
            for k in range(14, 20):
                tiles_with_units("in2", k, k >= 18)

            wait_copied(pe, o + 18)
            wait_copied(pe, o + 19)
            pe.wait_ge(mixer_rows, 8)
            attend(U_FOX, U_END)
            pe.wait_ge(mixer_rows, 9)
            for name, rows in (("y0T", ya), ("y2T", yc), ("y3T", yd)):
                turn_branch(name, rows)
            wait_copied(pe, o_of("y2T"))
            wait_copied(pe, o_of("y3T"))
            merge("merge2")
            pe.wait_ge(gate_used, 16)
            mix_out("mixout2")
            pe.wait_ge(rows_ready, 5)
            turn_rows("x3T", rowsx)
            feed_forward("ff2", part_of(mixR))

        @block.scalar
        def _(act):
            f = nc.scalar.activation
            own = Count(act, s_link)

            def halves(o):
                return banks(o)[:, :, 0:S]

            def tile_out(name, k, dst, func=ACT.Copy, src=None, scale=1.0):
                o = o_of(name, k)
                wait_tile(act, name, k)
                release(f(dst, halves(o) if src is None else src(banks(o)), func, scale=scale), o)

            def part_out(name, k, dst, func=ACT.Copy, src=None):
                o = o_of(name, k)
                wait_part(act, name, k)
                release(f(dst, banks(o) if src is None else src(banks(o)), func), o)

            def turned_out(name, dst):
                for k in range(4):
                    part_out(name, k, dst[:, 4 * k:4 * k + 4, :].rearrange("p (a c) t -> p a (c t)", a=2))

            def branch_out(name, chunk):
                part_out(name, 0, brT[:, chunk:chunk + 4, :].rearrange("p (a c) t -> p a (c t)", a=2))

            def split(d, i):
                if d.k == 0:
                    reach(act, w_landed[d.tile % SLOTS], LANDED * (d.tile // SLOTS + 1), i,
                          LANDED * d.per_tile // SLOTS)
                if d.piece >= PIECES or not isinstance(i, int):
                    reach(act, piece_used, d.piece + 1 - PIECES, i, d.per_piece)
                f(part_of_piece(whi, d), raw(d), ACT.Copy).then_inc(hi_ready, 1)

            def high(R, src, k):
                f(R[:, 0, 4 * k:4 * k + 4, :], src, ACT.Copy).then_inc(hi_ready, 1)

            def turned_high(name, R, n=4):
                for k in range(n):
                    wait_part(act, name, k)
                    b = banks(o_of(name, k)).rearrange("p a (c t) -> p (a c) t", c=2)
                    high(R, b, k)

            def finish_copy(dst):
                def finish(d, i):
                    if d.ends:
                        product(act, d, i)
                        release(f(dst(d.c), halves(d.out), ACT.Copy), d.out)
                return finish

            def finish_none(d, i):
                pass

            def hidden_step(from_bank):
                def finish(d, i):
                    if not d.hid:
                        return
                    step, hd = d.hid
                    x, h = hd["x"], hd["h"]
                    silu = lambda src: f(siluS[:, x, :].rearrange("p (a c) -> p a c", a=2), src, ACT.Silu)
                    if step == ("gate" if from_bank else "silu"):
                        if h >= 2:
                            reach(act, hid_lo, h - 1, i, hd["per_h"])
                        if from_bank:
                            product(act, d, i)
                            release(silu(halves(hd["og"])), hd["og"])
                        else:
                            copied(act, hd["og"], i, hd["per_out"])
                            silu(convS[:, x, :].rearrange("p (a c) -> p a c", a=2)).then_inc(silu_ready, 1)
                    elif step == "hi":
                        copied(act, hd["ou"], i, hd["per_out"])
                        f(hidR(hd["par"], 0)[:, 2 * x:2 * x + 2, :],
                          siluS[:, x, :].rearrange("p (a c) -> p a c", a=2), ACT.Copy).then_inc(hid_hi, 1)
                return finish

            def feed_forward(name, from_bank):
                first, before, turn_, behind = ff_pieces(name)
                finish = hidden_step(from_bank)
                straight(before, split, finish)
                finish(Piece(0, 0, 0, 0, 0, 0, hid=("hi", first[1])), 0)
                in_turns(act, (GROUPS - 1) // 2, turn_, split, finish, behind)

            def root(k, n):
                act.wait_ge(var_ready, k)
                f(stats[:, 72:72 + n], stats[:, 64:64 + n], ACT.Sqrt).then_inc(std_ready, 1)

            def exps(u):
                act.wait_ge(max_ready, u + 1)
                c = 2 * (u % 4)
                for m in range(2):
                    s_ = score[:, u % 2, m * S:(m + 1) * S]
                    last = f(s_, s_, ACT.Exp, bias=vecs[:, c + m:c + m + 1],
                             accum_out=vecs[:, 8 + c + m:9 + c + m])
                if kind(u) == "swa":
                    for m in range(2):
                        h = ((u - U_SWA) // 2) + 4 * m
                        last = f(vecs[:, 24 + c + m:25 + c + m], sinks[:, h:h + 1], ACT.Exp,
                                 bias=vecs[:, c + m:c + m + 1])
                last.then_inc(probs_ready, 1)

            def copy_probs(u):
                act.wait_ge(probs_turned, u + 1)
                if u >= 2:
                    act.wait_ge(pv_done, u - 1)
                f(probT[:, u % 2, :], pt[:, :], ACT.Copy).then_inc(probT_ready, 1)

            def unit_step(u, a, b):
                if u == a:
                    exps(a)
                if u + 1 < b:
                    exps(u + 1)
                copy_probs(u)

            def attend(a, b):
                for u in range(a, b):
                    unit_step(u, a, b)

            def with_units(name, k, *out_, **kw):
                for u in unit_behind(name, k, 0):
                    unit_step(*u)
                tile_out(name, k, *out_, **kw)
                for u in unit_behind(name, k, 1):
                    unit_step(*u)

            wait_part(act, "cols")
            for i, st in enumerate(STACKS):
                r = sum(n for _, n in st)
                last = f(cols[:, i, 0:r], acc[:, 0, i * P:i * P + r], ACT.Copy)
            release(last, o_of("cols"))
            act.wait_ge(lb_max, 1)
            f(lbv[:, 4:8], lbv[:, 0:4], ACT.Exp).then_inc(lb_exp, 1)
            turned_out("xT1", actT)

            for k in range(2):
                tile_out(f"b{k}", 0, qn[:, 2 * k:2 * k + 2, :])
            for k, dst in enumerate((kvc, kvs, kvw)):
                tile_out(f"b{2 + k}", 0, dst)
            tile_out("b5", 0, ag.rearrange("p a b -> p (a b)"), ACT.Sigmoid, src=lambda b: b[:, 0, 0:48])
            for k in range(2):
                with_units("hin", k, hq[:, 2 * k:2 * k + 2, :])
            for k in range(2):
                with_units("hin", 2 + k, hp[:, 2 * k:2 * k + 2, :], ACT.Sigmoid)
            for k in range(2):
                with_units("hin", 4 + k, hi[:, :, k * W:(k + 1) * W])
            for k in range(2):
                with_units("hin", 6 + k, hg[:, :, k * W:(k + 1) * W], ACT.Silu)
            for k in range(2):
                tile_out(f"b{6 + k}", 0, cpad[:, 2 * k:2 * k + 2, 16:])
            for k in range(2):
                tile_out(f"b{8 + k}", 0, su[:, :, k * W:(k + 1) * W], ACT.Gelu_apprx_tanh)
            for k in range(2):
                tile_out(f"b{10 + k}", 0, sv[:, :, k * W:(k + 1) * W], ACT.Gelu_apprx_tanh)
            part_out("ho", 0, ho)
            root(1, 8)
            branch_out("hT", 4)
            root(2, 2)
            branch_out("sgT", 12)
            act.wait_ge(cmp_ready, 2)
            f(cS, cS, ACT.Exp).then_inc(cmp_exp, 1)
            for q in range(NT):
                part_out("cT", q, cPT[0:NC, q * NH:(q + 1) * NH, :].rearrange("p (a c) t -> p a (c t)", a=2),
                         src=lambda b: b[0:NC])
            branch_out("nT", 0)

            def merge_inputs():
                for k in range(4):
                    high(actR, actT[:, 4 * k:4 * k + 4, :], k)
                for k in range(4):
                    high(brR, brT[:, 4 * k:4 * k + 4, :], k)

            def gate(d, i):
                if d.ends == "gate":
                    product(act, d, i)
                    o = d.out + 1 - 4
                    reach(act, acc_free[o % 2], o // 2 + 1, i, d.per_out // 2)
                    release(f(gateS[:, d.b % 2, :].rearrange("p (a c) -> p a c", a=2), halves(d.out), ACT.Sigmoid),
                            d.out)

            wait_copied(act, o_of("nT"))
            merge_inputs()

            def gate_and_root(d, i):
                gate(d, i)
                if isinstance(i, int) and i == 0 and d == merge_pieces("merge1")[NORM_ROOT]:
                    root(3, 2)

            in_turns(act, D // W, merge_pieces("merge1"), split, gate_and_root)

            for k in range(4):
                wait_part(act, "memT", k)
                o = o_of("memT", k)
                b = banks(o).rearrange("p a (c t) -> p (a c) t", c=2)
                tmp = mem_tmp[k % 2].rearrange("p (c t) -> p c t", c=4)
                if k >= 2:
                    act.wait_ge(lo_ready, at["memT"][3] + k - 1)
                for c in range(4):
                    last = f(tmp[:, c, :], b[:, c, :], ACT.Identity,
                             scale=col("mem_ln_g", 4 * k + c), bias=col("mem_ln_b", 4 * k + c))
                release(last, o)
                wait_copied(act, o)
                high(brR, tmp, k)
            straight(tile_pieces("xk", 2), split, finish_copy(lambda c: kx[:, 2 * c:2 * c + 2, :]))
            straight(tile_pieces("xv", 2), split, finish_copy(lambda c: vx[:, :, c * W:(c + 1) * W]))
            in_turns(act, 4, tile_pieces("mixout1", 8, 4), split, finish_none)
            root(4, 2)
            turned_high("x1T", mixR)
            straight(tile_pieces("xq", 2), split, finish_copy(lambda c: qx[:, 2 * c:2 * c + 2, :]))
            attend(U_X, U_SWA)
            turned_high("xoT", brR, 1)
            straight(wide_pieces("xo"), split, finish_none)
            root(5, 2)
            turned_high("x2T", actR)
            feed_forward("ff1", False)
            root(6, 2)
            root(7, 2)

            def pair_out(k, dst, func=ACT.Copy, scale=1.0):
                for x in range(2):
                    with_units("in2", k + x, dst[:, 2 * x:2 * x + 2, :], func, scale=scale)

            def rows_out(k, dst):
                for x in range(2):
                    with_units("in2", k + x, dst[:, :, x * W:(x + 1) * W])

            pair_out(0, bx[:, :, 4:])
            pair_out(2, bg, ACT.Gelu_apprx_tanh)
            act.wait_ge(sp_abs, 1)
            f(lbv[:, 20:24], lbv[:, 16:20], ACT.Exp).then_inc(sp_exp, 1)
            act.wait_ge(lam_sum, 1)
            f(lbv[:, 34:36], lbv[:, 32:34], ACT.Exp).then_inc(lam_exp, 1)
            pair_out(4, dq)
            tile_out("in2", 6, dkv)
            for w_, (dst, bcol) in enumerate(((lr, "lru_ba_2"), (li, "lru_bx_2"))):
                wait_part(act, "lru", w_)
                b = banks(o_of("lru", w_)).rearrange("p a (c t) -> p (a c) t", c=2)
                for c in range(4):
                    last = f(dst[:, c, :], b[:, c, :], ACT.Sigmoid, bias=col(bcol, c))
                release(last, o_of("lru", w_))
            act.wait_ge(lru_arg, 1)
            f(lt, lr, ACT.Tanh, scale=-1.0)
            f(la, lr, ACT.Exp).then_inc(lru_exp, 1)
            tile_out("in2", 7, aq[:, 0:2, :])
            act.wait_ge(lru_sq, 1)
            f(lt, lt, ACT.Sqrt, scale=2.0).then_inc(lru_sqrt, 1)
            tile_out("in2", 8, aq[:, 2:4, :])
            pair_out(9, ak)
            rows_out(11, av)
            tile_out("in2", 13, cf[0:4, :], src=lambda b: b[0:4, 0, 0:S])
            act.wait_ge(sp_abs, 2)
            f(ftmp[0:4, 1, :], ftmp[0:4, 0, :], ACT.Exp).then_inc(sp_exp, 1)
            pair_out(14, cq, scale=P ** -0.5)
            pair_out(16, ck)
            rows_out(18, cv)
            attend(U_FOX, U_END)
            root(8, 8)
            branch_out("y0T", 0)
            branch_out("y2T", 8)
            branch_out("y3T", 12)

            def gate_in_place(d, i):
                if d.ends == "gate":
                    copied(act, d.out, i, d.per_out)
                    f(gateS[:, d.b % 2, :], gateS[:, d.b % 2, :], ACT.Sigmoid).then_inc(gate_ready, 1)

            wait_copied(act, o_of("y3T"))
            merge_inputs()
            in_turns(act, D // W, merge_pieces("merge2"), split, gate_in_place)
            in_turns(act, 4, tile_pieces("mixout2", 8, 4), split, finish_none)
            root(9, 2)
            for k in range(4):
                wait_copied(act, o_of("x3T", k))
                high(mixR, turn_tmp[k % 2].rearrange("p (c t) -> p c t", c=4), k)

            feed_forward("ff2", True)
            root(10, 2)

        @block.vector
        def _(dve):
            v = nc.vector
            own = Count(dve, v_link)
            link = own.link
            tt, ts_, stt = v.tensor_tensor, v.tensor_scalar, v.scalar_tensor_tensor
            mean_var = stats[:, 48:52].rearrange("p (q x) -> p q x", q=NT)
            rstd = stats[:, 80:88]

            def root(k, n):
                dve.wait_ge(std_ready, k)
                link(v.reciprocal(rstd[:, 0:n], stats[:, 72:72 + n]))

            def moments(X, width, k, eps, rms=False):
                g = width // 512
                st = stats[:, 0:NT * g * 6].rearrange("p (q g x) -> p q g x", q=NT, g=g)
                for q in range(NT):
                    for s_ in range(g):
                        own.tick(v.bn_stats(st[:, q, s_, :], X[:, q, s_ * 512:(s_ + 1) * 512]))
                own.done()
                for q in range(NT):
                    own.tick(v.bn_aggr(mean_var[:, q, :], st[:, q, :, :].rearrange("p g x -> p (g x)")))
                own.done()
                if rms:
                    link(tt(stats[:, 56:58], mean_var[:, :, 0], mean_var[:, :, 0], ALU.mult))
                    link(tt(mean_var[:, :, 1], stats[:, 56:58], mean_var[:, :, 1], ALU.add))
                ts_(stats[:, 64:66], mean_var[:, :, 1], eps, None, ALU.add).then_inc(var_ready, 1)
                root(k, 2)

            def center(dst, X):
                for q in range(NT):
                    own.tick(ts_(dst[:, q, :], X[:, q, :], mean_var[:, q, 0:1], rstd[:, q:q + 1],
                                 ALU.subtract, ALU.mult))
                own.done()

            def layer_norm_rows(k, rows_k, count):
                moments(xa, D, rows_k, LN_EPS)
                center(xa, xa)
                dve.wait_ge(norm_rows_landed, 32 * (k + 1))
                link(tt(xa[:, :, :], xa[:, :, :], lng[k].unsqueeze(1).broadcast_to([P, NT, D]), ALU.mult))
                ins = tt(xa[:, :, :], xa[:, :, :], lnb[k].unsqueeze(1).broadcast_to([P, NT, D]), ALU.add)
                if count:
                    ins.then_inc(rows_ready, 1)
                    dve.wait_ge(rows_ready, count)
                else:
                    link(ins)
                v.memset(stats[:, 90:91], 0.0).then_inc(norm_done, 1)

            def rms_rows(dst, k, count):
                moments(xa, D, k, RMS_EPS, rms=True)
                for q in range(NT):
                    ins = ts_(dst[:, q, :], xa[:, q, :], rstd[:, q:q + 1], None, ALU.mult)
                ins.then_inc(rows_ready, 1)

            def scaled_out(name, norm):
                for k in range(4):
                    wait_part(dve, name, k)
                    o = o_of(name, k)
                    b = banks(o).rearrange("p a (c t) -> p (a c) t", c=2)
                    release(tt(actT[:, 4 * k:4 * k + 4, :], b,
                               col(norm, 4 * k, 4).unsqueeze(2).broadcast_to([P, 4, S]), ALU.mult), o)

            def low(R, src, k):
                ks = slice(4 * k, 4 * k + 4)
                return tt(R[:, 1, ks, :], src, R[:, 0, ks, :].bitcast(F32), ALU.subtract)

            def wait_high(s_, i=None, per=0):
                reach(dve, hi_ready, s_ + 1, i, per)

            def split(d, i):
                wait_high(d.split, i, d.per_piece)
                tt(part_of_piece(wlo, d), raw(d), part_of_piece(whi, d).bitcast(F32), ALU.subtract)\
                    .then_inc(lo_ready, 1)

            def merge_inputs(name, name_br):
                for nm, R, src in ((name, actR, actT), (name_br, brR, brT)):
                    for k in range(4):
                        wait_high(at[nm][3] + k)
                        low(R, src[:, 4 * k:4 * k + 4, :], k).then_inc(lo_ready, 1)

            def turned_low(name, R, n=4):
                for k in range(n):
                    o = o_of(name, k)
                    wait_high(at[name][3] + k)
                    release(low(R, banks(o).rearrange("p a (c t) -> p (a c) t", c=2), k), o)
                    v.memset(stats[:, 96 + k:97 + k], 0.0).then_inc(lo_ready, 1)

            def finish_none(d, i):
                pass

            def finish_rows(alpha, stage, dynamic=False):
                def finish(d, i):
                    if d.ends == "rows":
                        product(dve, d, i)
                        x = xa[:, :, bass.ds(i * (2 * W) + d.c * W, W) if dynamic else slice(d.c * W, (d.c + 1) * W)]
                        b = banks(d.out)[:, :, 0:W]
                        release(stt(x, x, alpha, b, ALU.mult, ALU.add) if alpha else tt(x, x, b, ALU.add), d.out)
                    if stage:
                        stage(d, i)
                return finish

            def square_out(name, alpha):
                in_turns(dve, 4, tile_pieces(name, 8, 4), split, finish_rows(alpha, None, dynamic=True))
                for k in (6, 7):
                    wait_copied(dve, o_of(name, k))

            def hidden_step(conv):
                def finish(d, i):
                    if not d.hid:
                        return
                    step, hd = d.hid
                    x, h, per_o = hd["x"], hd["h"], hd["per_out"]
                    pair = siluS[:, x, :].rearrange("p (a c) -> p a c", a=2)
                    if step == "gate" and conv:
                        product(dve, d, i)
                        g = banks(hd["og"])
                        cv_ = lambda a, off: convS[:, x, a * S + off:(a + 1) * S]

                        def tap(st, r, a):
                            at_col = r + hd["chunk"] + a
                            return cols[:, st, at_col:at_col + 1] if not hd["per_chunk"] or isinstance(i, int) and i == 0 \
                                else cols[:, st, bass.ds(i * hd["per_chunk"] + at_col, 1)]

                        for a in range(2):
                            own.tick(ts_(cv_(a, 0), g[:, a, 0:S], tap(3, 0, a), tap(1, 64, a), ALU.mult, ALU.add))
                        own.done()
                        for a in range(2):
                            own.tick(stt(cv_(a, 1), g[:, a, 0:S - 1], tap(2, FC, a), cv_(a, 1), ALU.mult, ALU.add))
                        own.done()
                        for a in range(2):
                            ins = stt(cv_(a, 2), g[:, a, 0:S - 2], tap(2, 0, a), cv_(a, 2), ALU.mult, ALU.add)
                        release(ins, hd["og"])
                    elif step == "up":
                        if conv:
                            reach(dve, silu_ready, h + 1, i, hd["per_h"])
                        else:
                            copied(dve, hd["og"], i, per_o)
                        product(dve, d, i)
                        release(tt(pair, banks(hd["ou"])[:, :, 0:S], pair, ALU.mult), hd["ou"])
                    elif step == "lo":
                        reach(dve, hid_hi, h + 1, i, hd["per_h"])
                        lo, hi_ = (hidR(hd["par"], part)[:, 2 * x:2 * x + 2, :] for part in (1, 0))
                        tt(lo, pair, hi_.bitcast(F32), ALU.subtract).then_inc(hid_lo, 1)
                return finish

            def feed_forward(name, conv):
                first, before, turn_, behind = ff_pieces(name)
                finish = hidden_step(conv)
                straight(before, split, finish)
                finish(Piece(0, 0, 0, 0, 0, 0, hid=("lo", first[1])), 0)
                in_turns(dve, (GROUPS - 1) // 2, turn_, split, finish_rows(None, finish), behind,
                         own, 16 if conv else 0)
                for k in (6, 7):
                    wait_copied(dve, o_of(name + "end", k))

            def log1p(z, s_, s2, p_):
                link(ts_(s_, z, 2.0, None, ALU.add))
                link(v.reciprocal(s_, s_))
                link(tt(s_, s_, z, ALU.mult))
                link(tt(s2, s_, s_, ALU.mult))
                link(ts_(p_, s2, 1.0 / 15, None, ALU.mult))
                for c in (13, 11, 9, 7, 5, 3):
                    link(stt(p_, p_, 1.0 / c, s2, ALU.add, ALU.mult))
                link(stt(p_, p_, 1.0, s_, ALU.add, ALU.mult))
                link(ts_(p_, p_, 2.0, None, ALU.mult))

            def before(u):
                dve.wait_ge(scores_done, u + 1)
                if u >= 2:
                    dve.wait_ge(probs_turned, u - 1)
                S_ = score[:, u % 2, :]
                if bias_of(u) is None:
                    ts_(S_, sc[:, u % 2, :], scale_of(u), None, ALU.mult).then_inc(biased, 1)
                else:
                    dve.wait_ge(bias_landed[u % 2], 16 * biased_before(u))
                    stt(S_, sc[:, u % 2, :], scale_of(u), bias[:, u % 2, :], ALU.mult, ALU.add).then_inc(biased, 1)
                dve.wait_ge(biased, u + 1)
                c = 2 * (u % 4)
                ins = v.tensor_reduce(vecs[:, c:c + 2], S_.rearrange("p (m k) -> p m k", m=2), AX, ALU.max, negate=True)
                if kind(u) == "swa":
                    link(ins)
                    j = (u - U_SWA) // 2
                    ins = tt(vecs[:, c:c + 2], vecs[:, c:c + 2], vecs[:, 40 + j:48:4], ALU.min)
                ins.then_inc(max_ready, 1)

            def after(u):
                q, c = u % 2, 2 * (u % 4)
                rr = vecs[:, 16 + c:18 + c]
                dve.wait_ge(probs_ready, u + 1)
                if kind(u) == "swa":
                    link(tt(vecs[:, 8 + c:10 + c], vecs[:, 8 + c:10 + c], vecs[:, 24 + c:26 + c], ALU.add))
                link(v.reciprocal(rr, vecs[:, 8 + c:10 + c]))
                if u < U_X:
                    j = (u // 2) % 4
                    link(tt(rr, rr, ag[:, q, :].rearrange("p (h r) -> p h r", r=3)[:, j::4, 1 + u // 8], ALU.mult))
                elif kind(u) == "diff":
                    link(tt(rr, rr, lbv[:, 38:40], ALU.mult))
                dve.wait_ge(pv_done, u + 1)
                for m in range(2):
                    r_ = rr[:, m:m + 1]
                    if u < U_X:
                        h = (u // 2) % 4 + 4 * m
                        dst = oa[:, q, 64 * h:64 * h + 64]
                        pv_ = pv[:, 64 * m:64 * m + 64]
                        ins = ts_(dst, pv_, r_, None, ALU.mult) if u < 8 else stt(dst, pv_, r_, dst, ALU.mult, ALU.add)
                    elif kind(u) == "diff":
                        h = (u - U_DIFF) // 2
                        dst = ya[:, q, h * P:(h + 1) * P]
                        if m == 0:
                            link(ts_(dst, pv[:, 0:P], r_, None, ALU.mult))
                        else:
                            ins = stt(dst, pv[:, P:2 * P], r_, dst, ALU.mult, ALU.add)
                    elif kind(u) == "swa":
                        h = (u - U_SWA) // 2 + 4 * m
                        ins = ts_(yd[:, q, 64 * h:64 * h + 64], pv[:, 64 * m:64 * m + 64], r_, None, ALU.mult)
                    else:
                        rows, h = (ox, 2 * ((u - U_X) // 2) + m) if kind(u) == "x" else (yc, 2 * ((u - U_FOX) // 2) + m)
                        ins = ts_(rows[:, q, h * P:(h + 1) * P], pv[:, m * P:(m + 1) * P], r_, None, ALU.mult)
                ins.then_inc(pv_used, 1)

            def attend(a, b):
                before(a)
                for u in range(a, b):
                    if u + 1 < b:
                        before(u + 1)
                    if u > a:
                        after(u - 1)
                after(b - 1)
                dve.wait_ge(pv_used, b)

            wait_copied(dve, o_of("cols"))
            tt(lbv[:, 0:4], col("hgrn_lb_logits", 0, 4), col("hgrn_lb_logits", 0, 4), ALU.subtract).then_inc(lb_max, 1)
            dve.wait_ge(lb_exp, 1)
            link(v.reciprocal(lbv[:, 8:12], lbv[:, 4:8]))
            link(tt(lbv[:, 4:8], lbv[:, 4:8], lbv[:, 8:12], ALU.mult))
            link(tt(lbv[:, 8:12], lbv[:, 4:8], lbv[:, 4:8], ALU.subtract))
            link(ts_(lbv[:, 12:16], lbv[:, 8:12], -1.0, 1.0, ALU.mult, ALU.add))

            link(v.memset(cpad[:, :, 0:16], 0.0))
            wait_copied(dve, o_of("b5"))
            attend(U_NSA, U_X)

            wait_copied(dve, o_of("hin", 2))
            wait_copied(dve, o_of("hin", 3))
            for h in range(4):
                own.tick(ts_(hp[:, h, :], hp[:, h, :], lbv[:, 12 + h:13 + h], lbv[:, 8 + h:9 + h], ALU.mult, ALU.add))
            own.done()
            link(ts_(hp, hp, 1e-6, None, ALU.max))
            link(ts_(hk, hp, -1.0, 1.0, ALU.mult, ALU.add))
            link(v.memset(hr, 1.0))
            dve.wait_ge(level_tab_landed, 32)
            flat = lambda ap: ap.rearrange("p h t -> p (h t)")
            for lv in range(HL + 2):
                if lv:
                    wait_part(dve, f"lvl{lv - 1}")
                if lv == 0:
                    own.tick(v.tensor_copy(hqd, hq))
                    v.tensor_copy(hkd, hk).then_inc(level_ready, 1)
                else:
                    own.tick(tt(hqd, hq, hp, ALU.mult))
                    tt(hkd, hk, hr, ALU.mult).then_inc(level_ready, 1)
                if 1 <= lv <= HL:
                    h = 1 << (lv - 1)
                    P4 = flat(hp).rearrange("p (n z h) -> p n z h", z=2, h=h)
                    R4 = flat(hr).rearrange("p (n z h) -> p n z h", z=2, h=h)
                    n = 4 * S // (2 * h)
                    dve.wait_ge(level_ready, lv + 1)
                    link(tt(R4[:, :, 0, :], R4[:, :, 0, :], P4[:, :, 1, h - 1:h].broadcast_to([P, n, h]), ALU.mult))
                    link(tt(P4[:, :, 1, :], P4[:, :, 1, :], P4[:, :, 0, h - 1:h].broadcast_to([P, n, h]), ALU.mult))
                wait_part(dve, f"lvl{lv}")
                o = o_of(f"lvl{lv}")
                b = banks(o).rearrange("p a (h t) -> p (a h) t", h=4)
                if lv > HL:
                    release(v.tensor_copy(ATx, banks(o)[:, 0, :].rearrange("p (h t) -> p h t", h=4)), o)
                    wait_copied(dve, o)
                    continue
                mask = lmask[:, lv, :].unsqueeze(1).broadcast_to([P, 8, P])
                A3, tmp3 = (x.rearrange("p (a t) -> p a t", a=8) for x in (ATd, htmp))
                release(tt(A3 if lv == 0 else tmp3, b, mask, ALU.mult), o)
                wait_copied(dve, o)
                if lv:
                    link(tt(ATd, ATd, htmp, ALU.add))
            v.memset(stats[:, 92:93], 0.0).then_inc(decay_ready, 1)
            wait_copied(dve, o_of("ho"))
            hof = ho.rearrange("p q (h e) -> p (q h) e", h=4)
            tmpf = htmp.rearrange("p (a e) -> p a e", a=8)
            link(tt(tmpf, hof, hof, ALU.mult))
            link(v.tensor_reduce(stats[:, 56:64], tmpf, AX, ALU.add))
            ts_(stats[:, 64:72], stats[:, 56:64], 1.0 / P, LN_EPS, ALU.mult, ALU.add).then_inc(var_ready, 1)
            root(1, 8)
            link(tt(hof, hof, rstd.unsqueeze(2).broadcast_to([P, 8, P]), ALU.mult))
            link(tt(ho, ho, hgrow.unsqueeze(1).broadcast_to([P, NT, 512]), ALU.mult))
            tt(ho, ho, hg, ALU.mult).then_inc(mixer_rows, 1)

            wait_part(dve, "sgw")
            dve.wait_ge(mixer1_landed, 16 * MIXER1_LOADS)
            release(tt(wmT, banks(o_of("sgw"))[:, 0, :].rearrange("p (g t) -> p g t", g=4),
                       tri.unsqueeze(1).broadcast_to([P, 4, P]), ALU.mult), o_of("sgw"))

            wait_copied(dve, o_of("b6"))
            wait_copied(dve, o_of("b7"))
            own.tick(v.memset(ping[:, :, 0:16], 0.0))
            link(v.memset(pong[:, :, 0:16], 0.0))
            src = cpad
            for g, dst in enumerate((ping, pong, ping, pong)):
                w_ = 1 << g
                link(tt(dst[:, g:, 16:], src[:, g:, 16:], src[:, g:, 16 - w_:16 + S - w_], ALU.add))
                src = dst
            for g in range(4):
                own.tick(tt(ping[:, g, 16:], (ping, pong)[g % 2][:, g, 16:], invc[:, g, :], ALU.mult))
            own.done()
            tt(ping[:, :, 16:], ping[:, :, 16:], cpad[:, :, 16:], ALU.subtract).then_inc(mixer_rows, 1)
            wait_part(dve, "pool")
            o = o_of("pool")
            release(tt(brT[:, 8:12, :], banks(o).rearrange("p a (c t) -> p (a c) t", c=2),
                       col("pool_scale", 0, 4).unsqueeze(2).broadcast_to([P, 4, S]), ALU.mult), o)

            wait_copied(dve, o_of("b10"))
            wait_copied(dve, o_of("b11"))
            moments(sv, 512, 2, LN_EPS)
            center(sv, sv)
            link(tt(sv, sv, slg.unsqueeze(1).broadcast_to([P, NT, 512]), ALU.mult))
            tt(sv, sv, slb.unsqueeze(1).broadcast_to([P, NT, 512]), ALU.add).then_inc(mixer_rows, 1)
            wait_part(dve, "sgo")
            o = o_of("sgo")
            for g in range(4):
                gs = slice(g * P, (g + 1) * P)
                ins = stt(su[:, :, gs], banks(o)[:, :, gs], col("sg_b", g), su[:, :, gs], ALU.add, ALU.mult)
                if g == 2:
                    own.tick(ins)
            release(ins, o)
            wait_copied(dve, o)
            v.memset(stats[:, 93:94], 0.0).then_inc(mixer_rows, 1)

            wait_part(dve, "pos")
            o = o_of("pos")
            release(v.tensor_copy(posT.rearrange("p a b -> p (a b)"), banks(o)[:, 0, 0:64]), o)
            wait_copied(dve, o)
            for i in range(2):
                x = kvc[:, i, :].rearrange("p (m b) -> p b m", b=16)
                for a in range(2):
                    ins = tt(win[:, i, 16 * a:16 * a + 16, :], x[:, :, a:a + NC],
                             posT[:, i, 16 * a:16 * a + 16].unsqueeze(2).broadcast_to([P, 16, NC]), ALU.add)
            ins.then_inc(cmp_ready, 1)
            wait_part(dve, "ckv")
            o = o_of("ckv")
            v.tensor_copy(kcmp, banks(o)[:, 0, 0:NC])
            release(v.tensor_copy(vcmp[0:NC, :], banks(o)[0:NC, 1, 0:P]), o)
            wait_part(dve, "cs")
            o = o_of("cs")
            cS2 = cS.rearrange("p (q c) -> p q c", q=NT)
            cS3 = cS.rearrange("p (a c) -> p a c", c=NC)
            release(stt(cS2, banks(o)[:, :, 0:NH * NC], 64 ** -0.5,
                        ctab[:, 0:240].rearrange("p (q c) -> p q c", q=NT), ALU.mult, ALU.add), o)
            wait_copied(dve, o)
            link(v.tensor_reduce(csm[:, 0:16], cS3, AX, ALU.max))
            tt(cS3, cS3, csm[:, 0:16].unsqueeze(2).broadcast_to([P, 16, NC]), ALU.subtract).then_inc(cmp_ready, 1)
            dve.wait_ge(cmp_exp, 1)
            link(v.tensor_reduce(csm[:, 16:32], cS3, AX, ALU.add))
            link(v.reciprocal(csm[:, 32:48], csm[:, 16:32]))
            link(tt(csm[:, 48:64].rearrange("p (q h) -> p q h", q=NT),
                    csm[:, 32:48].rearrange("p (q h) -> p q h", q=NT),
                    ag.rearrange("p q (h r) -> p q h r", r=3)[:, :, :, 0], ALU.mult))
            tt(cS, cS, ctab[:, 240:480], ALU.mult).then_inc(cmp_ready, 1)
            wait_part(dve, "co")
            o = o_of("co")
            release(tt(co_rows.rearrange("p q (h e) -> p (q h) e", e=64),
                       banks(o).rearrange("p q (h e) -> p (q h) e", e=64),
                       csm[:, 48:64].unsqueeze(2).broadcast_to([P, 16, 64]), ALU.mult), o)
            wait_copied(dve, o)
            tt(oa, oa, co_rows, ALU.add).then_inc(mixer_rows, 1)

            def merged(biased_gates, between):
                pairs = lambda ap: ap.rearrange("p (a c) -> p a c", a=2)
                sum_ = pairs(mixS)

                def finish(d, i):
                    b, G = d.b, pairs(gateS[:, d.b % 2, :])
                    if d.ends == "gate" and biased_gates:
                        product(dve, d, i)
                        for x in range(2):
                            bcol = cols[:, 1, bass.ds(i * 2 + (16 * b + x), 1)]
                            ins = ts_(G[:, x, :], banks(d.out)[:, x, 0:S], bcol, None, ALU.add)
                        release(ins, d.out)
                    if d.ends == "y":
                        if biased_gates:
                            reach(dve, gate_ready, b + 1, i, NBR)
                        else:
                            copied(dve, d.out - 1, i, d.per_out)
                        product(dve, d, i)
                        y = sum_ if b == 0 else pairs(yS)
                        release(tt(y, banks(d.out)[:, :, 0:S], G, ALU.mult), d.out)
                        if b:
                            copied(dve, d.out, i, d.per_out)
                            link(tt(mixS, mixS, yS, ALU.add))
                        if b == NBR - 1:
                            hi_, lo = (mixR[:, part, bass.ds(i * 2, 2), :] for part in (0, 1))
                            link(ts_(hi_, sum_, 1.0, None, ALU.mult))
                            tt(lo, sum_, hi_.bitcast(F32), ALU.subtract).then_inc(gate_used, 1)
                    if between:
                        between(d, i)
                return finish

            def merge(name, biased_gates, between=None):
                in_turns(dve, D // W, merge_pieces(name), split, merged(biased_gates, between), own=own, per=4)

            def mem_norm(d, i):
                if not (isinstance(i, int) and i == 0 and d in merge_pieces("merge1")[:NORM_ROOT + 2]):
                    return
                q = merge_pieces("merge1").index(d)
                st = stats[:, 0:48].rearrange("p (q g x) -> p q g x", q=NT, g=4)
                if q < 8:
                    if q == 0:
                        dve.wait_ge(mem_landed, 16)
                    own.tick(v.bn_stats(st[:, q // 4, q % 4, :], xa[:, q // 4, q % 4 * 512:(q % 4 + 1) * 512]))
                elif q == 8:
                    own.done()
                    for a in range(NT):
                        own.tick(v.bn_aggr(mean_var[:, a, :], st[:, a, :, :].rearrange("p g x -> p (g x)")))
                    own.done()
                    ts_(stats[:, 64:66], mean_var[:, :, 1], LN_EPS, None, ALU.add).then_inc(var_ready, 1)
                elif q == NORM_ROOT:
                    root(3, 2)
                    own.tick(ts_(xa[:, 0, :], xa[:, 0, :], mean_var[:, 0, 0:1], rstd[:, 0:1], ALU.subtract, ALU.mult))
                elif q == NORM_ROOT + 1:
                    ts_(xa[:, 1, :], xa[:, 1, :], mean_var[:, 1, 0:1], rstd[:, 1:2], ALU.subtract, ALU.mult)\
                        .then_inc(rows_ready, 1)

            merge_inputs("act1", "br1")
            merge("merge1", False, mem_norm)

            for k in range(4):
                wait_high(at["memT"][3] + k)
                low(brR, mem_tmp[k % 2].rearrange("p (c t) -> p c t", c=4), k).then_inc(lo_ready, 1)
            straight(tile_pieces("xk", 2), split, finish_none)
            straight(tile_pieces("xv", 2), split, finish_none)

            dve.wait_ge(resid_landed, 16)
            square_out("mixout1", ALPHA)
            layer_norm_rows(0, 4, 2)
            turned_low("x1T", mixR)
            straight(tile_pieces("xq", 2), split, finish_none)

            attend(U_X, U_SWA)
            v.memset(stats[:, 88:89], 0.0).then_inc(mixer_rows, 1)
            turned_low("xoT", brR, 1)
            straight(wide_pieces("xo"), split, finish_rows(ALPHA, None))
            wait_copied(dve, o_of("xo", 6))
            wait_copied(dve, o_of("xo", 7))
            layer_norm_rows(1, 5, 3)
            turned_low("x2T", actR)

            link(ts_(xa[:, :, :], xa[:, :, :], ALPHA, None, ALU.mult))
            feed_forward("ff1", True)
            layer_norm_rows(2, 6, 0)

            rms_rows(rowsx, 7, 4)
            scaled_out("xT2", "norm_mix_2")
            link(v.memset(bx[:, :, 0:4], 0.0))
            lam_ = col("lru_lambda_2", 0, 4)
            link(ts_(lbv[:, 24:28], lam_, -1.0, None, ALU.mult))
            tt(lbv[:, 16:20], lbv[:, 24:28], lam_, ALU.min).then_inc(sp_abs, 1)
            wait_copied(dve, o_of("in2", 0))
            wait_copied(dve, o_of("in2", 1))
            for c in range(4):
                own.tick(ts_(xc[:, c, :], bx[:, c, 4:], col("lru_conv_w_2", 12 + c), col("lru_conv_b_2", c),
                             ALU.mult, ALU.add))
            own.done()
            for tap_ in (2, 1, 0):
                for c in range(4):
                    ins = stt(xc[:, c, :], bx[:, c, tap_ + 1:tap_ + 1 + S], col("lru_conv_w_2", 4 * tap_ + c),
                              xc[:, c, :], ALU.mult, ALU.add)
                    if tap_ or c < 3:
                        own.tick(ins)
                if tap_:
                    own.done()
            ins.then_inc(lru_conv, 1)
            dve.wait_ge(lru_conv, 1)
            dve.wait_ge(mixer2_landed, 16 * MIXER2_LOADS)
            for k in range(2):
                own.tick(tt(lrow[:, 128 * k:128 * k + 64], lrow[:, 128 * k:128 * k + 64],
                            lrow[:, 128 * k + 64:128 * k + 128], ALU.mult))
            own.done()
            for k in range(2):
                ins = v.tensor_reduce(lbv[:, 32 + k:33 + k], lrow[:, 128 * k:128 * k + 64], AX, ALU.add)
            ins.then_inc(lam_sum, 1)
            dve.wait_ge(lam_exp, 1)
            link(tt(lbv[:, 36:37], lbv[:, 35:36], lbv[:, 34:35], ALU.subtract))
            link(ts_(lbv[:, 36:37], lbv[:, 36:37], LAM_INIT, None, ALU.subtract))
            link(ts_(lbv[:, 37:38], lbv[:, 36:37], -1.0, None, ALU.mult))
            link(tt(lbv[:, 37:38], lbv[:, 37:38], lbv[:, 36:37], ALU.max))
            link(ts_(lbv[:, 37:38], lbv[:, 37:38], 1.0, None, ALU.max))
            link(v.reciprocal(lbv[:, 38:39], lbv[:, 37:38]))
            link(tt(lbv[:, 39:40], lbv[:, 36:37], lbv[:, 38:39], ALU.mult))
            link(ts_(lbv[:, 37:38], lbv[:, 38:39], RMS_EPS, lbv[:, 38:39], ALU.mult, ALU.mult))
            link(ts_(lbv[:, 37:38], lbv[:, 37:38], 1e-37, None, ALU.max))
            link(ts_(vecs[:, 40:48], sinks, -1.0, None, ALU.mult))
            dve.wait_ge(sp_exp, 1)
            log1p(lbv[:, 20:24], lbv[:, 40:44], lbv[:, 44:48], lbv[:, 48:52])
            link(stt(lbv[:, 24:28], lbv[:, 24:28], 0.0, lbv[:, 48:52], ALU.max, ALU.add))
            link(ts_(lbv[:, 24:28], lbv[:, 24:28], -8.0, None, ALU.mult))
            wait_copied(dve, o_of("lru", 0))
            wait_copied(dve, o_of("lru", 1))
            for c in range(4):
                ins = ts_(lr[:, c, :], lr[:, c, :], lbv[:, 24 + c:25 + c], None, ALU.mult)
            ins.then_inc(lru_arg, 1)
            link(tt(li, li, xc, ALU.mult))
            dve.wait_ge(lru_exp, 1)
            link(ts_(bfree, lt, 1.0, None, ALU.add))
            link(v.reciprocal(bfree, bfree))
            tt(lt, lt, bfree, ALU.mult).then_inc(lru_sq, 1)
            dve.wait_ge(lru_sqrt, 1)
            link(tt(li, li, lt, ALU.mult))
            for c in range(4):
                own.tick(v.tensor_tensor_scan(xc[:, c, :], la[:, c, :], li[:, c, :], 0.0, ALU.mult, ALU.add))
            own.done()
            wait_copied(dve, o_of("in2", 3))
            link(tt(brT[:, 4:8, :], xc, bg, ALU.mult))
            v.memset(stats[:, 89:90], 0.0).then_inc(mixer_rows, 1)
            attend(U_SWA, U_DIFF)

            wait_copied(dve, o_of("in2", 13))
            z4 = cf[0:4, :]
            na, ez, t1, t2, t3 = (ftmp[0:4, k, :] for k in (0, 1, 2, 3, 0))
            link(ts_(z4, z4, bf[0:4, :], None, ALU.add))
            link(ts_(na, z4, -1.0, None, ALU.mult))
            tt(na, na, z4, ALU.min).then_inc(sp_abs, 1)
            dve.wait_ge(sp_exp, 2)
            log1p(ez, t1, t2, t3)
            link(stt(t1, z4, 0.0, t3, ALU.min, ALU.subtract))
            link(v.tensor_tensor_scan(cum[0:4, :], heads[0:4, 4, :], t1, 0.0, ALU.mult, ALU.add))
            link(ts_(ncum[0:4, :], cum[0:4, :], -1.0, None, ALU.mult))
            v.memset(stats[:, 95:96], 0.0).then_inc(mixer_rows, 1)
            attend(U_DIFF, U_FOX)
            attend(U_FOX, U_END)
            dve.wait_ge(probs_turned, U_END)
            yaf = ya.rearrange("p q (h e) -> p (q h) e", h=4)
            sqf = ysq.rearrange("p q (h e) -> p (q h) e", h=4)
            link(tt(sqf, yaf, yaf, ALU.mult))
            link(v.tensor_reduce(stats[:, 56:64], sqf, AX, ALU.add))
            ts_(stats[:, 64:72], stats[:, 56:64], 1.0 / P, lbv[:, 37:38], ALU.mult, ALU.add).then_inc(var_ready, 1)
            root(8, 8)
            link(tt(yaf, yaf, rstd.unsqueeze(2).broadcast_to([P, 8, P]), ALU.mult))
            link(tt(yaf, yaf, subln.unsqueeze(1).broadcast_to([P, 8, P]), ALU.mult))
            ts_(ya, ya, 1.0 - LAM_INIT, None, ALU.mult).then_inc(mixer_rows, 1)
            merge_inputs("act2", "br2")
            merge("merge2", True)
            square_out("mixout2", None)
            rms_rows(rowsx, 9, 5)

            def weighted(k):
                o = o_of("x3T", k)
                if k >= 2:
                    dve.wait_ge(lo_ready, at["x3T"][3] + k - 1)
                wait_part(dve, "x3T", k)
                release(tt(turn_tmp[k % 2].rearrange("p (c t) -> p c t", c=4),
                           banks(o).rearrange("p a (c t) -> p (a c) t", c=2),
                           col("norm_ffn_2", 4 * k, 4).unsqueeze(2).broadcast_to([P, 4, S]), ALU.mult), o)

            weighted(0)
            for k in range(4):
                if k < 3:
                    weighted(k + 1)
                wait_high(at["x3T"][3] + k)
                low(mixR, turn_tmp[k % 2].rearrange("p (c t) -> p c t", c=4), k).then_inc(lo_ready, 1)
            feed_forward("ff2", False)
            moments(xa, D, 10, RMS_EPS, rms=True)
            for q in range(NT):
                own.tick(ts_(xa[:, q, :], xa[:, q, :], rstd[:, q:q + 1], None, ALU.mult))
            own.done()
            dve.wait_ge(norm_rows_landed, 32 * 4)
            tt(xa[:, :, :], xa[:, :, :], lng[3].unsqueeze(1).broadcast_to([P, NT, D]), ALU.mult).then_inc(rows_ready, 1)


def laid_out(x):
    r = lambda name, *shape: x[name].reshape(*shape)
    stacked = {name: r(name, -1, P) for st in STACKS for name, _ in st if not name.startswith("conv_w")}
    taps = r("ffn_conv_w", 3 * FC, P)
    stacked["conv_w_01"], stacked["conv_w_2"] = taps[:2 * FC], taps[2 * FC:]
    return stacked | {
        "x": r("x", S, D), "mem": r("mem", S, D), "w_in": r("w_in", D, -1), "w_in_2": r("w_in_2", D, -1),
        "nsa_cmp_pos": r("nsa_cmp_pos", 64, 64), "nsa_cmp_w": r("nsa_cmp_w", 2, 32, 64, 64),
        "hgrn_norm_g": r("hgrn_norm_g", -1), "pool_w": r("pool_w", 4, P, P),
        "sg_ln_g": r("sg_ln_g", -1), "sg_ln_b": r("sg_ln_b", -1), "sg_w": r("sg_w", 4, P, P),
        "w_branch": r("w_branch", D, D), "w_branch_2": r("w_branch_2", D, D),
        "w_mix_out": r("w_mix_out", D, D), "w_out_2": r("w_out_2", D, D),
        "ln_mix_g": r("ln_mix_g", -1), "ln_mix_b": r("ln_mix_b", -1), "ln_x_g": r("ln_x_g", -1),
        "ln_x_b": r("ln_x_b", -1), "ln_ffn_g": r("ln_ffn_g", -1), "ln_ffn_b": r("ln_ffn_b", -1),
        "xattn_q": r("xattn_q", D, -1), "xattn_k": r("xattn_k", D, -1), "xattn_v": r("xattn_v", D, -1),
        "xattn_o": r("xattn_o", -1, D), "ffn_in": r("ffn_in", D, -1), "ffn_out": r("ffn_out", -1, D),
        "diff_lq1_2": r("diff_lq1_2", -1), "diff_lk1_2": r("diff_lk1_2", -1),
        "diff_lq2_2": r("diff_lq2_2", -1), "diff_lk2_2": r("diff_lk2_2", -1),
        "diff_subln_2": r("diff_subln_2", -1), "lru_wa_2": r("lru_wa_2", 8, 64, 64),
        "lru_wx_2": r("lru_wx_2", 8, 64, 64), "fox_b_f_2": r("fox_b_f_2", -1),
        "swa_sinks_2": r("swa_sinks_2", -1), "w_ffn_gate_2": r("w_ffn_gate_2", D, -1),
        "w_ffn_up_2": r("w_ffn_up_2", D, -1), "w_ffn_down_2": r("w_ffn_down_2", -1, D),
        "norm_final_2": r("norm_final_2", -1),
    }


def kernel(**inputs):
    import concourse.bacc as _bacc
    from concourse.bass_utils import run_bass_kernel_spmd as _run

    nc = _bacc.Bacc("TRN2", target_bir_lowering=False, num_devices=1)
    arrays = {k: np.ascontiguousarray(a) for k, a in laid_out({k: np.asarray(a) for k, a in inputs.items()}).items()}
    arrays.update(shape_tables())
    arrays = {f"in_{k}": a for k, a in arrays.items()}
    t = {k[3:]: nc.dram_tensor(k, a.shape, F32, kind="ExternalInput").ap() for k, a in arrays.items()}
    out = nc.dram_tensor("out", (S, D), F32, kind="ExternalOutput").ap()
    two_layer_block_kernel(nc, t, out)
    r = _run(nc, [arrays], core_ids=[0])
    return r.results[0]["out"].reshape(1, S, D)
```

```python
from collections import namedtuple
from contextlib import ExitStack
import math

import numpy as np
import concourse.bass as bass
from concourse import mybir

P = 128
S = 256
NT = S // P
D = 2048
KC = D // P
MIX = 512
NBR = 4
FF = 5632
FC = FF // P
W = 256
SLOTS = 2
LANDED = 64
U = 4 * W
PIECES = 4
GROUPS = FC // 4
NORM_ROOT = 11
LAG = 2
NH = 8
NJ = NH // 2
NC = (S - 32) // 16 + 1
NEG = -1e30
MIXER2_LOADS = 8
ALPHA = 2.0 ** 0.25
LN_EPS = 1e-5
RMS_EPS = 1e-6
HL = 7
LAM_INIT = 0.8 - 0.6 * math.exp(0.0)

A_Q, A_KV, A_G, B_IN, C_IN, D_IN, MERGE = 0, 512, 1280, 1304, 3352, 3864, 4888
AQ2, AK2, AV2, BX2, BG2, CQ2, CK2, CV2, CF2, DQ2, DKV2, GZ2 = (
    0, 512, 1024, 1536, 2048, 2560, 3072, 3584, 4096, 4100, 4612, 4868)

ALU = mybir.AluOpType
ACT = mybir.ActivationFunctionType
F32 = mybir.dt.float32
F32R = mybir.dt.float32r
AX = mybir.AxisListType.X

STACKS = (
    (("mem_ln_g", 16), ("mem_ln_b", 16), ("norm_mix_2", 16), ("norm_ffn_2", 16), ("pool_scale", 4),
     ("hgrn_lb_logits", 4), ("lru_conv_w_2", 16), ("lru_conv_b_2", 4), ("lru_ba_2", 4), ("lru_bx_2", 4),
     ("lru_lambda_2", 4), ("sg_b", 4)),
    (("b_gate_2", 64), ("ffn_conv_b", FC)),
    (("conv_w_01", 2 * FC),),
    (("conv_w_2", FC),),
)

BIAS_NSA, BIAS_SWA, BIAS_DIFF, BIAS_FOX = 0, 8, 16, 24
T_LEVEL, T_TRI, T_COUNT, T_CBIAS, T_CMASK, T_HEAD, T_ONES = 0, 1024, 1152, 2176, 2416, 2656, 3680
T_END = 3936


def shape_tables():
    t = np.arange(S)[:, None]
    k = np.arange(S)[None, :]
    dist = (t - k).astype(np.float32)
    causal = dist >= 0
    window = causal & (dist < P)

    def table(slopes, mask):
        maps = [np.where(mask, -np.float32(s) * dist, np.float32(NEG)) for s in slopes]
        both = np.concatenate(maps, axis=1)
        return [both[q * P:(q + 1) * P] for q in range(NT)]

    bias = []
    for mask in (causal, window):
        for j in range(NJ):
            bias += table((2.0 ** -(j + 1), 2.0 ** -(j + 5)), mask)
    for h in range(4):
        bias += table((2.0 ** -(2 * (h + 1)),) * 2, causal)
    bias += table((0.0, 0.0), causal)

    small = np.zeros((P, T_END), np.float32)
    s_, t_ = np.arange(P)[:, None], np.arange(P)[None, :]
    small[:, T_LEVEL:T_LEVEL + P] = s_ == t_
    for lv in range(HL):
        h = 1 << lv
        same = s_ // (2 * h) == t_ // (2 * h)
        small[:, T_LEVEL + (lv + 1) * P:T_LEVEL + (lv + 2) * P] = same & (s_ // h % 2 == 0) & (t_ // h % 2 == 1)
    small[:, T_TRI:T_TRI + P] = s_ <= t_
    for g, win in enumerate((2, 4, 8, 16)):
        small[:, T_COUNT + g * S:T_COUNT + (g + 1) * S] = 1.0 / np.minimum(np.arange(S) + 1, win)
    end = np.arange(NC) * 16 + 31
    for q in range(NT):
        d = ((np.arange(P) + q * P)[:, None] - end[None, :]).astype(np.float32)
        for h in range(NH):
            at = (q * NH + h) * NC
            small[:, T_CBIAS + at:T_CBIAS + at + NC] = np.where(d >= 0, -np.float32(2.0 ** -(h + 1)) * d, NEG)
            small[:, T_CMASK + at:T_CMASK + at + NC] = d >= 0
    for h in range(4):
        small[h, T_HEAD + h * S:T_HEAD + (h + 1) * S] = 1.0
    small[:, T_ONES:T_ONES + S] = 1.0
    return {"t_ident": np.eye(P, dtype=np.float32), "t_bias": np.stack(bias).astype(np.float32), "t_small": small}


Piece = namedtuple("Piece", "tile k wide split piece out ends b x c hid per_tile per_piece per_out w",
                   defaults=(None, 0, 0, 0, None, 0, 0, 0, W))


class Plan:

    def __init__(self):
        self.tile, self.part, self.out, self.split, self.piece = 0, 0, 0, 0, 0
        self.at, self.freed = {}, []

    def add(self, name, parts=0, outs=0, splits=0):
        self.at[name] = (self.tile, self.part, self.out, self.split, self.piece)
        self.part += parts
        self.out += outs
        self.split += splits

    def add_split(self, name, tiles, outs, times=1):
        self.at[name] = (self.tile, self.part, self.out, self.split, self.piece)
        for n in tiles * times:
            self.tile += 1
            self.split += n
            self.piece += n
            self.freed.append(self.split)
        self.out += outs * times


class Count:

    def __init__(self, eng, sem):
        self.eng, self.sem, self.n, self.i, self.per = eng, sem, 0, None, 0

    def tick(self, ins):
        ins.then_inc(self.sem, 1)
        self.n += 1
        return ins

    def value(self):
        return self.n if self.i is None else self.i * self.per + self.n

    def done(self):
        self.eng.wait_ge(self.sem, self.value())

    def link(self, ins):
        self.tick(ins)
        self.done()

    def enter(self, i, per, start=0):
        self.n -= start * per
        self.i, self.per, self.n0 = i, per, self.n

    def leave(self, times):
        assert self.n - self.n0 == self.per, (self.n, self.n0, self.per)
        self.n = self.n0 + self.per * times
        self.i = None


def two_layer_block_kernel(nc, t, out):
    pl = Plan()
    add = pl.add
    add("xT1", parts=4, outs=4, splits=4)
    for n in range(6):
        pl.add_split(f"b{n}", [4], 1)
        if n == 1:
            add("cols", parts=1, outs=1)
    pl.add_split("hin", [4] * 8, 8)
    pl.add_split("b6", [4], 1)
    B_AFTER = (1, 1, 1, 1, 1, 0, 0, 0, 0)
    n = 7
    for lv, k in enumerate(B_AFTER):
        add(f"lvl{lv}", parts=1, outs=1)
        for _ in range(k):
            pl.add_split(f"b{n}", [4], 1)
            n += 1
    add("ho", parts=1, outs=1)
    add("hT", parts=1, outs=1)
    add("sgw", parts=1, outs=1)
    add("pool", parts=1, outs=1)
    add("sgo", parts=1, outs=1)
    add("sgT", parts=1, outs=1)
    add("pos", parts=1, outs=1)
    add("ckv", parts=1, outs=1)
    add("cs", parts=1, outs=1)
    add("cT", parts=2, outs=2)
    add("co", parts=1, outs=1)
    add("nT", parts=1, outs=1)
    add("br1", splits=4)
    pl.add_split("merge1", [5] * 4, 8, D // W)
    add("memT", parts=4, outs=4, splits=4)
    pl.add_split("xk", [4] * 2, 2)
    pl.add_split("xv", [4] * 2, 2)
    pl.add_split("mixout1", [4] * 8, 8)
    add("x1T", parts=4, outs=4, splits=4)
    pl.add_split("xq", [4] * 2, 2)
    add("xoT", parts=1, outs=1, splits=1)
    pl.add_split("xo", [4] * 2, 8)
    add("x2T", parts=4, outs=4, splits=4)
    pl.add_split("ff1", [4] * 4, 4)
    pl.add_split("ff1loop", [4] * 12, 24, (GROUPS - 1) // 2)
    pl.add_split("ff1end", [4] * 2, 8)
    add("xT2", parts=4, outs=4, splits=4)
    pl.add_split("in2", [4] * 7, 7)
    add("lru", parts=2, outs=2)
    pl.add_split("in2b", [4] * 13, 13)
    add("y0T", parts=1, outs=1)
    add("y2T", parts=1, outs=1)
    add("y3T", parts=1, outs=1)
    add("br2", splits=4)
    pl.add_split("merge2", [5] * 4, 8, D // W)
    pl.add_split("mixout2", [4] * 8, 8)
    add("x3T", parts=4, outs=4, splits=4)
    pl.add_split("ff2", [4] * 4, 4)
    pl.add_split("ff2loop", [4] * 12, 24, (GROUPS - 1) // 2)
    pl.add_split("ff2end", [4] * 2, 8)
    at = pl.at

    U_NSA, U_X, U_SWA, U_DIFF, U_FOX, U_END = 0, 16, 20, 28, 36, 40

    def kind(u):
        return ("nsa", "x", "swa", "diff", "fox")[sum(u >= a for a in (U_X, U_SWA, U_DIFF, U_FOX))]

    def bias_of(u):
        if kind(u) == "nsa":
            return BIAS_NSA + (u // 2) % 4 * 2 + u % 2
        return {"x": None, "swa": BIAS_SWA + u - U_SWA, "diff": BIAS_DIFF + u - U_DIFF, "fox": BIAS_FOX + u % 2}[kind(u)]

    BEHIND_HALVES = {"hin": [(U_NSA, U_X, 0)], "in2": [(U_SWA, U_DIFF, 9), (U_DIFF, U_FOX, 14)]}

    def groups_at(name, k):
        return [(a, b) for a, b, first in BEHIND_HALVES[name] if first == k]

    def unit_behind(name, k, half):
        for a, b, first in BEHIND_HALVES[name]:
            u = a + 2 * (k - first) + half
            if a <= u < b:
                return [(u, a, b)]
        return []

    def biased_before(u):
        return len([v for v in range(u % 2, u + 1, 2) if bias_of(v) is not None])

    with ExitStack() as ctx:
        def sb(name, shape):
            return ctx.enter_context(nc.sbuf_tensor(name, shape, F32))

        def sem(name):
            return ctx.enter_context(nc.semaphore(name))

        ring = sb("ring", [P, SLOTS, 20 * W])
        whi = ctx.enter_context(nc.sbuf_tensor("whi", [P, PIECES, U], F32R))
        wlo = ctx.enter_context(nc.sbuf_tensor("wlo", [P, PIECES, U], F32R))
        xa = sb("xa", [P, NT, D])
        A_BR, A_MIX, A_ACT = (1024 + i * 2 * KC * S for i in range(3))
        shared = ExitStack()
        arena = shared.enter_context(nc.sbuf_tensor("arena", [P, A_ACT + 2 * KC * S], F32))
        shared.close()
        sb("arena_head", [P, A_BR])
        brR, mixR, actR = (ctx.enter_context(nc.sbuf_tensor(n, [P, 2, KC, S], F32R)) for n in ("brR", "mixR", "actR"))
        ident = sb("ident", [P, P])
        bias = sb("bias", [P, 2, 512])
        score = sb("score", [P, 2, 512])
        probT = sb("probT", [P, 2, 512])
        cols = sb("cols", [P, 4, P])
        stats = sb("stats", [P, 100])
        vecs = sb("vecs", [P, 96])
        lbv = sb("lbv", [P, 64])
        acc = ctx.enter_context(nc.psum_tensor("acc", [P, 4, 512], F32))
        sc = ctx.enter_context(nc.psum_tensor("sc", [P, 2, 512], F32))
        pt = ctx.enter_context(nc.psum_tensor("pt", [P, 512], F32))
        pv = ctx.enter_context(nc.psum_tensor("pv", [P, 512], F32))

        def place(off):
            return off - 4096 if off >= 4096 else A_ACT - 4096 + off

        def piece(off, n):
            return arena[:, place(off):place(off) + n]

        def cut(off, a, b):
            return piece(off, a * b).rearrange("p (a b) -> p a b", a=a)

        xaf = xa[:, :, :].rearrange("p a b -> p (a b)")
        def tail(s_):
            return ring[:, s_, 16 * W:20 * W]

        brT = cut(0, KC, S)
        rowsx = cut(4096, NT, D)
        hq, hp, hk, hr, hqd, hkd = (cut(4096 + i * 1024, 4, S) for i in range(6))
        hi, hg = cut(10240, NT, 512), cut(11264, NT, 512)
        ATd, ATx = piece(12288, 1024), cut(13312, 4, P)
        lmask = cut(13824, 8, P)
        hgrow = piece(14848, 512)
        ho, htmp = cut(15360, NT, 512), piece(16384, 1024)
        xapart = lambda off, a, b: xaf[:, off:off + a * b].rearrange("p (a b) -> p a b", a=a)
        qn = xapart(0, NJ, S)
        kvc, kvs, kvw = (xapart(1024 + i * 512, 2, S) for i in range(3))
        ag = xapart(2560, NT, 24)
        cpad = xapart(2624, 4, 16 + S)
        su, sv = (tail(i).rearrange("p (a b) -> p a b", a=NT) for i in range(2))
        cw = piece(4096, 4096).rearrange("p (i l e) -> p i l e", i=2, l=32)
        posT = cut(8192, 2, 32)
        win = piece(8256, 960).rearrange("p (i l c) -> p i l c", i=2, l=32)
        kcmp, vcmp = piece(9216, NC), piece(9232, P)
        oa = cut(0, NT, 512)
        co_rows = cut(4096, NT, 512)
        ctab = piece(10400, 480)
        cS = piece(10880, 240)
        csm = piece(11120, 160)
        ping, pong = cut(11280, 4, 16 + S), cut(12368, 4, 16 + S)
        cPT = cut(11280, NT * NH, P)
        invc = cut(13456, 4, S)
        poolw = cut(14480, 4, P)
        sgrow, wmT = cut(9632, 4, P), cut(15504, 4, P)
        slg, slb = piece(16016, 512), piece(16528, 512)
        posrow = piece(9376, P)
        tri = piece(9504, P)
        def at_(off, a, b):
            return arena[:, off:off + a * b].rearrange("p (a b) -> p a b", a=a)

        kx, vx = at_(A_ACT, 4, S), at_(A_ACT + 1024, NT, 512)
        lng = [arena[:, o:o + D] for o in (A_ACT + 2048, A_BR + 1024, A_MIX, A_ACT)]
        lnb = [arena[:, o:o + D] for o in (A_ACT + 4096, A_BR + 5120, A_MIX + D)]
        qx, ox = at_(A_ACT + 6144, 4, S), at_(A_ACT + 7168, NT, 512)
        mem_tmp = [arena[:, A_ACT + 4096 + i * U:A_ACT + 4096 + (i + 1) * U] for i in range(2)]
        hidR = lambda par, part: brR[:, part, 4 * par:4 * par + 4, :]
        convS, siluS = at_(A_BR + 2048, 2, 512), at_(A_BR + 3072, 2, 512)
        aq, ak = (tail(i).rearrange("p (a b) -> p a b", a=4) for i in range(2))
        av, cq, ck, cv = cut(4096, NT, 512), cut(5120, 4, S), cut(6144, 4, S), cut(7168, NT, 512)
        dq, dkv = cut(8192, NJ, S), cut(9216, 2, S)
        cf, cum, ncum = piece(9728, S), piece(9984, S), piece(10240, S)
        bg = cut(10496, 4, S)
        bx = cut(11520, 4, 4 + S)
        bfree = cut(11520, 4, S)
        ftmp = bfree
        xc, lr, li = (cut(12560 + i * 1024, 4, S) for i in range(3))
        lt = score[:, :, :].rearrange("p a (b c) -> p (a b) c", b=2)
        la = probT[:, :, :].rearrange("p a (b c) -> p (a b) c", b=2)
        wl = score[:, :, :].rearrange("p i (c d) -> p i c d", c=4)
        ya, yc, yd = (cut(12560 + i * 1024, NT, 512) for i in range(3))
        lrow = piece(15632, 256)
        sinks = piece(15888, NH)
        subln = piece(15904, P)
        heads = piece(16032, 1280).rearrange("p (h c) -> p h c", h=5)
        bf = piece(17320, 1)
        ysq = bfree.rearrange("p c t -> p (c t)")
        gateS, yS, mixS = score[:, :, :], probT[:, 0, :], probT[:, 1, :]
        turn_tmp = [score[:, :, :].rearrange("p a b -> p (a b)"), probT[:, :, :].rearrange("p a b -> p (a b)")]

        def stack_rows(i):
            return piece(i * P, P)

        def col(name, k=0, n=1):
            for i, st in enumerate(STACKS):
                r = 0
                for nm, rows in st:
                    if nm == name:
                        return cols[:, i, r + k:r + k + n]
                    r += rows
            raise KeyError(name)

        w_landed = [sem(f"w_landed{i}") for i in range(SLOTS)]
        piece_used = sem("piece_used")
        hi_ready = sem("hi_ready")
        lo_ready = sem("lo_ready")
        hid_hi = sem("hid_hi")
        hid_lo = sem("hid_lo")
        part_done = sem("part_done")
        acc_free = [sem("acc_free0"), sem("acc_free1")]
        ident_landed = sem("ident_landed")
        stack_landed = sem("stack_landed")
        x_landed = sem("x_landed")
        level_tab_landed = sem("level_tab_landed")
        weights1_landed = sem("weights1_landed")
        tables1_landed = sem("tables1_landed")
        mixer1_landed = sem("mixer1_landed")
        mixer2_landed = sem("mixer2_landed")
        lru_zeroed = sem("lru_zeroed")
        lru_landed = sem("lru_landed")
        mem_landed = sem("mem_landed")
        resid_landed = sem("resid_landed")
        norm_rows_landed = sem("norm_rows_landed")
        bias_landed = [sem("bias_landed0"), sem("bias_landed1")]
        out_landed = sem("out_landed")
        pe_rows = sem("pe_rows")
        v_link = sem("vector_link")
        s_link = sem("scalar_link")
        rows_ready = sem("rows_ready")
        norm_done = sem("norm_done")
        var_ready = sem("var_ready")
        std_ready = sem("std_ready")
        lb_max = sem("lb_max")
        lb_exp = sem("lb_exp")
        level_ready = sem("level_ready")
        decay_ready = sem("decay_ready")
        ho_copied = sem("ho_copied")
        mixer_rows = sem("mixer_rows")
        cmp_ready = sem("cmp_ready")
        cmp_exp = sem("cmp_exp")
        gate_ready = sem("gate_ready")
        gate_used = sem("gate_used")
        silu_ready = sem("silu_ready")
        scores_done = sem("scores_done")
        biased = sem("biased")
        max_ready = sem("max_ready")
        probs_ready = sem("probs_ready")
        probs_turned = sem("probs_turned")
        probT_ready = sem("probT_ready")
        pv_done = sem("pv_done")
        pv_used = sem("pv_used")
        lru_conv = sem("lru_conv")
        lru_sig = sem("lru_sig")
        lru_arg = sem("lru_arg")
        lru_exp = sem("lru_exp")
        lru_sq = sem("lru_sq")
        lru_sqrt = sem("lru_sqrt")
        gelu_ready = sem("gelu_ready")
        sp_abs = sem("softplus_abs")
        sp_exp = sem("softplus_exp")
        lam_sum = sem("lam_sum")
        lam_exp = sem("lam_exp")
        sub_sq = sem("sub_sq")

        def wait_part(eng, name, k=0):
            eng.wait_ge(part_done, at[name][1] + k + 1)

        def reach(eng, semaphore, n, i=None, per=0):
            eng.wait_ge(semaphore, n if i is None else i * per + n)

        ROWS_BEFORE = {"memT": 0, "x1T": 1, "x2T": 5, "xT2": 9, "x3T": 13, "out": 17}

        def wait_rows(eng, name, k=0):
            eng.wait_ge(rows_ready, ROWS_BEFORE[name] + k + 1)

        def o_of(name, k=0):
            return at[name][2] + k + (2 if name == "in2" and k >= 7 else 0)

        def banks(o):
            return acc[:, 2 * (o % 2):2 * (o % 2) + 2, :]

        def wait_bank(o, i=None, per=0):
            if o >= 2:
                nc.tensor.wait_ge(acc_free[o % 2], o // 2 if i is None else i * (per // 2) + o // 2)

        def wait_copied(eng, o):
            eng.wait_ge(acc_free[o % 2], o // 2 + 1)

        def release(ins, o):
            ins.then_inc(acc_free[o % 2], 1)

        hid0 = {"ff1": 0, "ff2": GROUPS}

        def copied(eng, o, i, per):
            reach(eng, acc_free[o % 2], o // 2 + 1, i, per // 2)

        def product(eng, d, i):
            reach(eng, piece_used, d.piece + 1, i, d.per_piece)

        def raw(d):
            if d.wide:
                return ring[:, d.tile % SLOTS, 0:16 * W].rearrange("p (k c) -> p k c", k=4)[:, :, d.k * W:(d.k + 1) * W]
            return ring[:, d.tile % SLOTS, d.k * 4 * d.w:(d.k + 1) * 4 * d.w].rearrange("p (k c) -> p k c", k=4)

        def part_of_piece(w, d):
            return w[:, d.piece % PIECES, 0:4 * d.w].rearrange("p (k c) -> p k c", k=4)

        def width(name, k):
            return {("in2", 13): 4}.get((name, k), W)

        def projection_pieces(name, k=0):
            n, _, _, s_, p_ = at[name]
            return [Piece(n + k, q, False, s_ + 4 * k + q, p_ + 4 * k + q, o_of(name, k), "tile" if q == 3 else None,
                          b=(name, k), w=width(name, k)) for q in range(4)]

        def units_behind(d):
            return unit_behind(*d.b, d.k // 2) if d.b[0] in BEHIND_HALVES and d.k % 2 else []

        BLOCK1_TILES = [(f"b{k}", 0) for k in range(6)] + [("hin", k) for k in range(8)] + [("b6", 0)]

        def tile_pieces(name, tiles, turns=1):
            n, _, o, s_, p_ = at[name]
            m = tiles // turns
            return [Piece(n + c, k, False, s_ + 4 * c + k, p_ + 4 * c + k, o + c, "rows" if k == 3 else None,
                          c=c, per_tile=m, per_piece=4 * m, per_out=m) for c in range(m) for k in range(4)]

        def wide_pieces(name, x0=0):
            n, _, o, s_, p_ = at[name]
            return [Piece(n + x, k, True, s_ + 4 * x + k, p_ + 4 * x + k, o + 4 * x + k, "rows", c=4 * x + k)
                    for x in range(2) for k in range(4)]

        def merge_pieces(name):
            n, _, o, s_, p_ = at[name]
            ends = (None, None, None, "gate", "y")
            return [Piece(n + b, k, False, s_ + 5 * b + k, p_ + 5 * b + k, o + 2 * b + (k == 4), ends[k], b=b,
                          per_tile=4, per_piece=20, per_out=8) for b in range(NBR) for k in range(5)]

        def hidden(name, g, x, o, loop):
            per = (4, 8, 24) if loop else (0, 0, 0)
            return dict(h=2 * (hid0[name] + g) + x, x=x, par=g % 2, og=o, ou=o + 1, chunk=4 * g + 2 * x,
                        per_h=per[0], per_chunk=per[1], per_out=per[2])

        def ff_pieces(name):
            def gate_up(n, s_, p_, o, hd, steps, **kw):
                both = []
                for k in range(8):
                    hid = {3: ("gate", hd), 4: ("silu", hd), 7: ("up", hd)}.get(k, steps.get(k))
                    both.append(Piece(n + k // 4, k % 4, False, s_ + k, p_ + k, o + k // 4, None, hid=hid, **kw))
                return both

            n, _, o, s_, p_ = at[name]
            first = [hidden(name, 0, x, o + 2 * x, False) for x in range(2)]
            before = gate_up(n, s_, p_, o, first[0], {})
            before += gate_up(n + 2, s_ + 8, p_ + 8, o + 2, first[1], {0: ("hi", first[0]), 1: ("lo", first[0])})
            n, _, o, s_, p_ = at[name + "loop"]
            kw = dict(per_tile=12, per_piece=48, per_out=24)
            turn_ = []
            for z in range(2):
                for x in range(2):
                    a, d, e = 6 * z + 3 * x, 24 * z + 12 * x, 12 * z + 6 * x
                    hd = hidden(name, z + 1, x, o + e, True)
                    turn_ += gate_up(n + a, s_ + d, p_ + d, o + e, hd, {}, **kw)
                    turn_ += [Piece(n + a + 2, k, True, s_ + d + 8 + k, p_ + d + 8 + k, o + e + 2 + k, "rows",
                                    c=4 * x + k, hid={0: ("hi", hd), 1: ("lo", hd)}.get(k), **kw) for k in range(4)]
            return first, before, turn_, wide_pieces(name + "end")

        def step_through(pieces, split, finish, earlier=()):
            for q, (d, i) in enumerate(pieces):
                split(d, i)
                if q >= LAG:
                    finish(*pieces[q - LAG])
                elif earlier:
                    finish(*earlier[q - LAG])

        def straight(pieces, split, finish):
            pieces = [(d, 0) for d in pieces]
            step_through(pieces, split, finish)
            for d in pieces[-LAG:]:
                finish(*d)

        def in_turns(eng, times, turn_, split, finish, behind=(), own=None, per=0):
            step_through([(d, 0) for d in turn_], split, finish)
            with eng.Fori(1, times) as i:
                if own:
                    own.enter(i, per, 1)
                step_through([(d, i) for d in turn_], split, finish, [(d, i - 1) for d in turn_[-LAG:]])
                if own:
                    own.leave(times)
            rest = [(d, times - 1) for d in turn_[-LAG:]]
            if behind:
                step_through([(d, 0) for d in behind], split, finish, rest)
                rest = [(d, 0) for d in behind[-LAG:]]
            for d in rest:
                finish(*d)

        def unit(u):
            q_ = u % 2
            qs = slice(q_ * P, (q_ + 1) * P)
            if kind(u) in ("nsa", "swa"):
                j = (u - U_SWA) // 2 if kind(u) == "swa" else (u // 2) % 4
                kv_, qq = (dkv, dq) if kind(u) == "swa" else ((kvs, kvw)[u // 8], qn)
                half = lambda m: slice(64 * m, 64 * m + 64)
                return (lambda m: qq[half(m), j, qs], lambda m: kv_[half(m), 0, :], lambda m: [],
                        lambda m, kt: kv_[:, 1, kt * P + 64 * m:kt * P + 64 * m + 64], 64)
            if kind(u) == "x":
                p_ = (u - U_X) // 2
                return (lambda m: qx[:, 2 * p_ + m, qs], lambda m: kx[:, 2 * p_ + m, :], lambda m: [],
                        lambda m, kt: vx[:, kt, (2 * p_ + m) * P:(2 * p_ + m + 1) * P], P)
            if kind(u) == "diff":
                h = (u - U_DIFF) // 2
                half = lambda m: slice(64 * m, 64 * m + 64)
                return (lambda m: aq[half(m), h, qs], lambda m: ak[half(m), h, :], lambda m: [],
                        lambda m, kt: av[:, kt, h * P:(h + 1) * P], P)
            p_ = (u - U_FOX) // 2
            return (lambda m: cq[:, 2 * p_ + m, qs], lambda m: ck[:, 2 * p_ + m, :],
                    lambda m: [(cum[0:4, qs], heads[0:4, 2 * p_ + m, :]),
                               (heads[0:4, 2 * p_ + m, 0:P], ncum[0:4, :])],
                    lambda m, kt: cv[:, kt, (2 * p_ + m) * P:(2 * p_ + m + 1) * P], P)

        def scale_of(u):
            return {"fox": 1.0, "x": 128 ** -0.5}.get(kind(u), 64 ** -0.5)

        block = ctx.enter_context(nc.Block())

        @block.sync
        def _(sp):
            kp = lambda ap: ap.rearrange("(k p) c -> p k c", p=P)
            w_in, w_in2 = kp(t["w_in"]), kp(t["w_in_2"])

            def slot(n, k, w, off=0):
                return ring[:, n % SLOTS, off:off + k * w].rearrange("p (k c) -> p k c", k=k)

            def load(n, pieces, i=None, per=0, splits=0):
                if n >= SLOTS:
                    v = pl.freed[n - SLOTS + (per if i is not None else 0)]
                    reach(sp, lo_ready, v - splits if i is not None else v, i, splits)
                for dst, src in pieces:
                    sp.dma_start(dst, src).then_inc(w_landed[n % SLOTS], LANDED // len(pieces))

            def turns(times, turn):
                turn(0, None)
                with sp.Fori(1, times) as i:
                    turn(i, i)

            def plain(n, w, c, **kw):
                load(n, [(slot(n, KC, W), w[:, :, bass.ds(c, W)])], **kw)

            def paired(n, w, c):
                s_ = slot(n, KC, W)
                load(n, [(s_[:, :, y * P + g * 64:y * P + g * 64 + 64],
                          w[:, :, c + g * 256 + y * 64:c + g * 256 + y * 64 + 64])
                         for y in range(2) for g in range(2)])

            def cols_at(ap, c, w=W):
                return ap[:, :, c:c + w] if isinstance(c, int) else ap[:, :, bass.ds(c, w)]

            def merge_tiles(n0, w, c0, wbr):
                def turn(c, i):
                    for b in range(NBR):
                        load(n0 + b, [(slot(n0 + b, KC, W), cols_at(w, c * W + (c0 + b * D))),
                                      (slot(n0 + b, 4, W, KC * W), cols_at(wbr[:, 4 * b:4 * b + 4, :], c * W))],
                             i, 4, 20)
                turns(D // W, turn)

            def square_tiles(n0, w):
                for k in range(8):
                    load(n0 + k, [(slot(n0 + k, KC, W), w[:, :, k * W:(k + 1) * W])])

            def ff_tiles(name, gate, up, g0, u0, down):
                def gate_up(n, g, x, i):
                    for k, (w, c0) in enumerate(((gate, g0), (up, u0))):
                        load(n + k, [(slot(n + k, KC, W), cols_at(w, g * (2 * W) + (c0 + x * W)))], i, 12, 48)

                def down_half(n, g, x, i):
                    rows = down[:, 4 * g:4 * g + 4, x * 4 * W:(x + 1) * 4 * W] if isinstance(g, int) else \
                        down[:, bass.ds(g * 4, 4), x * 4 * W:(x + 1) * 4 * W]
                    load(n, [(slot(n, 4, 4 * W), rows)], i, 12, 48)

                n0 = at[name][0]
                gate_up(n0, 0, 0, None)
                gate_up(n0 + 2, 0, 1, None)
                n0 = at[name + "loop"][0]

                def turn(j, i):
                    for z in range(2):
                        n, g = n0 + 6 * z, 2 * j + (z + 1)
                        for x in range(2):
                            gate_up(n + 3 * x, g, x, i)
                            down_half(n + 3 * x + 2, 2 * j + z, x, i)
                turns((GROUPS - 1) // 2, turn)
                for x in range(2):
                    down_half(at[name + "end"][0] + x, GROUPS - 1, x, None)

            for c in range(2):
                paired(at["b0"][0] + c, w_in, A_Q + c * P)
            for c in range(3):
                plain(at["b2"][0] + c, w_in, A_KV + c * W)
            plain(at["b5"][0], w_in, A_G)
            for c in range(8):
                plain(at["hin"][0] + c, w_in, B_IN + c * W)
            for c in range(6):
                plain(at[f"b{6 + c}"][0], w_in, C_IN + c * W)
            wait_copied(sp, o_of("sgT"))
            merge_tiles(at["merge1"][0], w_in, MERGE, kp(t["w_branch"]))
            for c in range(2):
                plain(at["xk"][0] + c, kp(t["xattn_k"]), c * W)
            for c in range(2):
                plain(at["xv"][0] + c, kp(t["xattn_v"]), c * W)
            square_tiles(at["mixout1"][0], kp(t["w_mix_out"]))
            for c in range(2):
                plain(at["xq"][0] + c, kp(t["xattn_q"]), c * W)
            for c in range(2):
                n = at["xo"][0] + c
                load(n, [(slot(n, 4, 4 * W), kp(t["xattn_o"])[:, :, c * 4 * W:(c + 1) * 4 * W])])
            ff_tiles("ff1", kp(t["ffn_in"]), kp(t["ffn_in"]), 0, FF, kp(t["ffn_out"]))
            n = at["in2"][0]
            for c in range(4):
                plain(n + c, w_in2, BX2 + c * W)
            for c in range(2):
                paired(n + 4 + c, w_in2, DQ2 + c * P)
            plain(n + 6, w_in2, DKV2)
            for c in range(6):
                plain(n + 7 + c, w_in2, AQ2 + c * W)
            load(n + 13, [(slot(n + 13, KC, 4), w_in2[:, :, CF2:CF2 + 4])])
            for c in range(6):
                plain(n + 14 + c, w_in2, CQ2 + c * W)
            sp.wait_ge(pv_done, U_FOX)
            merge_tiles(at["merge2"][0], w_in2, GZ2, kp(t["w_branch_2"]))
            square_tiles(at["mixout2"][0], kp(t["w_out_2"]))
            ff_tiles("ff2", kp(t["w_ffn_gate_2"]), kp(t["w_ffn_up_2"]), 0, 0, kp(t["w_ffn_down_2"]))

            for q in range(NT):
                wait_rows(sp, "out", q)
                sp.dma_start(out[q * P:(q + 1) * P, :], xa[:, q, :]).then_inc(out_landed, 16)
            sp.wait_ge(out_landed, 16 * NT)

        @block.gpsimd
        def _(pool):
            rows = lambda ap: ap.partition_broadcast(P)

            def bias_table(u):
                if bias_of(u) is None:
                    return
                prev = [v for v in range(u % 2, u, 2) if bias_of(v) is not None]
                if prev:
                    pool.wait_ge(biased, prev[-1] + 1)
                pool.dma_start(bias[:, u % 2, :], t["t_bias"][bias_of(u)]).then_inc(bias_landed[u % 2], 16)

            def norm_rows(k, g, b):
                if k:
                    pool.wait_ge(norm_done, k)
                n = 0
                for dst, name in ((lng, g), (lnb, b)):
                    if name:
                        pool.dma_start(dst[k], rows(t[name])).then_inc(norm_rows_landed, 16 if b else 32)
                        n += 1

            pool.dma_start(ident[:, :], t["t_ident"]).then_inc(ident_landed, 16)
            pool.dma_start(rowsx, t["x"].rearrange("(a p) d -> p a d", p=P)).then_inc(x_landed, 16)
            for i, st in enumerate(STACKS):
                r = 0
                for name, n in st:
                    pool.dma_start(stack_rows(i)[r:r + n, :], t[name]).then_inc(stack_landed, 16)
                    r += n
            pool.dma_start(lmask, t["t_small"][:, T_LEVEL:T_LEVEL + 8 * P].rearrange("p (a b) -> p a b", a=8))\
                .then_inc(level_tab_landed, 16)
            pool.dma_start(hgrow, rows(t["hgrn_norm_g"])).then_inc(level_tab_landed, 16)

            for u in range(U_NSA, U_X):
                bias_table(u)

            ts = t["t_small"]
            half = lambda h: slice(64 * h, 64 * h + 64)

            def small(loads, landed_):
                for dst, src in loads:
                    pool.dma_start(dst, src).then_inc(landed_, 16)

            wait_part(pool, f"lvl{HL + 1}")
            small([
                (sgrow, t["sg_w"].rearrange("g q p -> q g p")),
                (tri, ts[:, T_TRI:T_TRI + P]),
                (posrow[0:64, 0:64], t["nsa_cmp_pos"]), (posrow[0:64, 64:128], t["nsa_cmp_pos"]),
                (cw[half(0)], t["nsa_cmp_w"].rearrange("i l d e -> d i l e")),
                (cw[half(1)], t["nsa_cmp_w"].rearrange("i l d e -> d i l e")),
            ], weights1_landed)
            wait_part(pool, "ho")
            small([(ctab, ts[:, T_CBIAS:T_CBIAS + 480]),
                   (invc, ts[:, T_COUNT:T_COUNT + 4 * S].rearrange("p (a b) -> p a b", a=4))], tables1_landed)
            wait_copied(pool, o_of("hT"))
            small([(poolw, t["pool_w"].rearrange("g c d -> c g d")),
                   (slg, rows(t["sg_ln_g"])), (slb, rows(t["sg_ln_b"]))], mixer1_landed)

            wait_copied(pool, o_of("nT"))
            pool.dma_start(xa[:, :, :], t["mem"].rearrange("(a p) d -> p a d", p=P)).then_inc(mem_landed, 16)
            wait_copied(pool, o_of("memT", 3))
            pool.dma_start(xa[:, :, :], t["x"].rearrange("(a p) d -> p a d", p=P)).then_inc(resid_landed, 16)
            pool.wait_ge(lo_ready, at["memT"][3] + 4)
            norm_rows(0, "ln_mix_g", "ln_mix_b")
            norm_rows(1, "ln_x_g", "ln_x_b")
            pool.wait_ge(piece_used, at["xq"][4] + 8)
            norm_rows(2, "ln_ffn_g", "ln_ffn_b")

            pool.wait_ge(lo_ready, at["xT2"][3] + 4)
            pool.wait_ge(norm_done, 3)
            pool.memset(score[:, :, :], 0.0).then_inc(lru_zeroed, 1)
            pool.wait_ge(lru_zeroed, 1)
            for i, name in enumerate(("lru_wa_2", "lru_wx_2")):
                for h in range(2):
                    pool.dma_start(wl[half(h), i, :, half(h)],
                                   t[name].rearrange("(c h) k d -> h k c d", h=2)[h]).then_inc(lru_landed, 16)
            for j, name in enumerate(("diff_lq1_2", "diff_lk1_2", "diff_lq2_2", "diff_lk2_2")):
                pool.dma_start(lrow[:, 64 * j:64 * j + 64], rows(t[name])).then_inc(mixer2_landed, 16)
            pool.dma_start(sinks, rows(t["swa_sinks_2"])).then_inc(mixer2_landed, 16)
            pool.dma_start(subln, rows(t["diff_subln_2"])).then_inc(mixer2_landed, 16)
            pool.dma_start(heads[0:4], ts[0:4, T_HEAD:T_END].rearrange("p (h c) -> p h c", h=5))\
                .then_inc(mixer2_landed, 16)
            pool.dma_start(bf[0:4], t["fox_b_f_2"].rearrange("(a b) -> a b", b=1)).then_inc(mixer2_landed, 16)
            for u in range(U_SWA, U_END):
                bias_table(u)
            wait_copied(pool, o_of("x3T", 3))
            wait_rows(pool, "x3T", 3)
            norm_rows(3, "norm_final_2", None)

        @block.tensor
        def _(pe):
            mm, turn = nc.tensor.matmul, nc.tensor.transpose
            rows_done = Count(pe, pe_rows)

            def turn_rows(name, rows, by_quarter=True):
                for k in range(4):
                    if by_quarter:
                        wait_rows(pe, name, k)
                    o = o_of(name, k)
                    wait_bank(o)
                    b = banks(o).rearrange("p a (c t) -> p (a c) t", c=2)
                    for c in range(4):
                        for q in range(NT):
                            last = turn(b[:, c, q * P:(q + 1) * P],
                                        rows[:, q, (4 * k + c) * P:(4 * k + c + 1) * P], ident[:, :])
                    last.then_inc(part_done, 1)

            def turn_branch(name, rows):
                o = o_of(name)
                wait_bank(o)
                b = banks(o).rearrange("p a (c t) -> p (a c) t", c=2)
                for c in range(4):
                    for q in range(NT):
                        last = turn(b[:, c, q * P:(q + 1) * P], rows[:, q, c * P:(c + 1) * P], ident[:, :])
                last.then_inc(part_done, 1)

            def piece_product(s_, p_, o, first, last_, act, k0, by_token, i=None, per_s=0, per_o=0,
                              m=W):
                reach(pe, lo_ready, s_ + 1, i, per_s)
                if first:
                    wait_bank(o, i, per_o)
                b = banks(o)
                w3 = [x[:, p_ % PIECES, 0:4 * m].rearrange("p (k c) -> p k c", k=4) for x in (whi, wlo)]
                for x in range(2 if by_token else -(-m // P)):
                    xs = slice(x * P, (x + 1) * P)
                    dst = b[:, x, 0:m] if by_token else b[0:min(m, P), x, 0:S]
                    for k in range(4):
                        for n, (wp, ap) in enumerate(((0, 0), (0, 1), (1, 0))):
                            if by_token:
                                l_, r_ = act(ap)[:, k0 + k, xs], w3[wp][:, k, :]
                            else:
                                l_, r_ = w3[wp][:, k, x * P:min((x + 1) * P, m)], act(ap)[:, k0 + k, :]
                            last = mm(dst, l_, r_, start=first and k == 0 and n == 0,
                                      stop=last_ and k == 3 and n == 2)
                last.then_inc(piece_used, 1)

            part_of = lambda R: lambda ap: R[:, ap]

            def whole(s_, p_, o, act, by_token, **kw):
                for k in range(4):
                    piece_product(s_ + k, p_ + k, o, k == 0, k == 3, act, 4 * k, by_token, **kw)

            def key_value_tile(s_, p_, o):
                act = part_of(actR)
                wait_bank(o)
                b = banks(o)
                w3 = lambda k, wp: (whi, wlo)[wp][:, (p_ + k) % PIECES, :].rearrange("p (k c) -> p k c", k=4)
                parts = tuple(enumerate(((0, 0), (0, 1), (1, 0))))
                for k in range(KC):
                    if k % 4 == 0:
                        reach(pe, lo_ready, s_ + k // 4 + 1)
                    for n, (wp, ap) in parts:
                        mm(b[:, 0, 0:S], w3(k // 4, wp)[:, k % 4, 0:P], act(ap)[:, k, :],
                           start=k == 0 and n == 0, stop=k == KC - 1 and n == 2)
                for q in range(NT):
                    for k in range(KC):
                        for n, (wp, ap) in parts:
                            last = mm(b[:, 1, q * P:(q + 1) * P], act(ap)[:, k, q * P:(q + 1) * P],
                                      w3(k // 4, wp)[:, k % 4, P:2 * P],
                                      start=k == 0 and n == 0, stop=k == KC - 1 and n == 2)
                        if q and k % 4 == 3:
                            last.then_inc(piece_used, 1)

            def projection(name, k, form):
                d4 = projection_pieces(name, k)
                o = o_of(name, k)
                if form == "both":
                    key_value_tile(d4[0].split, d4[0].piece, o)
                    return
                for q, d in enumerate(d4):
                    piece_product(d.split, d.piece, o, q == 0, q == 3, part_of(actR), 4 * q, form == "tokens", m=d.w)
                    for a, b in groups_at(name, k) if name in BEHIND_HALVES and q == 0 else []:
                        wait_copied(pe, o - 2)
                        wait_copied(pe, o - 1)
                        if a == U_SWA:
                            pe.wait_ge(mixer_rows, 7)
                        scores(a)
                    for u in units_behind(d):
                        unit_step(*u)

            def whole_tiles(name, n, act, by_token):
                _, _, o, s_, p_ = at[name]
                for k in range(n):
                    whole(s_ + 4 * k, p_ + 4 * k, o + k, act, by_token)

            def mix_out(name):
                _, _, o, s_, p_ = at[name]
                with pe.Fori(0, 4) as i:
                    for k in range(2):
                        whole(s_ + 4 * k, p_ + 4 * k, o + k, part_of(mixR), True, i=i, per_s=8, per_o=2)

            def merge(name):
                _, _, o0, s0, p0 = at[name]
                with pe.Fori(0, D // W) as i:
                    kw = dict(i=i, per_s=20, per_o=8)
                    for b in range(NBR):
                        whole(s0 + 5 * b, p0 + 5 * b, o0 + 2 * b, part_of(actR), False, **kw)
                        piece_product(s0 + 5 * b + 4, p0 + 5 * b + 4, o0 + 2 * b + 1, True, True, part_of(brR),
                                      4 * b, False, **kw)

            def feed_forward(name, act):
                def gate_up(s_, p_, o, **kw):
                    for k in range(2):
                        whole(s_ + 4 * k, p_ + 4 * k, o + k, act, False, **kw)

                def down_half(par, g, s_, p_, o, x, i=None, **kw):
                    if x == 0:
                        reach(pe, hid_lo, 2 * g + 2, i, 4)
                    for k in range(4):
                        piece_product(s_ + k, p_ + k, o + k, True, True, lambda ap: hidR(par, ap), 0, True, i=i, **kw)

                _, _, o, s_, p_ = at[name]
                gate_up(s_, p_, o)
                gate_up(s_ + 8, p_ + 8, o + 2)
                _, _, o, s_, p_ = at[name + "loop"]
                h0 = hid0[name]
                with pe.Fori(0, (GROUPS - 1) // 2) as i:
                    kw = dict(i=i, per_s=48, per_o=24)
                    for z in range(2):
                        for x in range(2):
                            d = 24 * z + 12 * x
                            gate_up(s_ + d, p_ + d, o + 12 * z + 6 * x, **kw)
                            down_half(z, h0 + z, s_ + d + 8, p_ + d + 8, o + 12 * z + 6 * x + 2, x, **kw)
                _, _, o, s_, p_ = at[name + "end"]
                for x in range(2):
                    down_half(0, h0 + GROUPS - 1, s_ + 4 * x, p_ + 4 * x, o + 4 * x, x)

            def scores(u):
                q_, k_, extra, _, _ = unit(u)
                if u >= 2:
                    pe.wait_ge(biased, u - 1)
                for m in range(2):
                    dst = sc[:, u % 2, m * S:(m + 1) * S]
                    more = extra(m)
                    last = mm(dst, q_(m), k_(m), start=True, stop=not more)
                    for x, (l_, r_) in enumerate(more):
                        last = mm(dst, l_, r_, start=False, stop=x == len(more) - 1)
                    if m == 0 and kind(u) not in ("x", "fox"):
                        rows_done.link(last)
                last.then_inc(scores_done, 1)

            def turn_probs(u):
                pe.wait_ge(probs_ready, u + 1)
                if u:
                    pe.wait_ge(probT_ready, u)
                for x in range(4):
                    last = turn(pt[:, x * P:(x + 1) * P], score[:, u % 2, x * P:(x + 1) * P], ident[:, :])
                last.then_inc(probs_turned, 1)

            def values(u):
                _, _, _, v_, dv = unit(u)
                pe.wait_ge(probT_ready, u + 1)
                if u:
                    pe.wait_ge(pv_used, u)
                for m in range(2):
                    for kt in range(NT):
                        last = mm(pv[:, m * dv:(m + 1) * dv], probT[:, u % 2, (2 * m + kt) * P:(2 * m + kt + 1) * P],
                                  v_(m, kt), start=kt == 0, stop=kt == NT - 1)
                last.then_inc(pv_done, 1)

            def unit_step(u, a, b):
                if u + 1 < b:
                    scores(u + 1)
                if u > a:
                    values(u - 1)
                turn_probs(u)
                if u == b - 1:
                    values(u)

            def attend(a, b):
                scores(a)
                for u in range(a, b):
                    unit_step(u, a, b)

            def vectors_to_columns():
                pe.wait_ge(stack_landed, 16 * sum(len(s_) for s_ in STACKS))
                o = o_of("cols")
                wait_bank(o)
                for i, st in enumerate(STACKS):
                    r = sum(n for _, n in st)
                    last = turn(banks(o)[:, 0, i * P:i * P + r], stack_rows(i)[0:r, :], ident[0:r, 0:r])
                last.then_inc(part_done, 1)

            pe.wait_ge(ident_landed, 16)
            pe.wait_ge(x_landed, 16)
            turn_rows("xT1", rowsx, False)

            b_form = lambda k: "features" if k in (0, 1, 2, 6, 7) else "both" if k in (3, 4) else "tokens"
            for name, k in BLOCK1_TILES:
                projection(name, k, b_form(int(name[1:])) if name != "hin" else "features" if k < 4 else "tokens")
                if name == "b1":
                    vectors_to_columns()
            n = 7
            for lv in range(HL + 2):
                pe.wait_ge(level_ready, lv + 1)
                o = o_of(f"lvl{lv}")
                wait_bank(o)
                b = banks(o)
                if lv <= HL:
                    for q in range(NT):
                        for h in range(4):
                            last = mm(b[:, q, h * P:(h + 1) * P], hkd[:, h, q * P:(q + 1) * P],
                                      hqd[:, h, q * P:(q + 1) * P], start=True, stop=True)
                else:
                    for h in range(4):
                        last = mm(b[:, 0, h * P:(h + 1) * P], hkd[:, h, 0:P], hqd[:, h, P:S], start=True, stop=True)
                last.then_inc(part_done, 1)
                for _ in range(B_AFTER[lv]):
                    projection(f"b{n}", 0, b_form(n))
                    n += 1
            pe.wait_ge(decay_ready, 1)
            o = o_of("ho")
            wait_bank(o)
            b = banks(o)
            A = lambda q, h: ATd[:, (q * 4 + h) * P:(q * 4 + h + 1) * P]
            for h in range(4):
                hs = slice(h * P, (h + 1) * P)
                mm(b[:, 0, hs], A(0, h), hi[:, 0, hs], start=True, stop=True)
                mm(b[:, 1, hs], A(1, h), hi[:, 1, hs], start=True, stop=False)
                last = mm(b[:, 1, hs], ATx[:, h, :], hi[:, 0, hs], start=False, stop=True)
            last.then_inc(part_done, 1)
            pe.wait_ge(mixer_rows, 1)
            turn_branch("hT", ho)

            pe.wait_ge(weights1_landed, 16 * 6)
            o = o_of("sgw")
            wait_bank(o)
            for g in range(4):
                last = turn(banks(o)[:, 0, g * P:(g + 1) * P], sgrow[:, g, :], ident[:, :])
            last.then_inc(part_done, 1)
            pe.wait_ge(mixer1_landed, 16 * 3)
            pe.wait_ge(mixer_rows, 2)
            o = o_of("pool")
            wait_bank(o)
            b = banks(o).rearrange("p a (c t) -> p (a c) t", c=2)
            for g in range(4):
                last = mm(b[:, g, :], poolw[:, g, :], ping[:, g, 16:], start=True, stop=True)
            last.then_inc(part_done, 1)
            pe.wait_ge(mixer_rows, 3)
            o = o_of("sgo")
            wait_bank(o)
            for q in range(NT):
                for g in range(4):
                    gs = slice(g * P, (g + 1) * P)
                    last = mm(banks(o)[:, q, gs], wmT[:, g, :], sv[:, q, gs], start=True, stop=True)
            last.then_inc(part_done, 1)
            pe.wait_ge(mixer_rows, 4)
            turn_branch("sgT", su)

            o = o_of("pos")
            wait_bank(o)
            turn(banks(o)[:, 0, 0:64], posrow[0:64, :], ident[0:64, 0:64]).then_inc(part_done, 1)
            pe.wait_ge(cmp_ready, 1)
            o = o_of("ckv")
            wait_bank(o)
            b = banks(o)
            for g in range(2):
                gh = slice(64 * g, 64 * g + 64)
                for l in range(32):
                    mm(b[gh, 0, 0:NC], cw[gh, 0, l, :], win[gh, 0, l, :], start=l == 0, stop=l == 31)
            for g in range(2):
                gh = slice(64 * g, 64 * g + 64)
                for l in range(32):
                    last = mm(b[0:NC, 1, gh], win[gh, 1, l, :], cw[gh, 1, l, :], start=l == 0, stop=l == 31)
                if g == 0:
                    rows_done.link(last)
            last.then_inc(part_done, 1)
            wait_copied(pe, o_of("ckv"))
            o = o_of("cs")
            wait_bank(o)
            b = banks(o)
            for g in range(2):
                gh = slice(64 * g, 64 * g + 64)
                for q in range(NT):
                    for h in range(4 * g, 4 * g + 4):
                        last = mm(b[:, q, h * NC:(h + 1) * NC], qn[gh, h % 4, q * P:(q + 1) * P], kcmp[gh, :],
                                  start=True, stop=True)
                if g == 0:
                    rows_done.link(last)
            last.then_inc(part_done, 1)
            pe.wait_ge(cmp_ready, 3)
            for q in range(NT):
                o = o_of("cT", q)
                wait_bank(o)
                b = banks(o).rearrange("p a (c t) -> p (a c) t", c=4)
                for h in range(NH):
                    at_ = (q * NH + h) * NC
                    last = turn(b[0:NC, h, :], cS[:, at_:at_ + NC], ident[:, :])
                last.then_inc(part_done, 1)
            wait_copied(pe, o_of("cT", 0))
            wait_copied(pe, o_of("cT", 1))
            o = o_of("co")
            wait_bank(o)
            for q in range(NT):
                for h in range(NH):
                    g = h // 4
                    last = mm(banks(o)[:, q, 64 * h:64 * h + 64], cPT[0:NC, q * NH + h, :],
                              vcmp[0:NC, 64 * g:64 * g + 64], start=True, stop=True)
            last.then_inc(part_done, 1)
            pe.wait_ge(mixer_rows, 5)
            turn_branch("nT", oa)
            wait_copied(pe, o_of("nT"))

            merge("merge1")
            wait_rows(pe, "memT")
            turn_rows("memT", xa, False)
            whole_tiles("xk", 2, part_of(brR), False)
            whole_tiles("xv", 2, part_of(brR), True)
            pe.wait_ge(gate_used, 8)
            mix_out("mixout1")

            turn_rows("x1T", xa)
            whole_tiles("xq", 2, part_of(mixR), False)
            wait_copied(pe, o_of("xq", 0))
            wait_copied(pe, o_of("xq", 1))
            attend(U_X, U_SWA)
            pe.wait_ge(mixer_rows, 6)
            turn_branch("xoT", ox)
            _, _, o, s_, p_ = at["xo"]
            for k in range(8):
                piece_product(s_ + k, p_ + k, o + k, True, True, part_of(brR), 0, True)

            turn_rows("x2T", xa)
            feed_forward("ff1", part_of(actR))

            turn_rows("xT2", rowsx)
            def lru_gates():
                pe.wait_ge(lru_landed, 64)
                pe.wait_ge(lru_conv, 1)
                for w_ in range(2):
                    o = o_of("lru", w_)
                    wait_bank(o)
                    b = banks(o).rearrange("p a (c t) -> p (a c) t", c=2)
                    for c in range(4):
                        last = mm(b[:, c, :], wl[:, w_, c, :], xc[:, c, :], start=True, stop=True)
                    last.then_inc(part_done, 1)

            for k in range(20):
                projection("in2", k, "both" if k == 6 else "tokens" if k in (11, 12, 18, 19) else "features")
                if k == 6:
                    lru_gates()

            wait_copied(pe, o_of("in2", 18))
            wait_copied(pe, o_of("in2", 19))
            pe.wait_ge(mixer_rows, 8)
            attend(U_FOX, U_END)
            pe.wait_ge(mixer_rows, 9)
            for name, rows in (("y0T", ya), ("y2T", yc), ("y3T", yd)):
                turn_branch(name, rows)
            wait_copied(pe, o_of("y2T"))
            wait_copied(pe, o_of("y3T"))
            merge("merge2")
            pe.wait_ge(gate_used, 16)
            mix_out("mixout2")
            turn_rows("x3T", rowsx)
            feed_forward("ff2", part_of(mixR))

        @block.scalar
        def _(act):
            f = nc.scalar.activation
            own = Count(act, s_link)

            def halves(o):
                return banks(o)[:, :, 0:S]

            def part_out(name, k, dst, func=ACT.Copy, src=None):
                o = o_of(name, k)
                wait_part(act, name, k)
                release(f(dst, banks(o) if src is None else src(banks(o)), func), o)

            def branch_out(name, chunk):
                part_out(name, 0, brT[:, chunk:chunk + 4, :].rearrange("p (a c) t -> p a (c t)", a=2))

            def split(d, i):
                if d.k == 0:
                    reach(act, w_landed[d.tile % SLOTS], LANDED * (d.tile // SLOTS + 1), i,
                          LANDED * d.per_tile // SLOTS)
                if d.piece >= PIECES or not isinstance(i, int):
                    reach(act, piece_used, d.piece + 1 - PIECES, i, d.per_piece)
                f(part_of_piece(whi, d), raw(d), ACT.Copy).then_inc(hi_ready, 1)

            def high(R, src, k):
                f(R[:, 0, 4 * k:4 * k + 4, :], src, ACT.Copy).then_inc(hi_ready, 1)

            def turned_high(name, R, n=4):
                for k in range(n):
                    wait_part(act, name, k)
                    b = banks(o_of(name, k)).rearrange("p a (c t) -> p (a c) t", c=2)
                    high(R, b, k)

            def finish_copy(dst):
                def finish(d, i):
                    if d.ends:
                        product(act, d, i)
                        release(f(dst(d.c), halves(d.out), ACT.Copy), d.out)
                return finish

            def finish_none(d, i):
                pass

            def hidden_step(from_bank):
                def finish(d, i):
                    if not d.hid:
                        return
                    step, hd = d.hid
                    x, h = hd["x"], hd["h"]
                    silu = lambda src: f(siluS[:, x, :].rearrange("p (a c) -> p a c", a=2), src, ACT.Silu)
                    if step == ("gate" if from_bank else "silu"):
                        if h >= 2:
                            reach(act, hid_lo, h - 1, i, hd["per_h"])
                        if from_bank:
                            product(act, d, i)
                            release(silu(halves(hd["og"])), hd["og"])
                        else:
                            copied(act, hd["og"], i, hd["per_out"])
                            silu(convS[:, x, :].rearrange("p (a c) -> p a c", a=2)).then_inc(silu_ready, 1)
                    elif step == "hi":
                        copied(act, hd["ou"], i, hd["per_out"])
                        f(hidR(hd["par"], 0)[:, 2 * x:2 * x + 2, :],
                          siluS[:, x, :].rearrange("p (a c) -> p a c", a=2), ACT.Copy).then_inc(hid_hi, 1)
                return finish

            def feed_forward(name, from_bank):
                first, before, turn_, behind = ff_pieces(name)
                finish = hidden_step(from_bank)
                straight(before, split, finish)
                finish(Piece(0, 0, 0, 0, 0, 0, hid=("hi", first[1])), 0)
                in_turns(act, (GROUPS - 1) // 2, turn_, split, finish, behind)

            def root(k, n):
                act.wait_ge(var_ready, k)
                f(stats[:, 72:72 + n], stats[:, 64:64 + n], ACT.Sqrt).then_inc(std_ready, 1)

            def exps(u):
                act.wait_ge(max_ready, u + 1)
                c = 2 * (u % 4)
                for m in range(2):
                    s_ = score[:, u % 2, m * S:(m + 1) * S]
                    last = f(s_, s_, ACT.Exp, bias=vecs[:, c + m:c + m + 1],
                             accum_out=vecs[:, 8 + c + m:9 + c + m])
                if kind(u) == "swa":
                    for m in range(2):
                        h = ((u - U_SWA) // 2) + 4 * m
                        last = f(vecs[:, 24 + c + m:25 + c + m], sinks[:, h:h + 1], ACT.Exp,
                                 bias=vecs[:, c + m:c + m + 1])
                last.then_inc(probs_ready, 1)

            def copy_probs(u):
                act.wait_ge(probs_turned, u + 1)
                if u >= 2:
                    act.wait_ge(pv_done, u - 1)
                f(probT[:, u % 2, :], pt[:, :], ACT.Copy).then_inc(probT_ready, 1)

            def unit_step(u, a, b):
                if u == a:
                    exps(a)
                if u + 1 < b:
                    exps(u + 1)
                copy_probs(u)

            def attend(a, b):
                for u in range(a, b):
                    unit_step(u, a, b)

            def finish_projection(outs):
                def finish(d, i):
                    if d.ends:
                        dst, func, src, scale, then = (outs[d.b] + (ACT.Copy, halves, 1.0, None)[len(outs[d.b]) - 1:])
                        product(act, d, i)
                        release(f(dst, src(d.out), func, scale=scale), d.out)
                        if then:
                            then()
                    for u in units_behind(d):
                        unit_step(*u)
                return finish

            turned_high("xT1", actR)

            def columns_out():
                wait_part(act, "cols")
                for i, st in enumerate(STACKS):
                    r = sum(n for _, n in st)
                    last = f(cols[:, i, 0:r], banks(o_of("cols"))[:, 0, i * P:i * P + r], ACT.Copy)
                release(last, o_of("cols"))

            def lower_bound_exp():
                act.wait_ge(lb_max, 1)
                f(lbv[:, 4:8], lbv[:, 0:4], ACT.Exp).then_inc(lb_exp, 1)

            outs = {("b5", 0): (ag, ACT.Sigmoid, lambda o: banks(o)[:, :, 0:24])}
            for k, dst in enumerate((kvc, kvs, kvw)):
                outs[f"b{2 + k}", 0] = (dst, ACT.Copy, halves, 1.0, lower_bound_exp if k == 1 else None)
            for k in range(2):
                pair, cs = slice(2 * k, 2 * k + 2), slice(k * W, (k + 1) * W)
                outs[f"b{k}", 0] = (qn[:, pair, :], ACT.Copy, halves, 1.0, columns_out if k else None)
                outs["hin", k] = (hq[:, pair, :],)
                outs["hin", 2 + k] = (hp[:, pair, :], ACT.Sigmoid)
                outs["hin", 4 + k] = (hi[:, :, cs],)
                outs["hin", 6 + k] = (hg[:, :, cs], ACT.Silu)
                outs[f"b{6 + k}", 0] = (cpad[:, pair, 16:],)
                outs[f"b{8 + k}", 0] = (su[:, :, cs], ACT.Gelu_apprx_tanh)
                outs[f"b{10 + k}", 0] = (sv[:, :, cs], ACT.Gelu_apprx_tanh)
            straight([d for tile in BLOCK1_TILES + [(f"b{k}", 0) for k in range(7, 12)]
                      for d in projection_pieces(*tile)], split, finish_projection(outs))
            part_out("ho", 0, ho)
            root(1, 8)
            branch_out("hT", 4)
            root(2, 2)
            branch_out("sgT", 12)
            act.wait_ge(cmp_ready, 2)
            f(cS, cS, ACT.Exp).then_inc(cmp_exp, 1)
            for q in range(NT):
                part_out("cT", q, cPT[0:NC, q * NH:(q + 1) * NH, :].rearrange("p (a c) t -> p a (c t)", a=2),
                         src=lambda b: b[0:NC])
            branch_out("nT", 0)

            def branches_high():
                for k in range(4):
                    high(brR, brT[:, 4 * k:4 * k + 4, :], k)

            def gate(d, i):
                if d.ends == "gate":
                    product(act, d, i)
                    o = d.out + 1 - 4
                    reach(act, acc_free[o % 2], o // 2 + 1, i, d.per_out // 2)
                    release(f(gateS[:, d.b % 2, :].rearrange("p (a c) -> p a c", a=2), halves(d.out), ACT.Sigmoid),
                            d.out)

            wait_copied(act, o_of("nT"))
            branches_high()

            def gate_and_root(d, i):
                gate(d, i)
                if isinstance(i, int) and i == 0 and d == merge_pieces("merge1")[NORM_ROOT]:
                    root(3, 2)

            in_turns(act, D // W, merge_pieces("merge1"), split, gate_and_root)

            for k in range(4):
                wait_part(act, "memT", k)
                o = o_of("memT", k)
                b = banks(o).rearrange("p a (c t) -> p (a c) t", c=2)
                tmp = mem_tmp[k % 2].rearrange("p (c t) -> p c t", c=4)
                if k >= 2:
                    act.wait_ge(lo_ready, at["memT"][3] + k - 1)
                for c in range(4):
                    last = f(tmp[:, c, :], b[:, c, :], ACT.Identity,
                             scale=col("mem_ln_g", 4 * k + c), bias=col("mem_ln_b", 4 * k + c))
                release(last, o)
                wait_copied(act, o)
                high(brR, tmp, k)
            straight(tile_pieces("xk", 2), split, finish_copy(lambda c: kx[:, 2 * c:2 * c + 2, :]))
            straight(tile_pieces("xv", 2), split, finish_copy(lambda c: vx[:, :, c * W:(c + 1) * W]))
            in_turns(act, 4, tile_pieces("mixout1", 8, 4), split, finish_none)
            root(4, 2)
            turned_high("x1T", mixR)
            straight(tile_pieces("xq", 2), split, finish_copy(lambda c: qx[:, 2 * c:2 * c + 2, :]))
            attend(U_X, U_SWA)
            turned_high("xoT", brR, 1)
            straight(wide_pieces("xo"), split, finish_none)
            root(5, 2)
            turned_high("x2T", actR)
            feed_forward("ff1", False)
            root(6, 2)
            root(7, 2)

            for k in range(4):
                wait_copied(act, o_of("xT2", k))
                high(actR, turn_tmp[k % 2].rearrange("p (c t) -> p c t", c=4), k)

            def small_exps():
                act.wait_ge(sp_abs, 1)
                f(lbv[:, 20:24], lbv[:, 16:20], ACT.Exp).then_inc(sp_exp, 1)
                act.wait_ge(lam_sum, 1)
                f(lbv[:, 34:36], lbv[:, 32:34], ACT.Exp).then_inc(lam_exp, 1)

            def lru_gates():
                for w_, (dst, bcol) in enumerate(((lr, "lru_ba_2"), (li, "lru_bx_2"))):
                    wait_part(act, "lru", w_)
                    b = banks(o_of("lru", w_)).rearrange("p a (c t) -> p (a c) t", c=2)
                    for c in range(4):
                        last = f(dst[:, c, :], b[:, c, :], ACT.Sigmoid, bias=col(bcol, c))
                    release(last, o_of("lru", w_))

            def lru_decay():
                act.wait_ge(lru_arg, 1)
                f(lt, lr, ACT.Tanh, scale=-1.0)
                f(la, lr, ACT.Exp).then_inc(lru_exp, 1)

            def lru_root():
                act.wait_ge(lru_sq, 1)
                f(lt, lt, ACT.Sqrt, scale=2.0).then_inc(lru_sqrt, 1)

            def forget_exp():
                act.wait_ge(sp_abs, 2)
                f(ftmp[0:4, 1, :], ftmp[0:4, 0, :], ACT.Exp).then_inc(sp_exp, 1)

            outs = {("in2", 6): (dkv, ACT.Copy, halves, 1.0, lru_gates),
                    ("in2", 13): (cf[0:4, :], ACT.Copy, lambda o: banks(o)[0:4, 0, 0:S], 1.0, forget_exp)}
            for k in range(2):
                pair, cs = slice(2 * k, 2 * k + 2), slice(k * W, (k + 1) * W)
                outs["in2", k] = (bx[:, pair, 4:],)
                outs["in2", 2 + k] = (bg[:, pair, :], ACT.Gelu_apprx_tanh, halves, 1.0, small_exps if k else None)
                outs["in2", 4 + k] = (dq[:, pair, :],)
                outs["in2", 7 + k] = (aq[:, pair, :], ACT.Copy, halves, 1.0, lru_root if k else lru_decay)
                outs["in2", 9 + k] = (ak[:, pair, :],)
                outs["in2", 11 + k] = (av[:, :, cs],)
                outs["in2", 14 + k] = (cq[:, pair, :], ACT.Copy, halves, P ** -0.5)
                outs["in2", 16 + k] = (ck[:, pair, :],)
                outs["in2", 18 + k] = (cv[:, :, cs], ACT.Copy, halves, 1.0, None if k else lambda: root(8, 8))
            straight([d for k in range(20) for d in projection_pieces("in2", k)], split, finish_projection(outs))
            attend(U_FOX, U_END)
            branch_out("y0T", 0)
            branch_out("y2T", 8)
            branch_out("y3T", 12)

            def gate_in_place(d, i):
                if d.ends == "gate":
                    copied(act, d.out, i, d.per_out)
                    f(gateS[:, d.b % 2, :], gateS[:, d.b % 2, :], ACT.Sigmoid).then_inc(gate_ready, 1)

            wait_copied(act, o_of("y3T"))
            branches_high()
            in_turns(act, D // W, merge_pieces("merge2"), split, gate_in_place)
            in_turns(act, 4, tile_pieces("mixout2", 8, 4), split, finish_none)
            root(9, 2)
            for k in range(4):
                wait_copied(act, o_of("x3T", k))
                high(mixR, turn_tmp[k % 2].rearrange("p (c t) -> p c t", c=4), k)

            feed_forward("ff2", True)
            root(10, 2)

        @block.vector
        def _(dve):
            v = nc.vector
            own = Count(dve, v_link)
            link = own.link
            tt, ts_, stt = v.tensor_tensor, v.tensor_scalar, v.scalar_tensor_tensor
            mean_var = stats[:, 48:52].rearrange("p (q x) -> p q x", q=NT)
            rstd = stats[:, 80:88]

            def root(k, n):
                dve.wait_ge(std_ready, k)
                link(v.reciprocal(rstd[:, 0:n], stats[:, 72:72 + n]))

            def sums(X, c, g=4):
                st = stats[:, 0:NT * g * 6].rearrange("p (q g x) -> p q g x", q=NT, g=g)
                for q in range(NT):
                    own.tick(v.bn_stats(st[:, q, c, :], X[:, q, c * 512:(c + 1) * 512]))

            def moments(g, k, eps, rms=False):
                st = stats[:, 0:NT * g * 6].rearrange("p (q g x) -> p q g x", q=NT, g=g)
                own.done()
                for q in range(NT):
                    own.tick(v.bn_aggr(mean_var[:, q, :], st[:, q, :, :].rearrange("p g x -> p (g x)")))
                own.done()
                if rms:
                    link(tt(stats[:, 56:58], mean_var[:, :, 0], mean_var[:, :, 0], ALU.mult))
                    link(tt(mean_var[:, :, 1], stats[:, 56:58], mean_var[:, :, 1], ALU.add))
                ts_(stats[:, 64:66], mean_var[:, :, 1], eps, None, ALU.add).then_inc(var_ready, 1)
                root(k, 2)

            def center(dst, X):
                for q in range(NT):
                    own.tick(ts_(dst[:, q, :], X[:, q, :], mean_var[:, q, 0:1], rstd[:, q:q + 1],
                                 ALU.subtract, ALU.mult))
                own.done()

            def normed_quarter(k, c):
                cs = slice(c * 512, (c + 1) * 512)
                for q in range(NT):
                    own.tick(stt(xa[:, q, cs], xa[:, q, cs], mean_var[:, q, 0:1], lng[k][:, cs],
                                 ALU.subtract, ALU.mult))
                own.done()
                for q in range(NT):
                    last = stt(xa[:, q, cs], xa[:, q, cs], rstd[:, q:q + 1], lnb[k][:, cs], ALU.mult, ALU.add)
                    if q == 0:
                        own.tick(last)
                return last

            def norm_and_turn(k, rows_k, name, R):
                moments(4, rows_k, LN_EPS)
                dve.wait_ge(norm_rows_landed, 32 * (k + 1))
                for c in range(5):
                    if c < 4:
                        normed_quarter(k, c).then_inc(rows_ready, 1)
                    if c:
                        turned_low(name, R, c - 1)
                v.memset(stats[:, 90:91], 0.0).then_inc(norm_done, 1)

            def rms_rows(dst, k):
                moments(4, k, RMS_EPS, rms=True)
                for c in range(4):
                    cs = slice(c * 512, (c + 1) * 512)
                    for q in range(NT):
                        ins = ts_(dst[:, q, cs], xa[:, q, cs], rstd[:, q:q + 1], None, ALU.mult)
                    ins.then_inc(rows_ready, 1)

            def low(R, src, k):
                ks = slice(4 * k, 4 * k + 4)
                return tt(R[:, 1, ks, :], src, R[:, 0, ks, :].bitcast(F32), ALU.subtract)

            def wait_high(s_, i=None, per=0):
                reach(dve, hi_ready, s_ + 1, i, per)

            def split(d, i):
                wait_high(d.split, i, d.per_piece)
                tt(part_of_piece(wlo, d), raw(d), part_of_piece(whi, d).bitcast(F32), ALU.subtract)\
                    .then_inc(lo_ready, 1)

            def branches_low(name):
                for k in range(4):
                    wait_high(at[name][3] + k)
                    low(brR, brT[:, 4 * k:4 * k + 4, :], k).then_inc(lo_ready, 1)

            def weighted(name, norm, R):
                def four(k):
                    o = o_of(name, k)
                    if k >= 2:
                        dve.wait_ge(lo_ready, at[name][3] + k - 1)
                    wait_part(dve, name, k)
                    release(tt(turn_tmp[k % 2].rearrange("p (c t) -> p c t", c=4),
                               banks(o).rearrange("p a (c t) -> p (a c) t", c=2),
                               col(norm, 4 * k, 4).unsqueeze(2).broadcast_to([P, 4, S]), ALU.mult), o)

                four(0)
                for k in range(4):
                    if k < 3:
                        four(k + 1)
                    wait_high(at[name][3] + k)
                    low(R, turn_tmp[k % 2].rearrange("p (c t) -> p c t", c=4), k).then_inc(lo_ready, 1)

            def turned_low(name, R, k):
                o = o_of(name, k)
                wait_high(at[name][3] + k)
                release(low(R, banks(o).rearrange("p a (c t) -> p (a c) t", c=2), k), o)
                v.memset(stats[:, 96 + k:97 + k], 0.0).then_inc(lo_ready, 1)

            def finish_none(d, i):
                pass

            def finish_rows(alpha, stage, last_tiles):
                def finish(d, i):
                    if d.ends == "rows":
                        product(dve, d, i)
                        x = xa[:, :, d.c * W:(d.c + 1) * W]
                        b = banks(d.out)[:, :, 0:W]
                        release(stt(x, x, alpha, b, ALU.mult, ALU.add) if alpha else tt(x, x, b, ALU.add), d.out)
                        if d.tile >= last_tiles and d.c % 2:
                            wait_copied(dve, d.out)
                            sums(xa, d.c // 2)
                    if stage:
                        stage(d, i)
                return finish

            def square_out(name, alpha):
                straight(tile_pieces(name, 8), split, finish_rows(alpha, None, at[name][0]))

            def hidden_step(conv):
                def finish(d, i):
                    if not d.hid:
                        return
                    step, hd = d.hid
                    x, h, per_o = hd["x"], hd["h"], hd["per_out"]
                    pair = siluS[:, x, :].rearrange("p (a c) -> p a c", a=2)
                    if step == "gate" and conv:
                        product(dve, d, i)
                        g = banks(hd["og"])
                        cv_ = lambda a, off: convS[:, x, a * S + off:(a + 1) * S]

                        def tap(st, r, a):
                            at_col = r + hd["chunk"] + a
                            return cols[:, st, at_col:at_col + 1] if not hd["per_chunk"] or isinstance(i, int) and i == 0 \
                                else cols[:, st, bass.ds(i * hd["per_chunk"] + at_col, 1)]

                        for a in range(2):
                            own.tick(ts_(cv_(a, 0), g[:, a, 0:S], tap(3, 0, a), tap(1, 64, a), ALU.mult, ALU.add))
                        own.done()
                        for a in range(2):
                            own.tick(stt(cv_(a, 1), g[:, a, 0:S - 1], tap(2, FC, a), cv_(a, 1), ALU.mult, ALU.add))
                        own.done()
                        for a in range(2):
                            ins = stt(cv_(a, 2), g[:, a, 0:S - 2], tap(2, 0, a), cv_(a, 2), ALU.mult, ALU.add)
                        release(ins, hd["og"])
                    elif step == "up":
                        if conv:
                            reach(dve, silu_ready, h + 1, i, hd["per_h"])
                        else:
                            copied(dve, hd["og"], i, per_o)
                        product(dve, d, i)
                        release(tt(pair, banks(hd["ou"])[:, :, 0:S], pair, ALU.mult), hd["ou"])
                    elif step == "lo":
                        reach(dve, hid_hi, h + 1, i, hd["per_h"])
                        lo, hi_ = (hidR(hd["par"], part)[:, 2 * x:2 * x + 2, :] for part in (1, 0))
                        tt(lo, pair, hi_.bitcast(F32), ALU.subtract).then_inc(hid_lo, 1)
                return finish

            def feed_forward(name, conv):
                first, before, turn_, behind = ff_pieces(name)
                finish = hidden_step(conv)
                straight(before, split, finish)
                finish(Piece(0, 0, 0, 0, 0, 0, hid=("lo", first[1])), 0)
                in_turns(dve, (GROUPS - 1) // 2, turn_, split,
                         finish_rows(None, finish, at[name + "end"][0]), behind,
                         own, 16 if conv else 0)

            def log1p(z, s_, s2, p_):
                link(ts_(s_, z, 2.0, None, ALU.add))
                link(v.reciprocal(s_, s_))
                link(tt(s_, s_, z, ALU.mult))
                link(tt(s2, s_, s_, ALU.mult))
                link(ts_(p_, s2, 1.0 / 15, None, ALU.mult))
                for c in (13, 11, 9, 7, 5, 3):
                    link(stt(p_, p_, 1.0 / c, s2, ALU.add, ALU.mult))
                link(stt(p_, p_, 1.0, s_, ALU.add, ALU.mult))
                link(ts_(p_, p_, 2.0, None, ALU.mult))

            def before(u):
                dve.wait_ge(scores_done, u + 1)
                if u >= 2:
                    dve.wait_ge(probs_turned, u - 1)
                S_ = score[:, u % 2, :]
                if bias_of(u) is None:
                    ts_(S_, sc[:, u % 2, :], scale_of(u), None, ALU.mult).then_inc(biased, 1)
                else:
                    dve.wait_ge(bias_landed[u % 2], 16 * biased_before(u))
                    stt(S_, sc[:, u % 2, :], scale_of(u), bias[:, u % 2, :], ALU.mult, ALU.add).then_inc(biased, 1)
                dve.wait_ge(biased, u + 1)
                c = 2 * (u % 4)
                ins = v.tensor_reduce(vecs[:, c:c + 2], S_.rearrange("p (m k) -> p m k", m=2), AX, ALU.max, negate=True)
                if kind(u) == "swa":
                    link(ins)
                    j = (u - U_SWA) // 2
                    ins = tt(vecs[:, c:c + 2], vecs[:, c:c + 2], vecs[:, 40 + j:48:4], ALU.min)
                ins.then_inc(max_ready, 1)

            def after(u):
                q, c = u % 2, 2 * (u % 4)
                rr = vecs[:, 16 + c:18 + c]
                dve.wait_ge(probs_ready, u + 1)
                if kind(u) == "swa":
                    link(tt(vecs[:, 8 + c:10 + c], vecs[:, 8 + c:10 + c], vecs[:, 24 + c:26 + c], ALU.add))
                link(v.reciprocal(rr, vecs[:, 8 + c:10 + c]))
                if u < U_X:
                    j = (u // 2) % 4
                    link(tt(rr, rr, ag[:, q, :].rearrange("p (h r) -> p h r", r=3)[:, j::4, 1 + u // 8], ALU.mult))
                elif kind(u) == "diff":
                    link(tt(rr, rr, lbv[:, 38:40], ALU.mult))
                dve.wait_ge(pv_done, u + 1)
                for m in range(2):
                    r_ = rr[:, m:m + 1]
                    if u < U_X:
                        h = (u // 2) % 4 + 4 * m
                        dst = oa[:, q, 64 * h:64 * h + 64]
                        pv_ = pv[:, 64 * m:64 * m + 64]
                        ins = ts_(dst, pv_, r_, None, ALU.mult) if u < 8 else stt(dst, pv_, r_, dst, ALU.mult, ALU.add)
                    elif kind(u) == "diff":
                        h = (u - U_DIFF) // 2
                        dst = ya[:, q, h * P:(h + 1) * P]
                        if m == 0:
                            link(ts_(dst, pv[:, 0:P], r_, None, ALU.mult))
                        else:
                            ins = stt(dst, pv[:, P:2 * P], r_, dst, ALU.mult, ALU.add)
                    elif kind(u) == "swa":
                        h = (u - U_SWA) // 2 + 4 * m
                        ins = ts_(yd[:, q, 64 * h:64 * h + 64], pv[:, 64 * m:64 * m + 64], r_, None, ALU.mult)
                    else:
                        rows, h = (ox, 2 * ((u - U_X) // 2) + m) if kind(u) == "x" else (yc, 2 * ((u - U_FOX) // 2) + m)
                        ins = ts_(rows[:, q, h * P:(h + 1) * P], pv[:, m * P:(m + 1) * P], r_, None, ALU.mult)
                ins.then_inc(pv_used, 1)

            def unit_step(u, a, b):
                if u == a:
                    before(a)
                if u + 1 < b:
                    before(u + 1)
                if u > a:
                    after(u - 1)
                if u == b - 1:
                    after(u)
                    dve.wait_ge(pv_used, b)

            def attend(a, b):
                for u in range(a, b):
                    unit_step(u, a, b)

            for k in range(4):
                turned_low("xT1", actR, k)

            def lower_bound_shifted():
                wait_copied(dve, o_of("cols"))
                tt(lbv[:, 0:4], col("hgrn_lb_logits", 0, 4), col("hgrn_lb_logits", 0, 4), ALU.subtract).then_inc(lb_max, 1)

            link(v.memset(cpad[:, :, 0:16], 0.0))

            def finish_units(d, i):
                if d.b == ("b2", 0) and d.ends:
                    lower_bound_shifted()
                for u in units_behind(d):
                    if u[0] == U_NSA:
                        wait_copied(dve, o_of("b5"))
                    unit_step(*u)

            straight([d for tile in BLOCK1_TILES for d in projection_pieces(*tile)], split, finish_units)

            dve.wait_ge(lb_exp, 1)
            link(v.reciprocal(lbv[:, 8:12], lbv[:, 4:8]))
            link(tt(lbv[:, 4:8], lbv[:, 4:8], lbv[:, 8:12], ALU.mult))
            link(tt(lbv[:, 8:12], lbv[:, 4:8], lbv[:, 4:8], ALU.subtract))
            link(ts_(lbv[:, 12:16], lbv[:, 8:12], -1.0, 1.0, ALU.mult, ALU.add))

            wait_copied(dve, o_of("hin", 2))
            wait_copied(dve, o_of("hin", 3))
            for h in range(4):
                own.tick(ts_(hp[:, h, :], hp[:, h, :], lbv[:, 12 + h:13 + h], lbv[:, 8 + h:9 + h], ALU.mult, ALU.add))
            own.done()
            link(ts_(hp, hp, 1e-6, None, ALU.max))
            link(ts_(hk, hp, -1.0, 1.0, ALU.mult, ALU.add))
            link(v.memset(hr, 1.0))
            dve.wait_ge(level_tab_landed, 32)
            flat = lambda ap: ap.rearrange("p h t -> p (h t)")
            for lv in range(HL + 2):
                if lv:
                    wait_part(dve, f"lvl{lv - 1}")
                if lv == 0:
                    own.tick(v.tensor_copy(hqd, hq))
                    v.tensor_copy(hkd, hk).then_inc(level_ready, 1)
                else:
                    own.tick(tt(hqd, hq, hp, ALU.mult))
                    tt(hkd, hk, hr, ALU.mult).then_inc(level_ready, 1)
                for k in range(sum(B_AFTER[:lv]), sum(B_AFTER[:lv + 1])):
                    for d in projection_pieces(f"b{7 + k}"):
                        split(d, 0)
                if 1 <= lv <= HL:
                    h = 1 << (lv - 1)
                    P4 = flat(hp).rearrange("p (n z h) -> p n z h", z=2, h=h)
                    R4 = flat(hr).rearrange("p (n z h) -> p n z h", z=2, h=h)
                    n = 4 * S // (2 * h)
                    dve.wait_ge(level_ready, lv + 1)
                    link(tt(R4[:, :, 0, :], R4[:, :, 0, :], P4[:, :, 1, h - 1:h].broadcast_to([P, n, h]), ALU.mult))
                    link(tt(P4[:, :, 1, :], P4[:, :, 1, :], P4[:, :, 0, h - 1:h].broadcast_to([P, n, h]), ALU.mult))
                wait_part(dve, f"lvl{lv}")
                o = o_of(f"lvl{lv}")
                b = banks(o).rearrange("p a (h t) -> p (a h) t", h=4)
                if lv > HL:
                    release(v.tensor_copy(ATx, banks(o)[:, 0, :].rearrange("p (h t) -> p h t", h=4)), o)
                    wait_copied(dve, o)
                    continue
                mask = lmask[:, lv, :].unsqueeze(1).broadcast_to([P, 8, P])
                A3, tmp3 = (x.rearrange("p (a t) -> p a t", a=8) for x in (ATd, htmp))
                release(tt(A3 if lv == 0 else tmp3, b, mask, ALU.mult), o)
                wait_copied(dve, o)
                if lv:
                    link(tt(ATd, ATd, htmp, ALU.add))
            v.memset(stats[:, 92:93], 0.0).then_inc(decay_ready, 1)
            wait_copied(dve, o_of("ho"))
            hof = ho.rearrange("p q (h e) -> p (q h) e", h=4)
            tmpf = htmp.rearrange("p (a e) -> p a e", a=8)
            link(tt(tmpf, hof, hof, ALU.mult))
            link(v.tensor_reduce(stats[:, 56:64], tmpf, AX, ALU.add))
            ts_(stats[:, 64:72], stats[:, 56:64], 1.0 / P, LN_EPS, ALU.mult, ALU.add).then_inc(var_ready, 1)
            root(1, 8)
            link(tt(hof, hof, rstd.unsqueeze(2).broadcast_to([P, 8, P]), ALU.mult))
            link(tt(ho, ho, hgrow.unsqueeze(1).broadcast_to([P, NT, 512]), ALU.mult))
            tt(ho, ho, hg, ALU.mult).then_inc(mixer_rows, 1)

            wait_part(dve, "sgw")
            dve.wait_ge(weights1_landed, 16 * 6)
            release(tt(wmT, banks(o_of("sgw"))[:, 0, :].rearrange("p (g t) -> p g t", g=4),
                       tri.unsqueeze(1).broadcast_to([P, 4, P]), ALU.mult), o_of("sgw"))

            wait_copied(dve, o_of("b6"))
            wait_copied(dve, o_of("b7"))
            own.tick(v.memset(ping[:, :, 0:16], 0.0))
            link(v.memset(pong[:, :, 0:16], 0.0))
            src = cpad
            for g, dst in enumerate((ping, pong, ping, pong)):
                w_ = 1 << g
                link(tt(dst[:, g:, 16:], src[:, g:, 16:], src[:, g:, 16 - w_:16 + S - w_], ALU.add))
                src = dst
            dve.wait_ge(tables1_landed, 16 * 2)
            for g in range(4):
                own.tick(tt(ping[:, g, 16:], (ping, pong)[g % 2][:, g, 16:], invc[:, g, :], ALU.mult))
            own.done()
            tt(ping[:, :, 16:], ping[:, :, 16:], cpad[:, :, 16:], ALU.subtract).then_inc(mixer_rows, 1)
            wait_part(dve, "pool")
            o = o_of("pool")
            release(tt(brT[:, 8:12, :], banks(o).rearrange("p a (c t) -> p (a c) t", c=2),
                       col("pool_scale", 0, 4).unsqueeze(2).broadcast_to([P, 4, S]), ALU.mult), o)

            wait_copied(dve, o_of("b10"))
            wait_copied(dve, o_of("b11"))
            sums(sv, 0, 1)
            moments(1, 2, LN_EPS)
            center(sv, sv)
            dve.wait_ge(mixer1_landed, 16 * 3)
            link(tt(sv, sv, slg.unsqueeze(1).broadcast_to([P, NT, 512]), ALU.mult))
            tt(sv, sv, slb.unsqueeze(1).broadcast_to([P, NT, 512]), ALU.add).then_inc(mixer_rows, 1)
            wait_part(dve, "sgo")
            o = o_of("sgo")
            for g in range(4):
                gs = slice(g * P, (g + 1) * P)
                ins = stt(su[:, :, gs], banks(o)[:, :, gs], col("sg_b", g), su[:, :, gs], ALU.add, ALU.mult)
                if g == 2:
                    own.tick(ins)
            release(ins, o)
            wait_copied(dve, o)
            v.memset(stats[:, 93:94], 0.0).then_inc(mixer_rows, 1)

            wait_part(dve, "pos")
            o = o_of("pos")
            release(v.tensor_copy(posT.rearrange("p a b -> p (a b)"), banks(o)[:, 0, 0:64]), o)
            wait_copied(dve, o)
            for i in range(2):
                x = kvc[:, i, :].rearrange("p (m b) -> p b m", b=16)
                for a in range(2):
                    ins = tt(win[:, i, 16 * a:16 * a + 16, :], x[:, :, a:a + NC],
                             posT[:, i, 16 * a:16 * a + 16].unsqueeze(2).broadcast_to([P, 16, NC]), ALU.add)
            ins.then_inc(cmp_ready, 1)
            wait_part(dve, "ckv")
            o = o_of("ckv")
            v.tensor_copy(kcmp, banks(o)[:, 0, 0:NC])
            release(v.tensor_copy(vcmp[0:NC, :], banks(o)[0:NC, 1, 0:P]), o)
            wait_part(dve, "cs")
            o = o_of("cs")
            cS2 = cS.rearrange("p (q c) -> p q c", q=NT)
            cS3 = cS.rearrange("p (a c) -> p a c", c=NC)
            release(stt(cS2, banks(o)[:, :, 0:NH * NC], 64 ** -0.5,
                        ctab[:, 0:240].rearrange("p (q c) -> p q c", q=NT), ALU.mult, ALU.add), o)
            wait_copied(dve, o)
            link(v.tensor_reduce(csm[:, 0:16], cS3, AX, ALU.max))
            tt(cS3, cS3, csm[:, 0:16].unsqueeze(2).broadcast_to([P, 16, NC]), ALU.subtract).then_inc(cmp_ready, 1)
            dve.wait_ge(cmp_exp, 1)
            link(v.tensor_reduce(csm[:, 16:32], cS3, AX, ALU.add))
            link(v.reciprocal(csm[:, 32:48], csm[:, 16:32]))
            link(tt(csm[:, 48:64].rearrange("p (q h) -> p q h", q=NT),
                    csm[:, 32:48].rearrange("p (q h) -> p q h", q=NT),
                    ag.rearrange("p q (h r) -> p q h r", r=3)[:, :, :, 0], ALU.mult))
            tt(cS, cS, ctab[:, 240:480], ALU.mult).then_inc(cmp_ready, 1)
            wait_part(dve, "co")
            o = o_of("co")
            release(tt(co_rows.rearrange("p q (h e) -> p (q h) e", e=64),
                       banks(o).rearrange("p q (h e) -> p (q h) e", e=64),
                       csm[:, 48:64].unsqueeze(2).broadcast_to([P, 16, 64]), ALU.mult), o)
            wait_copied(dve, o)
            tt(oa, oa, co_rows, ALU.add).then_inc(mixer_rows, 1)

            def merged(biased_gates, between):
                pairs = lambda ap: ap.rearrange("p (a c) -> p a c", a=2)
                sum_ = pairs(mixS)

                def finish(d, i):
                    b, G = d.b, pairs(gateS[:, d.b % 2, :])
                    if d.ends == "gate" and biased_gates:
                        product(dve, d, i)
                        for x in range(2):
                            bcol = cols[:, 1, bass.ds(i * 2 + (16 * b + x), 1)]
                            ins = ts_(G[:, x, :], banks(d.out)[:, x, 0:S], bcol, None, ALU.add)
                        release(ins, d.out)
                    if d.ends == "y":
                        if biased_gates:
                            reach(dve, gate_ready, b + 1, i, NBR)
                        else:
                            copied(dve, d.out - 1, i, d.per_out)
                        product(dve, d, i)
                        y = sum_ if b == 0 else pairs(yS)
                        release(tt(y, banks(d.out)[:, :, 0:S], G, ALU.mult), d.out)
                        if b:
                            copied(dve, d.out, i, d.per_out)
                            link(tt(mixS, mixS, yS, ALU.add))
                        if b == NBR - 1:
                            hi_, lo = (mixR[:, part, bass.ds(i * 2, 2), :] for part in (0, 1))
                            link(ts_(hi_, sum_, 1.0, None, ALU.mult))
                            tt(lo, sum_, hi_.bitcast(F32), ALU.subtract).then_inc(gate_used, 1)
                    if between:
                        between(d, i)
                return finish

            def merge(name, biased_gates, between=None):
                in_turns(dve, D // W, merge_pieces(name), split, merged(biased_gates, between), own=own, per=4)

            def mem_norm(d, i):
                if not (isinstance(i, int) and i == 0 and d in merge_pieces("merge1")[:NORM_ROOT + 2]):
                    return
                q = merge_pieces("merge1").index(d)
                st = stats[:, 0:48].rearrange("p (q g x) -> p q g x", q=NT, g=4)
                if q < 8:
                    if q == 0:
                        dve.wait_ge(mem_landed, 16)
                    own.tick(v.bn_stats(st[:, q // 4, q % 4, :], xa[:, q // 4, q % 4 * 512:(q % 4 + 1) * 512]))
                elif q == 8:
                    own.done()
                    for a in range(NT):
                        own.tick(v.bn_aggr(mean_var[:, a, :], st[:, a, :, :].rearrange("p g x -> p (g x)")))
                    own.done()
                    ts_(stats[:, 64:66], mean_var[:, :, 1], LN_EPS, None, ALU.add).then_inc(var_ready, 1)
                elif q == NORM_ROOT:
                    root(3, 2)
                    own.tick(ts_(xa[:, 0, :], xa[:, 0, :], mean_var[:, 0, 0:1], rstd[:, 0:1], ALU.subtract, ALU.mult))
                elif q == NORM_ROOT + 1:
                    ts_(xa[:, 1, :], xa[:, 1, :], mean_var[:, 1, 0:1], rstd[:, 1:2], ALU.subtract, ALU.mult)\
                        .then_inc(rows_ready, 1)

            branches_low("br1")
            merge("merge1", False, mem_norm)

            for k in range(4):
                wait_high(at["memT"][3] + k)
                low(brR, mem_tmp[k % 2].rearrange("p (c t) -> p c t", c=4), k).then_inc(lo_ready, 1)
            straight(tile_pieces("xk", 2), split, finish_none)
            straight(tile_pieces("xv", 2), split, finish_none)

            dve.wait_ge(resid_landed, 16)
            square_out("mixout1", ALPHA)
            norm_and_turn(0, 4, "x1T", mixR)
            straight(tile_pieces("xq", 2), split, finish_none)

            attend(U_X, U_SWA)
            v.memset(stats[:, 88:89], 0.0).then_inc(mixer_rows, 1)
            turned_low("xoT", brR, 0)
            straight(wide_pieces("xo"), split, finish_rows(ALPHA, None, at["xo"][0]))
            norm_and_turn(1, 5, "x2T", actR)

            link(ts_(xa[:, :, :], xa[:, :, :], ALPHA, None, ALU.mult))
            feed_forward("ff1", True)
            moments(4, 6, LN_EPS)
            dve.wait_ge(norm_rows_landed, 32 * 3)
            for c in range(4):
                link(normed_quarter(2, c))
                sums(xa, c)
            v.memset(stats[:, 90:91], 0.0).then_inc(norm_done, 1)

            rms_rows(rowsx, 7)
            weighted("xT2", "norm_mix_2", actR)
            link(v.memset(bx[:, :, 0:4], 0.0))

            def lru_convolved():
                wait_copied(dve, o_of("in2", 0))
                wait_copied(dve, o_of("in2", 1))
                for c in range(4):
                    own.tick(ts_(xc[:, c, :], bx[:, c, 4:], col("lru_conv_w_2", 12 + c), col("lru_conv_b_2", c),
                                 ALU.mult, ALU.add))
                own.done()
                for tap_ in (2, 1, 0):
                    for c in range(4):
                        ins = stt(xc[:, c, :], bx[:, c, tap_ + 1:tap_ + 1 + S], col("lru_conv_w_2", 4 * tap_ + c),
                                  xc[:, c, :], ALU.mult, ALU.add)
                        if tap_ or c < 3:
                            own.tick(ins)
                    if tap_:
                        own.done()
                ins.then_inc(lru_conv, 1)
                dve.wait_ge(lru_conv, 1)

            def lambda_sums():
                lam_ = col("lru_lambda_2", 0, 4)
                link(ts_(lbv[:, 24:28], lam_, -1.0, None, ALU.mult))
                tt(lbv[:, 16:20], lbv[:, 24:28], lam_, ALU.min).then_inc(sp_abs, 1)
                dve.wait_ge(mixer2_landed, 16 * MIXER2_LOADS)
                for k in range(2):
                    own.tick(tt(lrow[:, 128 * k:128 * k + 64], lrow[:, 128 * k:128 * k + 64],
                                lrow[:, 128 * k + 64:128 * k + 128], ALU.mult))
                own.done()
                for k in range(2):
                    ins = v.tensor_reduce(lbv[:, 32 + k:33 + k], lrow[:, 128 * k:128 * k + 64], AX, ALU.add)
                ins.then_inc(lam_sum, 1)

            def lambda_of_differences():
                dve.wait_ge(lam_exp, 1)
                link(tt(lbv[:, 36:37], lbv[:, 35:36], lbv[:, 34:35], ALU.subtract))
                link(ts_(lbv[:, 36:37], lbv[:, 36:37], LAM_INIT, None, ALU.subtract))
                link(ts_(lbv[:, 37:38], lbv[:, 36:37], -1.0, None, ALU.mult))
                link(tt(lbv[:, 37:38], lbv[:, 37:38], lbv[:, 36:37], ALU.max))
                link(ts_(lbv[:, 37:38], lbv[:, 37:38], 1.0, None, ALU.max))
                link(v.reciprocal(lbv[:, 38:39], lbv[:, 37:38]))
                link(tt(lbv[:, 39:40], lbv[:, 36:37], lbv[:, 38:39], ALU.mult))
                link(ts_(lbv[:, 37:38], lbv[:, 38:39], RMS_EPS, lbv[:, 38:39], ALU.mult, ALU.mult))
                link(ts_(lbv[:, 37:38], lbv[:, 37:38], 1e-37, None, ALU.max))
                link(ts_(vecs[:, 40:48], sinks, -1.0, None, ALU.mult))

            def lru_exponent():
                dve.wait_ge(sp_exp, 1)
                log1p(lbv[:, 20:24], lbv[:, 40:44], lbv[:, 44:48], lbv[:, 48:52])
                link(stt(lbv[:, 24:28], lbv[:, 24:28], 0.0, lbv[:, 48:52], ALU.max, ALU.add))
                link(ts_(lbv[:, 24:28], lbv[:, 24:28], -8.0, None, ALU.mult))

            def lru_arguments():
                wait_copied(dve, o_of("lru", 0))
                wait_copied(dve, o_of("lru", 1))
                for c in range(4):
                    ins = ts_(lr[:, c, :], lr[:, c, :], lbv[:, 24 + c:25 + c], None, ALU.mult)
                ins.then_inc(lru_arg, 1)
                link(tt(li, li, xc, ALU.mult))

            def lru_square():
                dve.wait_ge(lru_exp, 1)
                link(ts_(bfree, lt, 1.0, None, ALU.add))
                link(v.reciprocal(bfree, bfree))
                tt(lt, lt, bfree, ALU.mult).then_inc(lru_sq, 1)

            def lru_scan():
                dve.wait_ge(lru_sqrt, 1)
                link(tt(li, li, lt, ALU.mult))
                for c in range(4):
                    own.tick(v.tensor_tensor_scan(xc[:, c, :], la[:, c, :], li[:, c, :], 0.0, ALU.mult, ALU.add))
                own.done()
                v.memset(stats[:, 89:90], 0.0).then_inc(mixer_rows, 1)

            def lru_branch():
                wait_copied(dve, o_of("in2", 3))
                link(tt(brT[:, 4:8, :], xc, bg, ALU.mult))

            z4 = cf[0:4, :]
            na, ez, t1, t2, t3 = (ftmp[0:4, k, :] for k in (0, 1, 2, 3, 0))

            def forget_logits():
                wait_copied(dve, o_of("in2", 13))
                link(ts_(z4, z4, bf[0:4, :], None, ALU.add))
                link(ts_(na, z4, -1.0, None, ALU.mult))
                tt(na, na, z4, ALU.min).then_inc(sp_abs, 1)

            def forget_sums():
                dve.wait_ge(sp_exp, 2)
                log1p(ez, t1, t2, t3)
                link(stt(t1, z4, 0.0, t3, ALU.min, ALU.subtract))
                link(v.tensor_tensor_scan(cum[0:4, :], heads[0:4, 4, :], t1, 0.0, ALU.mult, ALU.add))
                link(ts_(ncum[0:4, :], cum[0:4, :], -1.0, None, ALU.mult))
                v.memset(stats[:, 95:96], 0.0).then_inc(mixer_rows, 1)

            yaf = ya.rearrange("p q (h e) -> p (q h) e", h=4)

            def differences_squared():
                sqf = ysq.rearrange("p (a e) -> p a e", a=8)
                link(tt(sqf, yaf, yaf, ALU.mult))
                link(v.tensor_reduce(stats[:, 56:64], sqf, AX, ALU.add))
                ts_(stats[:, 64:72], stats[:, 56:64], 1.0 / P, lbv[:, 37:38], ALU.mult, ALU.add).then_inc(var_ready, 1)

            def differences_normed():
                root(8, 8)
                link(tt(yaf, yaf, rstd.unsqueeze(2).broadcast_to([P, 8, P]), ALU.mult))
                link(tt(yaf, yaf, subln.unsqueeze(1).broadcast_to([P, 8, P]), ALU.mult))
                link(ts_(ya, ya, 1.0 - LAM_INIT, None, ALU.mult))

            steps = {(18, 1): differences_squared, (19, 1): differences_normed, (1, 3): lru_convolved, (2, 1): lambda_sums, (3, 3): lambda_of_differences, (4, 1): lru_exponent,
                     (7, 1): lru_arguments, (8, 0): lru_square, (8, 3): lru_scan, (9, 0): lru_branch,
                     (13, 3): forget_logits, (17, 3): forget_sums}

            def finish_steps(d, i):
                for u in units_behind(d):
                    unit_step(*u)
                if (d.b[1], d.k) in steps:
                    steps[d.b[1], d.k]()

            straight([d for k in range(20) for d in projection_pieces("in2", k)], split, finish_steps)
            attend(U_FOX, U_END)
            v.memset(stats[:, 91:92], 0.0).then_inc(mixer_rows, 1)

            branches_low("br2")
            merge("merge2", True)
            square_out("mixout2", None)
            rms_rows(rowsx, 9)

            weighted("x3T", "norm_ffn_2", mixR)
            feed_forward("ff2", False)
            moments(4, 10, RMS_EPS, rms=True)
            dve.wait_ge(norm_rows_landed, 32 * 4)
            for q in range(NT):
                stt(xa[:, q, :], xa[:, q, :], rstd[:, q:q + 1], lng[3], ALU.mult, ALU.mult).then_inc(rows_ready, 1)


def laid_out(x):
    r = lambda name, *shape: x[name].reshape(*shape)
    stacked = {name: r(name, -1, P) for st in STACKS for name, _ in st if not name.startswith("conv_w")}
    taps = r("ffn_conv_w", 3 * FC, P)
    stacked["conv_w_01"], stacked["conv_w_2"] = taps[:2 * FC], taps[2 * FC:]
    return stacked | {
        "x": r("x", S, D), "mem": r("mem", S, D), "w_in": r("w_in", D, -1), "w_in_2": r("w_in_2", D, -1),
        "nsa_cmp_pos": r("nsa_cmp_pos", 64, 64), "nsa_cmp_w": r("nsa_cmp_w", 2, 32, 64, 64),
        "hgrn_norm_g": r("hgrn_norm_g", -1), "pool_w": r("pool_w", 4, P, P),
        "sg_ln_g": r("sg_ln_g", -1), "sg_ln_b": r("sg_ln_b", -1), "sg_w": r("sg_w", 4, P, P),
        "w_branch": r("w_branch", D, D), "w_branch_2": r("w_branch_2", D, D),
        "w_mix_out": r("w_mix_out", D, D), "w_out_2": r("w_out_2", D, D),
        "ln_mix_g": r("ln_mix_g", -1), "ln_mix_b": r("ln_mix_b", -1), "ln_x_g": r("ln_x_g", -1),
        "ln_x_b": r("ln_x_b", -1), "ln_ffn_g": r("ln_ffn_g", -1), "ln_ffn_b": r("ln_ffn_b", -1),
        "xattn_q": r("xattn_q", D, -1), "xattn_k": r("xattn_k", D, -1), "xattn_v": r("xattn_v", D, -1),
        "xattn_o": r("xattn_o", -1, D), "ffn_in": r("ffn_in", D, -1), "ffn_out": r("ffn_out", -1, D),
        "diff_lq1_2": r("diff_lq1_2", -1), "diff_lk1_2": r("diff_lk1_2", -1),
        "diff_lq2_2": r("diff_lq2_2", -1), "diff_lk2_2": r("diff_lk2_2", -1),
        "diff_subln_2": r("diff_subln_2", -1), "lru_wa_2": r("lru_wa_2", 8, 64, 64),
        "lru_wx_2": r("lru_wx_2", 8, 64, 64), "fox_b_f_2": r("fox_b_f_2", -1),
        "swa_sinks_2": r("swa_sinks_2", -1), "w_ffn_gate_2": r("w_ffn_gate_2", D, -1),
        "w_ffn_up_2": r("w_ffn_up_2", D, -1), "w_ffn_down_2": r("w_ffn_down_2", -1, D),
        "norm_final_2": r("norm_final_2", -1),
    }


def kernel(**inputs):
    import concourse.bacc as _bacc
    from concourse.bass_utils import run_bass_kernel_spmd as _run

    nc = _bacc.Bacc("TRN2", target_bir_lowering=False, num_devices=1)
    arrays = {k: np.ascontiguousarray(a) for k, a in laid_out({k: np.asarray(a) for k, a in inputs.items()}).items()}
    arrays.update(shape_tables())
    arrays = {f"in_{k}": a for k, a in arrays.items()}
    t = {k[3:]: nc.dram_tensor(k, a.shape, F32, kind="ExternalInput").ap() for k, a in arrays.items()}
    out = nc.dram_tensor("out", (S, D), F32, kind="ExternalOutput").ap()
    two_layer_block_kernel(nc, t, out)
    r = _run(nc, [arrays], core_ids=[0])
    return r.results[0]["out"].reshape(1, S, D)
```
